# Optimizing a Trainium2 kernel written in Bass

```python
import jax
import jax.numpy as jnp
from jax import lax
import numpy as np

D_MODEL = 2048
BATCH = 1
SEQ = 256
DEPTH = 1
DEC_BATCH = 8
DEC_SEQ = 1
PAST_LEN = 2048
PAGE_SIZE = 128

MIX_WIDTH = D_MODEL
GLA_WIDTH = MIX_WIDTH // 2
RWKV_WIDTH = MIX_WIDTH - GLA_WIDTH
GLA_HEADS = 4
GLA_DV = GLA_WIDTH // GLA_HEADS
GLA_DK = GLA_DV // 2
GLA_KEY_WIDTH = GLA_HEADS * GLA_DK
GLA_GATE_RANK = 16
GLA_GATE_NORMALIZER = 16.0
GLA_CHUNK = 64
RWKV_HEAD = 64
RWKV_HEADS = RWKV_WIDTH // RWKV_HEAD
RWKV_W_RANK = 64
RWKV_A_RANK = 64
RWKV_G_RANK = 128
GLA_SPLITS = (GLA_KEY_WIDTH, GLA_KEY_WIDTH, GLA_WIDTH, GLA_GATE_RANK, GLA_WIDTH)
RWKV_SPLITS = (RWKV_WIDTH, RWKV_W_RANK, RWKV_WIDTH, RWKV_WIDTH, RWKV_A_RANK, RWKV_G_RANK)
GLA_COLS = sum(GLA_SPLITS)
RWKV_COLS = sum(RWKV_SPLITS)
IN_COLS = GLA_COLS + RWKV_COLS
N_GROUPS = 4
EXPERTS_PER_GROUP = 8
TOP_K_IN_GROUP = 2
EXPERT_FF = 512
NORM_EPS = 1e-6
GLA_NORM_EPS = 1e-5
RWKV_GN_EPS = 64e-5

kernel_name = 'hymba_gla_rwkv7_hmoe_adaln'

def split_cols(a, sizes):
    idx = [int(i) for i in np.cumsum(sizes)[:-1]]
    return jnp.split(a, idx, axis=-1)

def rmsnorm(x, g, eps=NORM_EPS):
    xf = x.astype(jnp.float32)
    return xf * lax.rsqrt(jnp.mean(xf * xf, axis=-1, keepdims=True) + eps) * g

def adaln(c, w, b, n):
    mod = jax.nn.silu(c.astype(jnp.float32)) @ w + b
    return jnp.split(mod[:, None, :], n, axis=-1)

def gla_chunked(q, k, v, logd, s0):
    B, T, H, _ = q.shape
    C = GLA_CHUNK
    n = T // C

    def to_chunks(a):
        return a.reshape(B, n, C, H, a.shape[-1]).transpose(1, 0, 3, 2, 4)

    mask = jnp.tril(jnp.ones((C, C), dtype=bool))[:, :, None]

    def step(S, inp):
        qi, ki, vi, gi = inp
        b = jnp.cumsum(gi, axis=2)
        o_inter = jnp.einsum('bhcd,bhde->bhce', qi * jnp.exp(b), S)
        rel = jnp.where(mask, b[:, :, :, None, :] - b[:, :, None, :, :], -jnp.inf)
        att = jnp.einsum('bhid,bhjd,bhijd->bhij', qi, ki, jnp.exp(rel))
        o = o_inter + jnp.einsum('bhij,bhje->bhie', att, vi)
        b_last = b[:, :, -1:, :]
        S = jnp.exp(b_last[:, :, 0, :, None]) * S + jnp.einsum('bhcd,bhce->bhde', ki * jnp.exp(b_last - b), vi)
        return S, o

    S, o = lax.scan(step, s0, (to_chunks(q), to_chunks(k), to_chunks(v), to_chunks(logd)))
    o = o.transpose(1, 0, 3, 2, 4).reshape(B, T, H, -1)
    return o, S

def gla_recurrent(q, k, v, logd, s0):
    def step(S, inp):
        qt, kt, vt, gt = inp
        S = jnp.exp(gt)[..., None] * S + kt[..., :, None] * vt[..., None, :]
        return S, jnp.einsum('bhd,bhde->bhe', qt, S)

    xs = tuple(a.transpose(1, 0, 2, 3) for a in (q, k, v, logd))
    S, o = lax.scan(step, s0, xs)
    return o.transpose(1, 0, 2, 3), S

def rwkv7_scan(r, decay, k, v, kk, a, s0):
    def step(S, inp):
        rt, wt, kt, vt, kkt, at = inp
        sa = jnp.einsum('bhij,bhj->bhi', S, -kkt)
        S = S * wt[:, :, None, :] + sa[..., None] * (kkt * at)[:, :, None, :] + vt[..., None] * kt[:, :, None, :]
        return S, jnp.einsum('bhij,bhj->bhi', S, rt)

    xs = tuple(t.transpose(1, 0, 2, 3) for t in (r, decay, k, v, kk, a))
    S, y = lax.scan(step, s0, xs)
    return y.transpose(1, 0, 2, 3), S

def token_mixers(h, s_gla, s_rwkv, shift_prev, w_in, gla_gate_w2, gla_gate_b, gla_norm,
                 rwkv_mu, rwkv_w0, rwkv_w2, rwkv_a0, rwkv_a2, rwkv_g2, rwkv_k_k, rwkv_k_a,
                 rwkv_r_k, rwkv_gn_w, rwkv_gn_b, w_out, chunked):
    B, T, _ = h.shape
    f32 = jnp.float32
    p = jnp.einsum('btd,dc->btc', h, w_in).astype(f32)
    gla_p, rwkv_p = p[..., :GLA_COLS], p[..., GLA_COLS:]

    q, k, v, gl, og = split_cols(gla_p, GLA_SPLITS)
    logd = jax.nn.log_sigmoid(gl @ gla_gate_w2 + gla_gate_b) / GLA_GATE_NORMALIZER
    q = q.reshape(B, T, GLA_HEADS, GLA_DK) * (GLA_DK ** -0.5)
    k = k.reshape(B, T, GLA_HEADS, GLA_DK)
    v = v.reshape(B, T, GLA_HEADS, GLA_DV)
    logd = logd.reshape(B, T, GLA_HEADS, GLA_DK)
    s0 = s_gla.astype(f32)
    if chunked:
        o, s_gla_new = gla_chunked(q, k, v, logd, s0)
    else:
        o, s_gla_new = gla_recurrent(q, k, v, logd, s0)
    o = rmsnorm(o, gla_norm, GLA_NORM_EPS) * jax.nn.silu(og).reshape(B, T, GLA_HEADS, GLA_DV)
    o_gla = o.reshape(B, T, GLA_WIDTH)

    prev = jnp.concatenate([shift_prev[:, None, :].astype(f32), rwkv_p[:, :-1]], axis=1)
    xs = rwkv_p + (prev - rwkv_p) * rwkv_mu
    new_shift = rwkv_p[:, -1]
    r, wl, k7, v7, al, gl7 = split_cols(xs, RWKV_SPLITS)
    w = -jax.nn.softplus(-(rwkv_w0 + jnp.tanh(wl) @ rwkv_w2)) - 0.5
    decay = jnp.exp(-jnp.exp(w))
    a = jax.nn.sigmoid(rwkv_a0 + al @ rwkv_a2)
    g = jax.nn.sigmoid(gl7) @ rwkv_g2
    heads = lambda t: t.reshape(B, T, RWKV_HEADS, RWKV_HEAD)
    kk = heads(k7 * rwkv_k_k)
    kk = kk / jnp.maximum(jnp.sqrt(jnp.sum(kk * kk, axis=-1, keepdims=True)), 1e-12)
    k7 = k7 * (1.0 + (a - 1.0) * rwkv_k_a)
    r, decay, k7, v7, a = heads(r), heads(decay), heads(k7), heads(v7), heads(a)
    y, s_rwkv_new = rwkv7_scan(r, decay, k7, v7, kk, a, s_rwkv.astype(f32))
    mu = jnp.mean(y, axis=-1, keepdims=True)
    var = jnp.mean(jnp.square(y - mu), axis=-1, keepdims=True)
    y = (y - mu) * lax.rsqrt(var + RWKV_GN_EPS) * rwkv_gn_w.reshape(RWKV_HEADS, RWKV_HEAD) \
        + rwkv_gn_b.reshape(RWKV_HEADS, RWKV_HEAD)
    bonus = jnp.sum(r * k7 * rwkv_r_k, axis=-1, keepdims=True) * v7
    o_rwkv = (y + bonus).reshape(B, T, RWKV_WIDTH) * g

    out = jnp.concatenate([o_gla, o_rwkv], axis=-1) @ w_out
    return out, s_gla_new, s_rwkv_new, new_shift

def hier_moe(h, w_router_group, w_router_expert, w_exp_gate, w_exp_up, w_exp_down):
    B, T, D = h.shape
    hf = h.reshape(B * T, D)
    p_group = jax.nn.softmax((hf @ w_router_group).astype(jnp.float32), axis=-1)
    g_sel = jnp.argmax(p_group, axis=-1)
    p_sel = jnp.take_along_axis(p_group, g_sel[:, None], axis=-1)
    logits_e = (hf @ w_router_expert).astype(jnp.float32).reshape(-1, N_GROUPS, EXPERTS_PER_GROUP)
    logits_e = jnp.take_along_axis(logits_e, g_sel[:, None, None], axis=1)[:, 0]
    top_v, top_i = lax.top_k(logits_e, TOP_K_IN_GROUP)
    w_top = jax.nn.softmax(top_v, axis=-1) * p_sel
    comb = jnp.einsum('nk,nke->ne', w_top, jax.nn.one_hot(top_i, EXPERTS_PER_GROUP, dtype=jnp.float32))
    out = jnp.zeros((B * T, D), jnp.float32)
    for grp in range(N_GROUPS):
        wgt = comb * (g_sel == grp)[:, None]
        hg = jnp.einsum('nd,edf->enf', hf, w_exp_gate[grp])
        hu = jnp.einsum('nd,edf->enf', hf, w_exp_up[grp])
        hid = jax.nn.silu(hg) * hu * wgt.T[:, :, None]
        out = out + jnp.einsum('enf,efd->nd', hid, w_exp_down[grp])
    return out.reshape(B, T, D)

def setup_inputs(seed: int = 0) -> dict:
    key = jax.random.key(seed)
    ks = iter(jax.random.split(key, 48))
    nrm = lambda shape, scale: jax.random.normal(next(ks), shape, jnp.float32) * scale
    unif = lambda shape, lo, hi: jax.random.uniform(next(ks), shape, jnp.float32, lo, hi)
    D = D_MODEL
    G, E, F = N_GROUPS, EXPERTS_PER_GROUP, EXPERT_FF
    d = {}
    d['x_prompt'] = nrm((BATCH, SEQ, D), 1.0)
    d['x_sample'] = nrm((DEC_BATCH, DEC_SEQ, D), 1.0)
    d['state_gla'] = nrm((DEPTH, DEC_BATCH, GLA_HEADS, GLA_DK, GLA_DV), 0.5)
    d['state_rwkv'] = nrm((DEPTH, DEC_BATCH, RWKV_HEADS, RWKV_HEAD, RWKV_HEAD), 0.3)
    d['state_shift'] = nrm((DEPTH, DEC_BATCH, RWKV_COLS), 1.0)
    d['c_prompt'] = nrm((BATCH, D), 1.0)
    d['c_sample'] = nrm((DEC_BATCH, D), 1.0)
    d['w_ada'] = nrm((DEPTH, D, 6 * D), 0.5 * D ** -0.5)
    d['b_ada'] = nrm((DEPTH, 6 * D), 0.01)
    d['norm_mix'] = 1.0 + nrm((DEPTH, D), 0.01)
    d['norm_ffn'] = 1.0 + nrm((DEPTH, D), 0.01)
    d['w_in'] = nrm((DEPTH, D, IN_COLS), D ** -0.5)
    d['gla_gate_w2'] = nrm((DEPTH, GLA_GATE_RANK, GLA_KEY_WIDTH), GLA_GATE_RANK ** -0.5)
    d['gla_gate_b'] = nrm((DEPTH, GLA_KEY_WIDTH), 0.1)
    d['gla_norm'] = 1.0 + nrm((DEPTH, GLA_DV), 0.01)
    d['rwkv_mu'] = unif((DEPTH, RWKV_COLS), 0.0, 1.0)
    d['rwkv_w0'] = unif((DEPTH, RWKV_WIDTH), -5.0, -1.0)
    d['rwkv_w2'] = nrm((DEPTH, RWKV_W_RANK, RWKV_WIDTH), 0.1 * RWKV_W_RANK ** -0.5)
    d['rwkv_a0'] = nrm((DEPTH, RWKV_WIDTH), 0.1)
    d['rwkv_a2'] = nrm((DEPTH, RWKV_A_RANK, RWKV_WIDTH), RWKV_A_RANK ** -0.5)
    d['rwkv_g2'] = nrm((DEPTH, RWKV_G_RANK, RWKV_WIDTH), RWKV_G_RANK ** -0.5)
    d['rwkv_k_k'] = 0.85 + nrm((DEPTH, RWKV_WIDTH), 0.02)
    d['rwkv_k_a'] = 1.0 + nrm((DEPTH, RWKV_WIDTH), 0.02)
    d['rwkv_r_k'] = nrm((DEPTH, RWKV_HEADS, RWKV_HEAD), 0.1)
    d['rwkv_gn_w'] = 1.0 + nrm((DEPTH, RWKV_WIDTH), 0.01)
    d['rwkv_gn_b'] = nrm((DEPTH, RWKV_WIDTH), 0.01)
    d['w_out'] = nrm((DEPTH, MIX_WIDTH, D), MIX_WIDTH ** -0.5)
    d['w_router_group'] = nrm((DEPTH, D, G), D ** -0.5)
    d['w_router_expert'] = nrm((DEPTH, D, G * E), D ** -0.5)
    d['w_exp_gate'] = nrm((DEPTH, G, E, D, F), D ** -0.5)
    d['w_exp_up'] = nrm((DEPTH, G, E, D, F), D ** -0.5)
    d['w_exp_down'] = nrm((DEPTH, G, E, F, D), F ** -0.5)
    d['norm_final'] = 1.0 + nrm((D,), 0.01)
    d['w_ada_final'] = nrm((D, 2 * D), 0.5 * D ** -0.5)
    d['b_ada_final'] = nrm((2 * D,), 0.01)
    return d

def reference(x_prompt, x_sample, state_gla, state_rwkv, state_shift, c_prompt, c_sample,
              w_ada, b_ada, norm_mix, norm_ffn, w_in, gla_gate_w2, gla_gate_b, gla_norm,
              rwkv_mu, rwkv_w0, rwkv_w2, rwkv_a0, rwkv_a2, rwkv_g2, rwkv_k_k, rwkv_k_a, rwkv_r_k,
              rwkv_gn_w, rwkv_gn_b, w_out, w_router_group, w_router_expert,
              w_exp_gate, w_exp_up, w_exp_down, norm_final, w_ada_final, b_ada_final):
    def trunk(x, c, gla0, rwkv0, shift0, chunked):
        new_gla, new_rwkv, new_shift = [], [], []
        for l in range(DEPTH):
            sh1, sc1, gt1, sh2, sc2, gt2 = adaln(c, w_ada[l], b_ada[l], 6)
            h = rmsnorm(x, norm_mix[l]) * (1.0 + sc1) + sh1
            mix, s_g, s_r, s_s = token_mixers(
                h, gla0[l], rwkv0[l], shift0[l], w_in[l], gla_gate_w2[l], gla_gate_b[l], gla_norm[l],
                rwkv_mu[l], rwkv_w0[l], rwkv_w2[l], rwkv_a0[l], rwkv_a2[l], rwkv_g2[l], rwkv_k_k[l],
                rwkv_k_a[l], rwkv_r_k[l], rwkv_gn_w[l], rwkv_gn_b[l], w_out[l], chunked)
            x = x + gt1 * mix
            h = rmsnorm(x, norm_ffn[l]) * (1.0 + sc2) + sh2
            x = x + gt2 * hier_moe(h, w_router_group[l], w_router_expert[l],
                                   w_exp_gate[l], w_exp_up[l], w_exp_down[l])
            new_gla.append(s_g)
            new_rwkv.append(s_r)
            new_shift.append(s_s)
        sh_f, sc_f = adaln(c, w_ada_final, b_ada_final, 2)
        y = rmsnorm(x, norm_final) * (1.0 + sc_f) + sh_f
        return y, jnp.stack(new_gla), jnp.stack(new_rwkv), jnp.stack(new_shift)

    bp = x_prompt.shape[0]
    gla0_p = jnp.zeros((DEPTH, bp, GLA_HEADS, GLA_DK, GLA_DV), jnp.float32)
    rwkv0_p = jnp.zeros((DEPTH, bp, RWKV_HEADS, RWKV_HEAD, RWKV_HEAD), jnp.float32)
    shift0_p = jnp.zeros((DEPTH, bp, RWKV_COLS), jnp.float32)
    y_prompt, sg_p, sr_p, ss_p = trunk(x_prompt, c_prompt, gla0_p, rwkv0_p, shift0_p, True)
    y_sample, sg_s, sr_s, ss_s = trunk(x_sample, c_sample, state_gla, state_rwkv, state_shift, False)
    return (y_prompt, y_sample, sg_p, sr_p, ss_p, sg_s, sr_s, ss_s)


_drawn_inputs = setup_inputs


def setup_inputs(seed=0):
    import zlib

    import numpy as np

    out = dict(_drawn_inputs(seed))
    spreads = {}
    factors = {'norm_mix': 4.073,
     'norm_ffn': 6.039,
     'gla_norm': 8.0,
     'rwkv_w2': 5.576,
     'rwkv_gn_w': 8.0,
     'rwkv_gn_b': 8.0,
     'norm_final': 5.612,
     'b_ada_final': 4.36}
    for name, (base, spread) in spreads.items():
        noise = np.random.default_rng([zlib.crc32(name.encode()), seed]).standard_normal(out[name].shape)
        drawn = base * np.exp(spread * noise) if base else spread * noise
        out[name] = jnp.asarray(drawn.astype(out[name].dtype))
    for name, factor in factors.items():
        out[name] = (out[name] * factor).astype(out[name].dtype)
    return out
```

```python
from contextlib import ExitStack

import numpy as np

import concourse.bass as bass
from concourse import mybir

F32 = mybir.dt.float32
I32 = mybir.dt.int32
ALU = mybir.AluOpType
ACT = mybir.ActivationFunctionType
AX = mybir.AxisListType

P = 128
D = 2048
KD = D // P
NP_ = 256
NS = 8
NT = NP_ + NS
TC = NP_ // P
COND = 1 + NS
CPAD = 32
BANK = 512
GLA_H, GLA_DK, GLA_DV = 4, 128, 256
GATE_RANK = 16
RH, RD = 16, 64
NPAIR = RH // 2
CH = 64
NCH = NP_ // CH
RCOLS = 3328
GCOLS = 3088
NG, NE, FF = 4, 8, 512
NEXP = NG * NE
SLOT = 64
CAP = SLOT - NS
PASSES = -(-NP_ // CAP)
RING = 4096
MIX_SLOTS, MOE_SLOTS = 4, 6
EPS, GLA_EPS, GN_EPS = 1e-6, 1e-5, 64e-5
HALF_E = float(np.exp(-0.5))
TQ, TK, TV, TOG, TR, TK7, TV7, TWA, TG7, TGL, NTILE = 0, 4, 8, 16, 24, 32, 40, 48, 49, 50, 51
SHIFT_PARTS = [(0, 0, 0, 1024), (8, 0, 1088, 1024), (16, 0, 2112, 1024), (24, 0, 1024, 64), (24, 64, 3136, 64),
               (25, 0, 3200, 128)]
V_ADA, V_NMIX, V_NFFN, V_NFIN, V_MU, V_GB, V_GN = 0, 128, 144, 160, 176, 202, 206
V_W0, V_A0, V_KK, V_KA, V_RK, V_GW, V_GBI, V_END = 208, 216, 224, 232, 240, 248, 256, 264
M_SH1, M_SC1, M_GT1, M_SH2, M_SC2, M_GT2, M_SHF, M_SCF = range(8)


def hymba_layer(nc, x_prompt, x_sample, state_gla, state_rwkv, state_shift, c_prompt, c_sample,
                w_ada, b_ada, norm_mix, norm_ffn, w_in, gla_gate_w2, gla_gate_b, gla_norm,
                rwkv_mu, rwkv_w0, rwkv_w2, rwkv_a0, rwkv_a2, rwkv_g2, rwkv_k_k, rwkv_k_a, rwkv_r_k,
                rwkv_gn_w, rwkv_gn_b, w_out, w_router_group, w_router_expert,
                w_exp_gate, w_exp_up, w_exp_down, norm_final, w_ada_final, b_ada_final,
                y_prompt, y_sample, sg_prompt, sr_prompt, ss_prompt, sg_sample, sr_sample, ss_sample, scratch):
    ctx = ExitStack()
    with ctx:
        sems = {}

        def S(name):
            if name not in sems:
                sems[name] = ctx.enter_context(nc.semaphore(name))
            return sems[name]

        ONCE = {
            "pe_step": (
                "cT_ps vec_ps shs_ps vs_ps ks_ps gz_ps kd_ps gst_ps gn_ps "
                "sr_ps ys_ps lg_ps lgt_ps rk_ps "),
            "act_step": (
                "c_silu in_small_a ks_evac g_ln eg kd_e gst_evac_a gst_evac gates_act "
                "gos_evac gla_sq gla_root kk_sq sv_w gn_sq gn_root lg_evac rt_e1 "
                "rt_e2 "),
            "dve_step": (
                "c_zeroed cT_ready vecs_ready shs_ready shift_mixed g_z g_log kd gla_ms "
                "gla_done lw kk_raw bonus_in sv_rest ck_zero rs_new ys_row y_all "
                "gn_c gn_ms rt_d1 rt_d2 routed cap_ready "),
        }

        def once(name):
            for sem, steps in ONCE.items():
                if name in steps.split():
                    return S(sem), steps.split().index(name) + 1
            raise KeyError(name)

        def sb(name, cols, rows=P, dt=F32):
            return ctx.enter_context(nc.sbuf_tensor(name, [rows, cols], dt))

        ring = sb("ring", MOE_SLOTS * RING)
        ta = ring[:, MIX_SLOTS * RING:MOE_SLOTS * RING]
        xt = sb("xt", KD * NT)[:].rearrange("p (k n) -> p k n", n=NT)
        ht_flat = sb("ht", KD * NT)
        ht = ht_flat[:].rearrange("p (k n) -> p k n", n=NT)
        pj_flat = sb("pj", NTILE * NT)
        pj = pj_flat[:].rearrange("p (k n) -> p k n", n=NT)
        mod = sb("mod", 8 * KD * COND)[:].rearrange("p (s k n) -> p s k n", s=8, n=COND)
        vecs = sb("vecs", V_END)
        ident = sb("ident", P)
        ones = sb("ones", P)
        bones = sb("bones", P)
        ct = sb("ct", KD * CPAD)[:].rearrange("p (k n) -> p k n", n=CPAD)
        lm = sb("lm", 8 * P)[:].rearrange("p (l n) -> p l n", n=P)
        mstrict = sb("mstrict", P)
        mincl = sb("mincl", CH)
        wa2 = ht_flat[:, 2112:3136]
        g2 = sb("g2", 1024)
        gw2 = ht_flat[0:GATE_RANK, 3136:3648]
        misc = sb("misc", 1040)
        ada_row = sb("ada_row", BANK)
        rstd = sb("rstd", NT)[:]
        tmp_s = sb("tmp_s", NS)[:]
        gscale = sb("gscale", KD * COND)[:].rearrange("p (k n) -> p k n", n=COND)
        shs = misc[:, 0:26 * NS].rearrange("p (t n) -> p t n", n=NS)
        pb = [ctx.enter_context(nc.psum_tensor(f"pb{i}", [P, BANK], F32)) for i in range(8)]

        x_tok = ta[:, 0:TC * D].rearrange("p (c d) -> p c d", d=D)
        x_row = ta[0:NS, TC * D:TC * D + D]
        c_row = ta[0:CPAD, TC * D + D:TC * D + 2 * D]
        small_w = ta[:, 0:KD * 272].rearrange("p (k c) -> p k c", c=272)
        shift_row = ta[0:NS, KD * 272:KD * 272 + RCOLS]
        vec_rows = pj_flat[:, 0:3 * P].rearrange("p (g c) -> p g c", c=P)
        idx_f = pj_flat[:, 512:640].bitcast(I32)
        idx_p = pj_flat[:, 640:768].bitcast(I32)
        idx_x = pj_flat[:, 768:896].bitcast(I32)
        xor_f = pj_flat[:, 896:1024]
        tri_f = pj_flat[:, 1024:1152]
        ge_f = pj_flat[:, 1152:1280]

        dl = ta[:, 0:26 * NT].rearrange("p (t n) -> p t n", n=NT)
        shift_out = ht_flat[0:COND, 0:RCOLS]
        cum = ta[:, 0:1024]
        cum4 = cum.rearrange("p (h n) -> p h n", n=NP_)
        e_flat = ta[:, 1024:2048]
        z4 = ta[:, 1024:2080].rearrange("p (h n) -> p h n", n=NT)
        l4 = ta[:, 2080:3136].rearrange("p (h n) -> p h n", n=NT)
        q4 = ta[:, 2080:3104].rearrange("p (h n) -> p h n", n=NP_)
        k4 = ta[:, 3104:4128].rearrange("p (h n) -> p h n", n=NP_)
        kd_tok = ta[:, 2080:3104].rearrange("p (c d) -> p c d", d=GLA_H * GLA_DK)
        v_tok = ta[:, 4128:6176].rearrange("p (c d) -> p c d", d=GLA_H * GLA_DV)
        at0 = ta[:, 6176:7200].rearrange("p (h n) -> p h n", n=NP_)
        at1 = ta[:, 7200:7712].rearrange("p (h n) -> p h n", n=P)
        sg_new = ta[:, 0:1024].rearrange("p (h e) -> p h e", e=GLA_DV)
        k_row, v_row = ht_flat[0:NS, 3648:4160], misc[0:NS, 0:1024]
        eg = rstd[:, 0:GLA_H * NS]
        gs = [ta[:, i * 2048:(i + 1) * 2048].rearrange("p (b e) -> p b e", e=GLA_DV) for i in range(2)]
        kz = ta[0:NS, 4128:5152].rearrange("p (b d) -> p b d", d=GLA_DK)
        gla_sq = ta[:, 5152:7264].rearrange("p (t n) -> p t n", n=NT)
        gla_r = pj[:, TQ:TQ + GLA_H, :]
        o_gla = ht[:, 0:8, :]
        W8 = NPAIR * NT

        def tiles8(flat):
            return flat.rearrange("p (t n) -> p t n", n=NT)

        ra, rb, bonus = (tiles8(pj_flat[:, i * W8:(i + 1) * W8]) for i in range(3))
        t0, t1, t2 = (tiles8(ta[:, i * W8:(i + 1) * W8]) for i in range(3))
        rr, rk, rv = pj[:, TR:TR + 8, :], pj[:, TK7:TK7 + 8, :], pj[:, TV7:TV7 + 8, :]
        sv = misc[:, 0:384].rearrange("p (t v b) -> p t v b", v=6, b=NS)
        svt = misc[:, 384:768].rearrange("p (v d) -> p v d", d=RD)
        sv_row = ht_flat[0:48, 2112:3136]
        wc = misc[:, 768:800].rearrange("p (t c) -> p t c", c=NCH)
        y8 = ht[:, 8:16, :]
        ar = ta[:, 0:768].rearrange("p (j n) -> p j n", n=192)
        bufs = [ta[:, 768 + i * 512:768 + (i + 1) * 512].rearrange("p (j n) -> p j n", n=P) for i in range(10)]
        bp, kp, vp, ltm, mtm, lo, tm, tt, pm, um = bufs
        rbm = ta[:, 5888:6144].rearrange("p (j n) -> p j n", n=CH)
        rkm = ta[:, 6144:6400].rearrange("p (j n) -> p j n", n=CH)
        st = ta[:, 6400:7424].rearrange("p (t n) -> p t n", n=P)
        sr_new = pj_flat[:, W8:W8 + 1024].rearrange("p (t n) -> p t n", n=P)
        rs = ta[:, 0:4096].rearrange("p (i j) -> p i j", j=RD)
        rt = ta[:, 4096:8192].rearrange("p (i j) -> p i j", j=RD)
        sa_row, y_row = misc[:, 800:864], misc[:, 864:928]
        at = [0]

        def room(cols):
            at[0] += cols
            return pj_flat[:, at[0] - cols:at[0]]

        w_rt = room(KD * 36).rearrange("p (k c) -> p k c", c=NG + NEXP)
        lg_t = room(NT)[0:NG + NEXP]
        lg = room(3 * 36).rearrange("p (c n) -> p c n", n=36)
        comb = room(3 * 34).rearrange("p (c e) -> p c e", e=NEXP + 2)
        slots = room(TC * 34).rearrange("p (c e) -> p c e", e=NEXP + 2)
        wide = room(3 * NEXP).rearrange("p (c g e) -> p c g e", g=NG, e=NE)
        pick, le, oh_1, oh_2 = (room(3 * NE).rearrange("p (c e) -> p c e", e=NE) for _ in range(4))
        g_exp, oh_g = (room(3 * NG).rearrange("p (c g) -> p c g", g=NG) for _ in range(2))
        top_g, top_1, top_2, least, e2, w_1, w_2 = (room(3) for _ in range(7))
        most_f, most = room(1), room(1).bitcast(I32)
        h_tok = room(TC * D).rearrange("p (c d) -> p c d", d=D)
        xg = room(2 * KD * SLOT).rearrange("p (q k s) -> p q k s", q=2, s=SLOT)
        y_slot = room(2 * 1024).rearrange("p (q d) -> p q d", q=2)
        sg = room(512).rearrange("p (q f) -> p q f", q=2)
        hid_t = room(512).rearrange("p (q f) -> p q f", q=2)
        pw = room(2 * 3 * P).rearrange("p (q c s) -> p q c s", q=2, c=3)
        disp = room(TC * P).rearrange("p (c s) -> p c s", c=TC)
        pwt = room(2 * NT).rearrange("p (q n) -> p q n", q=2)
        assert at[0] <= NTILE * NT
        h2s = misc[:, 0:KD * NS].rearrange("p (k n) -> p k n", n=NS)
        slot_no = misc[:, 128:256].rearrange("p (a s) -> p a s", a=2)
        own_slot = misc[0:NS, 256:384].rearrange("p (a s) -> p a s", a=2)
        own_w = comb[:, TC, :]
        eight = misc[:, 384:392]
        y_tok, ys_tok = h_tok, xg.rearrange("p q k s -> p (q k s)")[0:NS]

        def slot(s):
            return ring[:, s * RING:(s + 1) * RING]

        def ada_src(sec):
            return (w_ada[0, :, sec * D:(sec + 1) * D] if sec < 6 else
                    w_ada_final[:, (sec - 6) * D:(sec - 5) * D]).rearrange("(k p) c -> p k c", p=P)

        IN_ROUND, OUT_ROUND = 4, 22

        def ada_round(sec):
            return 2 * sec if isinstance(sec, int) and sec < 2 else sec * 2 + 6

        block = ctx.enter_context(nc.Block())

        class Chain:

            def __init__(self, eng, name):
                self.eng, self.sem, self.n = eng, S(name), 0

            def __call__(self, ins):
                self.n += 1
                ins.then_inc(self.sem, 1)
                self.eng.wait_ge(self.sem, self.n)

        def levels(flat, size):
            v = flat.rearrange("p (b n) -> p b n", n=size)
            return v, v[:, :, size // 2 - 1:size // 2].to_broadcast([P, GLA_H * NP_ // size, size])

        LEVELS = 8

        def inverse_step(dve, n, l):
            dve.wait_ge(S("iv_t"), n * 5 + l)
            last = dve.tensor_tensor(tt, tt, pb[3][:].rearrange("p (j n) -> p j n", n=P), ALU.add)
            if l < 5:
                last = dve.tensor_tensor(tm, tm, pb[4][:].rearrange("p (j n) -> p j n", n=P), ALU.add)
            last.then_inc(S("iv_tn"), 1)

        @block.sync
        def _(sp):
            def ring_wait(rnd, s):
                if rnd > 0:
                    sp.wait_ge(S("ring_free"), MIX_SLOTS * (rnd - 1) + s + 1)

            def ada_load(sec):
                src = ada_src(sec)
                for i in range(8):
                    rnd, s = ada_round(sec) + i // 4, i % 4
                    ring_wait(rnd, s)
                    sp.dma_start(slot(s).rearrange("p (k c) -> p k c", c=D), src[:, 2 * i:2 * i + 2, :])\
                        .then_inc(S(f"ring_full{s}"), 16)

            ada_load(M_SH1)
            ada_load(M_SC1)
            for pair in range(3):
                skip = (0, GATE_RANK, GATE_RANK + RD)[pair]
                with sp.Fori(2 * pair, 2 * pair + 2) as g:
                    for s in range(4):
                        sp.wait_ge(S("ring_free"), (g + IN_ROUND - 1) * 4 + s + 1)
                        src = w_in[0, :, bass.ds(g * 1024 + skip + s * 256, 256)]
                        sp.dma_start(slot(s).rearrange("p (k c) -> p k c", c=256),
                                     src.rearrange("(k p) c -> p k c", p=P)).then_inc(S(f"ring_full{s}"), 16)
            for sec in range(2, 8):
                ada_load(sec)
            for i in range(8):
                rnd, s = OUT_ROUND + i // 4, i % 4
                if rnd == OUT_ROUND:
                    ring_wait(rnd, s)
                else:
                    sp.wait_ge(S("out_ps"), 2 * s + 2)
                sp.dma_start(slot(s).rearrange("p (k c) -> p k c", c=256),
                             w_out[0, :, i * 256:(i + 1) * 256].rearrange("(k p) c -> p k c", p=P))\
                    .then_inc(S(f"ring_full{s}"), 16)
            sp.wait_ge(*once("ys_row"))
            sp.wait_ge(S("sr_out"), 48)

            def expert_load(expert, before=None):
                for s in range(MOE_SLOTS):
                    if before is not None:
                        sp.wait_ge(S("m_free"), before + (s + 1))
                    elif s < MIX_SLOTS:
                        sp.wait_ge(S("out_ps"), 8 + 2 * s + 2)
                    half, w = s % 2, (w_exp_gate, w_exp_up, w_exp_down)[s // 2]
                    src = w[0].rearrange("g e a b -> (g e) a b")[bass.ds(expert, 1)]
                    if s < 4:
                        src = src.rearrange("o (k p) f -> p (o k) f", p=P)[:, 8 * half:8 * half + 8, :]
                    else:
                        src = src.rearrange("o (k p) f -> p (o k) f", p=P)[:, 2 * half:2 * half + 2, :]
                    sp.dma_start(slot(s).rearrange("p (k f) -> p k f", f=src.shape[2]), src)\
                        .then_inc(S(f"m_full{s}"), 16)

            expert_load(0)
            with sp.Fori(1, NEXP) as e:
                expert_load(e, (e - 1) * MOE_SLOTS)
            sp.wait_ge(*once("cap_ready"))
            count = sp.value_load(most[0:1, 0:1], min_val=0, max_val=NP_)
            with sp.If(count > CAP):
                with sp.Fori(1, PASSES) as ps:
                    with sp.Fori(0, NEXP) as e:
                        expert_load(e, ps * (NEXP * MOE_SLOTS) + e * MOE_SLOTS - MOE_SLOTS)
            for c in range(TC):
                sp.wait_ge(S("yo_evac"), 4 * c + 4)
                sp.dma_start(y_prompt[0, c * P:(c + 1) * P, :], y_tok[:, c, :]).then_inc(S("y_out"), 16)
            sp.wait_ge(S("yo_evac"), 12)
            sp.dma_start(y_sample[:, 0, :], ys_tok).then_inc(S("y_out"), 16)
            sp.wait_ge(S("y_out"), 48)

        @block.gpsimd
        def _(pool):
            link = Chain(pool, "consts")
            link(pool.memset(ident[:], 0.0))
            link(pool.memset(bones[:], 0.0))
            link(pool.memset(ones[:], 1.0))
            pool.iota(idx_f, pattern=[[1, P]], base=0, channel_multiplier=0).then_inc(S("iotas"), 1)
            pool.iota(idx_p, pattern=[[0, P]], base=0, channel_multiplier=1).then_inc(S("iotas"), 1)
            link(pool.affine_select(out=ident[:], in_=ident[:], compare_op=ALU.not_equal, fill=1.0, base=0,
                                    pattern=[[-1, P]], channel_multiplier=1))
            link(pool.affine_select(out=mstrict[:], in_=ones[:], compare_op=ALU.is_gt, fill=0.0, base=0,
                                    pattern=[[1, P]], channel_multiplier=-1))
            for h in range(2):
                r = slice(RD * h, RD * h + RD)
                link(pool.memset(bones[r, r], 1.0))
                link(pool.affine_select(out=mincl[r, :], in_=ones[r, 0:CH], compare_op=ALU.is_ge, fill=0.0, base=0,
                                        pattern=[[1, CH]], channel_multiplier=-1))
            assert link.n == N_CONSTS
            pool.wait_ge(S("xT_ps"), KD)
            pool.wait_ge(*once("cT_ready"))
            for tile, part, col, width in SHIFT_PARTS:
                at = tile * P + part
                pool.dma_start(shift_row[:, at:at + width], state_shift[0, :, col:col + width])\
                    .then_inc(S("shift_in"), 16)
            cols = [(0, GCOLS + 1024, RD), (RD, GCOLS + 3136, RD), (2 * RD, GCOLS + 3200, P), (4 * RD, 2048, GATE_RANK)]
            for at, col, width in cols:
                pool.dma_start(small_w[:, :, at:at + width],
                               w_in[0, :, col:col + width].rearrange("(k p) c -> p k c", p=P))\
                    .then_inc(S("small_w_in"), 16)
            pool.wait_ge(S("so_evac"), 7)
            for tile, part, col, width in SHIFT_PARTS:
                at = tile * P + part
                pool.dma_start(ss_prompt[0, :, col:col + width], shift_out[0:1, at:at + width]).then_inc(S("ss_out"), 16)
                pool.dma_start(ss_sample[0, :, col:col + width], shift_out[1:COND, at:at + width])\
                    .then_inc(S("ss_out"), 16)
            pool.wait_ge(S("ss_out"), 16 * 2 * len(SHIFT_PARTS))
            pool.dma_start(wa2[0:RD, :], rwkv_w2[0]).then_inc(S("low_rank_in"), 16)
            pool.dma_start(wa2[RD:P, :], rwkv_a2[0]).then_inc(S("low_rank_in"), 16)
            pool.dma_start(gw2, gla_gate_w2[0]).then_inc(S("low_rank_in"), 16)
            pool.wait_ge(*once("gst_evac"))
            pool.dma_start(sg_prompt[0, 0].rearrange("h k v -> k h v"), sg_new).then_inc(S("sg_out"), 16)
            pool.wait_ge(S("sg_out"), 16)
            for h in range(GLA_H):
                if h >= 2:
                    pool.wait_ge(S("sgs_out"), 16 * (h - 1))
                    pool.wait_ge(S("gs_o"), h - 1)
                pool.dma_start(gs[h % 2], state_gla[0, :, h].rearrange("b k v -> k b v")).then_inc(S(f"sgs_in{h % 2}"), 16)
                if h >= 1:
                    pool.wait_ge(S("gs_s"), h)
                    pool.dma_start(sg_sample[0, :, h - 1].rearrange("b k v -> k b v"), gs[(h - 1) % 2])\
                        .then_inc(S("sgs_out"), 16)
            pool.wait_ge(S("gs_s"), GLA_H)
            pool.dma_start(sg_sample[0, :, GLA_H - 1].rearrange("b k v -> k b v"), gs[(GLA_H - 1) % 2])\
                .then_inc(S("sgs_out"), 16)
            pool.wait_ge(S("sgs_out"), 16 * GLA_H)
            pool.wait_ge(S("sv_evac"), 2)
            pool.dma_start(scratch, sv_row).then_inc(S("sv_store"), 16)
            pool.wait_ge(S("sv_store"), 16)
            for v in range(6):
                pool.dma_start(svt[:, v, :], scratch[v * NS:(v + 1) * NS, :].rearrange("b (h d) -> (b h) d", d=RD))\
                    .then_inc(S("sv_in"), 16)
            pool.wait_ge(S("sv_in"), 96)
            pool.wait_ge(*once("sr_ps"))
            pool.dma_start(rs, state_rwkv[0].rearrange("b h i j -> (b h) i j")).then_inc(S("rs_in"), 16)
            pool.wait_ge(S("sr_evac"), 2)
            for h in range(2):
                r = slice(RD * h, RD * h + RD)
                pool.dma_start(sr_prompt[0, 0].rearrange("(p h) i j -> h i p j", h=2)[h], sr_new[r, :, r])\
                    .then_inc(S("sr_out"), 16)
            pool.wait_ge(*once("rs_new"))
            pool.dma_start(sr_sample[0].rearrange("b h i j -> (b h) i j"), rs).then_inc(S("sr_out"), 16)
            pool.wait_ge(S("sr_out"), 48)
            pool.wait_ge(S("o_rwkv"), 8)
            pool.dma_start(w_rt[:, :, 0:NG], w_router_group[0].rearrange("(k p) c -> p k c", p=P)).then_inc(S("rt_in"), 16)
            pool.dma_start(w_rt[:, :, NG:NG + NEXP], w_router_expert[0].rearrange("(k p) c -> p k c", p=P))\
                .then_inc(S("rt_in"), 16)
            rlink = Chain(pool, "rt_consts")
            rlink(pool.iota(slot_no, pattern=[[0, 2], [1, SLOT]], base=0, channel_multiplier=0,
                            allow_small_or_imprecise_dtypes=True))
            rlink(pool.iota(eight, pattern=[[1, NE]], base=0, channel_multiplier=0, allow_small_or_imprecise_dtypes=True))
            rlink(pool.memset(own_slot, 0.0))
            rlink(pool.tensor_copy(own_slot[:, :, 0:NS], ident[0:NS, 0:NS].unsqueeze(1).to_broadcast([NS, 2, NS])))

        @block.scalar
        def _(act):
            act.dma_start(x_tok, x_prompt[0].rearrange("(c p) d -> p c d", p=P)).then_inc(S("x_in"), 16)
            act.dma_start(x_row, x_sample[:, 0, :]).then_inc(S("x_in"), 16)
            act.wait_ge(*once("c_zeroed"))
            act.dma_start(c_row[0:1, :], c_prompt).then_inc(S("c_in"), 16)
            act.dma_start(c_row[1:COND, :], c_sample).then_inc(S("c_in"), 16)
            rows = [[b_ada[0], b_ada_final],
                    [norm_mix[0], norm_ffn[0], norm_final, rwkv_mu[0, 0:1024], rwkv_mu[0, 1088:2112],
                     rwkv_mu[0, 2112:3136], (rwkv_mu[0, 1024:1088], 0), (rwkv_mu[0, 3136:3200], RD),
                     rwkv_mu[0, 3200:3328], gla_gate_b[0], gla_norm[0]],
                    [rwkv_w0[0], rwkv_a0[0], rwkv_k_k[0], rwkv_k_a[0], rwkv_r_k[0].rearrange("h d -> (h d)"),
                     rwkv_gn_w[0], rwkv_gn_b[0]]]
            n_vec = 0
            for g, group in enumerate(rows):
                at = 0
                for v in group:
                    if isinstance(v, tuple):
                        v, c = v
                        act.dma_start(vec_rows[at:at + 1, g, c:c + RD], v.rearrange("(r c) -> r c", c=RD))\
                            .then_inc(S("vec_in"), 16)
                        at += c // RD
                    else:
                        n = v.shape[0] // P
                        act.dma_start(vec_rows[at:at + n, g, :], v.rearrange("(r c) -> r c", c=P))\
                            .then_inc(S("vec_in"), 16)
                        at += n
                    n_vec += 1
            assert n_vec == N_VEC
            act.dma_start(g2[:], rwkv_g2[0]).then_inc(S("g2_in"), 16)
            act.wait_ge(S("c_in"), 32)
            act.activation(c_row, c_row, ACT.Silu).then_inc(once("c_silu")[0], 1)
            for k in range(KD):
                act.wait_ge(S("xT_ps"), k + 1)
                act.copy(xt[:, k, :], pb[2 + k % 4][:, 0:NT]).then_inc(S("xT_evac"), 1)

            def square(sem, out, in_):
                act.activation(out, in_, ACT.Square).then_inc(S(sem), 1)

            def root(n):
                act.wait_ge(S("ms_sum"), n)
                act.activation(rstd, rstd, ACT.Sqrt).then_inc(S("rms_root"), 1)

            act.wait_ge(S("xT_evac"), KD)
            square("norm_sq", ht[:, :, :], xt[:, :, :])
            root(1)

            def ada(sec):
                n = sec
                act.wait_ge(S("ring_free"), (ada_round(sec) + 2) * 4)
                act.wait_ge(S("ada_tr"), n)
                act.copy(ada_row[:], pb[7][:]).then_inc(S("ada_evac"), 1)

            ada(M_SH1)
            ada(M_SC1)
            for k in range(8, KD):
                act.wait_ge(S("mod_g"), 1)
                act.activation(ht[:, k, 0:NP_], ht[:, k, 0:NP_], ACT.Identity, bias=mod[:, M_SH1, k, 0:1],
                               scale=gscale[:, k, 0:1]).then_inc(S("h_act"), 1)
            with act.Fori(0, 6) as g:
                for t in range(0, 8, 2):
                    act.wait_ge(S("in_ps"), g * 4 + t // 2 + 1)
                    act.copy(pj[:, bass.ds(g * 8 + t, 1), :], pb[t % 4][:, 0:NT].rearrange("p (o n) -> p o n", o=1))\
                        .then_inc(S("in_evac_a"), 1)
            act.wait_ge(S("in_small"), 2)
            act.copy(pj[:, TG7, :], pb[1][:, 0:NT]).then_inc(once("in_small_a")[0], 1)
            for b in range(7):
                act.wait_ge(S("so_ps"), b + 1)
                n = min(BANK, RCOLS - b * BANK)
                act.copy(shift_out[:, b * BANK:b * BANK + n], pb[3 + b % 2][0:COND, 0:n]).then_inc(S("so_evac"), 1)
            act.wait_ge(*once("shift_mixed"))
            for b in range(4):
                act.wait_ge(S("vt_ps"), b + 1)
                act.copy(v_tok[:, b // 2, (b % 2) * BANK:(b % 2 + 1) * BANK], pb[b][:]).then_inc(S("vt_evac"), 1)
            act.wait_ge(*once("vs_ps"))
            for b in range(2):
                act.copy(v_row[:, b * BANK:(b + 1) * BANK], pb[4 + b][0:NS, :]).then_inc(S("vs_evac"), 1)
            act.wait_ge(*once("ks_ps"))
            act.copy(k_row, pb[0][0:NS, :]).then_inc(once("ks_evac")[0], 1)
            ada(2)
            act.wait_ge(*once("g_z"))
            link = Chain(act, "act_chain")
            link(act.activation(l4, z4, ACT.Abs))
            link(act.activation(l4, l4, ACT.Exp, scale=-1.0))
            act.activation(l4, l4, ACT.Ln, bias=1.0).then_inc(once("g_ln")[0], 1)
            act.wait_ge(*once("g_log"))
            act.activation(eg.rearrange("p (h b) -> p h b", b=NS), z4[:, :, NP_:NT], ACT.Exp).then_inc(once("eg")[0], 1)
            for l in range(LEVELS):
                act.wait_ge(S("lv_d"), l + 1)
                link(act.activation(e_flat, e_flat, ACT.Abs))
                act.activation(e_flat, e_flat, ACT.Exp, scale=-1.0).then_inc(S("lv_e"), 1)
            ada(3)
            act.wait_ge(S("lv_qk"), LEVELS)
            for h in range(GLA_H):
                last = act.activation(e_flat[:, h * NP_:(h + 1) * NP_], cum4[:, h, :], ACT.Exp, scale=-1.0,
                                      bias=cum4[:, h, NP_ - 1:NP_])
            last.then_inc(once("kd_e")[0], 1)
            act.wait_ge(*once("kd_ps"))
            for c in range(TC):
                act.copy(kd_tok[:, c, :], pb[4 + c][:]).then_inc(S("kd_evac"), 1)
            act.wait_ge(S("ss_out"), 16 * 2 * len(SHIFT_PARTS))
            for b in range(4):
                act.wait_ge(S("go_ps"), b + 1)
                act.copy(ht[:, 2 * b:2 * b + 2, 0:NP_], pb[b][:].rearrange("p (t n) -> p t n", n=NP_))\
                    .then_inc(S("go_evac"), 1)
            act.wait_ge(*once("gst_ps"))
            act.wait_ge(*once("kd_e"))
            act.copy(sg_new[:, 0:2, :], pb[4][:].rearrange("p (h e) -> p h e", e=GLA_DV)).then_inc(once("gst_evac_a")[0], 1)
            act.wait_ge(*once("gst_evac_a"))
            act.copy(sg_new[:, 2:4, :], pb[5][:].rearrange("p (h e) -> p h e", e=GLA_DV)).then_inc(once("gst_evac")[0], 1)
            link(act.activation(pj[:, TOG:TOG + 8, :], pj[:, TOG:TOG + 8, :], ACT.Silu))
            link(act.activation(pj[0:RD, TWA, :], pj[0:RD, TWA, :], ACT.Tanh))
            act.activation(pj[:, TG7, :], pj[:, TG7, :], ACT.Sigmoid).then_inc(once("gates_act")[0], 1)
            act.wait_ge(S("gs_o"), GLA_H)
            act.copy(ht[:, 0:8, NP_:NT], pb[4][:, 0:64].rearrange("p (t b) -> p t b", b=NS)).then_inc(once("gos_evac")[0], 1)
            act.wait_ge(*once("gos_evac"))
            act.wait_ge(S("go_evac"), 4)
            act.activation(gla_sq, o_gla, ACT.Square).then_inc(once("gla_sq")[0], 1)
            act.wait_ge(*once("gla_ms"))
            act.activation(gla_r, gla_r, ACT.Sqrt).then_inc(once("gla_root")[0], 1)
            act.wait_ge(S("sgs_out"), 16 * GLA_H)
            act.wait_ge(*once("gla_done"))
            for i in range(16):
                t = i % 8
                act.wait_ge(S("rs_ps"), i + 1)
                dst, at = ((t0, V_W0), (rb, V_A0))[i // 8]
                act.activation(dst[:, t, :], pb[i % 4][:, 0:NT], ACT.Sigmoid, bias=vecs[:, at + t:at + t + 1])\
                    .then_inc(S("rs_evac"), 1)
            act.wait_ge(*once("kk_raw"))
            act.activation(t2, ra, ACT.Square).then_inc(once("kk_sq")[0], 1)
            for t in range(8):
                act.wait_ge(S("kn_ps"), t + 1)
                act.activation(t1[:, t, :], pb[t % 4][:, 0:NT], ACT.Sqrt).then_inc(S("kn_evac"), 1)
            act.wait_ge(*once("lw"))
            act.activation(sv[:, :, 1, :], t0[:, :, NP_:NT], ACT.Exp).then_inc(once("sv_w")[0], 1)
            for b in range(2):
                act.wait_ge(S("sv_ps"), b + 1)
                act.copy(sv_row[:, b * BANK:(b + 1) * BANK], pb[b][0:48, :]).then_inc(S("sv_evac"), 1)
            for i, scale in enumerate((1.0, 1.0, -1.0)):
                act.wait_ge(S("cw_e"), i + 1)
                src = t2 if i == 0 else t1
                act.activation(t2[:, :, 0:NP_], src[:, :, 0:NP_], ACT.Exp, scale=scale).then_inc(S("cw_exp"), 1)

            act.wait_ge(S("sv_store"), 16)
            with act.Fori(0, NCH) as c:
                for hf in range(2):
                    n = c * 2 + hf
                    js = slice(4 * hf, 4 * hf + 4)
                    act.wait_ge(S("ck_y"), n)
                    act.wait_ge(*once("ck_zero"))
                    for h in range(2):
                        r = slice(CH * h, CH * h + CH)
                        act.copy(kp[r, :, r], rk[r, js, bass.ds(c * CH, CH)])
                        last = act.copy(vp[r, :, r], rv[r, js, bass.ds(c * CH, CH)])
                    last.then_inc(S("ck_pad_a"), 1)
                    act.wait_ge(S("ck_t1"), n + 1)
                    act.copy(bp, pb[4][:].rearrange("p (j n) -> p j n", n=P))
                    act.copy(kp, pb[5][:].rearrange("p (j n) -> p j n", n=P)).then_inc(S("ck_t1e"), 1)
                    act.wait_ge(S("ck_t2"), n + 1)
                    act.copy(vp, pb[0][:].rearrange("p (j n) -> p j n", n=P)).then_inc(S("ck_t2e"), 1)
                    act.wait_ge(S("ck_t0"), n + 1)
                    act.copy(tm, pb[1][:].rearrange("p (j n) -> p j n", n=P)).then_inc(S("ck_t0e"), 1)
                    act.wait_ge(S("ck_u"), n + 1)
                    act.copy(um, pb[5][:].rearrange("p (j n) -> p j n", n=P)).then_inc(S("ck_ue"), 1)
                    for l in range(1, 6):
                        act.wait_ge(S("iv_p"), n * 5 + l)
                        act.copy(pm, pb[2][:].rearrange("p (j n) -> p j n", n=P)).then_inc(S("iv_pe"), 1)
                    act.wait_ge(S("ck_sa"), n + 1)
                    act.copy(tm, pb[1][:].rearrange("p (j n) -> p j n", n=P)).then_inc(S("ck_sae"), 1)
                    act.wait_ge(S("ck_y"), n + 1)
                    act.copy(y8[:, js, bass.ds(c * CH, CH)], pb[2][:, 0:4 * CH].rearrange("p (j n) -> p j n", n=CH))\
                        .then_inc(S("ck_yev"), 1)
                ada(c + 4)
            act.wait_ge(*once("sr_ps"))
            for b in range(2):
                act.copy(sr_new[:, 4 * b:4 * b + 4, :], pb[b][:].rearrange("p (j n) -> p j n", n=P))\
                    .then_inc(S("sr_evac"), 1)
            act.wait_ge(*once("gn_c"))
            act.activation(ra, y8, ACT.Square).then_inc(once("gn_sq")[0], 1)
            act.wait_ge(*once("gn_ms"))
            act.activation(rr, rr, ACT.Sqrt).then_inc(once("gn_root")[0], 1)

            def scale_upper(n, sh):
                for k in range(8, KD):
                    act.wait_ge(S("mod_g"), n)
                    act.activation(ht[:, k, 0:NP_], ht[:, k, 0:NP_], ACT.Identity, bias=mod[:, sh, k, 0:1],
                                   scale=gscale[:, k, 0:1]).then_inc(S("h_act"), 1)

            act.wait_ge(S("x1"), KD)
            square("norm_sq", ht[:, :, :], xt[:, :, :])
            root(2)
            scale_upper(2, M_SH2)
            act.wait_ge(*once("lg_ps"))
            act.copy(lg_t, pb[1][0:NG + NEXP, 0:NT]).then_inc(once("lg_evac")[0], 1)
            for b in range(8):
                act.wait_ge(S("h2t_ps"), b + 1)
                act.copy(h_tok[:, b // 4, (b % 4) * BANK:(b % 4 + 1) * BANK], pb[3 + b % 4][:]).then_inc(S("h2t_evac"), 1)
            act.wait_ge(*once("rt_d1"))
            act.activation(g_exp, g_exp, ACT.Exp).then_inc(once("rt_e1")[0], 1)
            act.wait_ge(*once("rt_d2"))
            act.activation(e2, e2, ACT.Exp).then_inc(once("rt_e2")[0], 1)

            def moe_gather_out(n):
                for b in range(2):
                    act.wait_ge(S("m_ga"), n * 4 + (b + 1))
                    act.copy(xg[:, :, 4 * b:4 * b + 4, :], pb[b][:].rearrange("p (k q s) -> p q k s", q=2, s=SLOT))\
                        .then_inc(S("m_ga_a"), 1)

            def moe_act(ps):
                moe_gather_out(ps * 17)
                with act.Fori(0, NEXP // 2) as i:
                    t = ps * 16 + i
                    for q in range(2):
                        used = (t * 2 + q) * MOE_SLOTS
                        act.wait_ge(S(f"m_wt{q}"), t + 1)
                        act.copy(pwt[:, q, :], pb[5 - q][:, 0:NT]).then_inc(S(f"m_wte{q}"), 1)
                        act.wait_ge(S("m_free"), used + 4)
                        act.activation(sg[:, q, :], pb[4 + q][:, 0:256], ACT.Silu).then_inc(S(f"m_sg{q}"), 1)
                        if q == 1:
                            moe_gather_out(ps * 17 + i + 1)
                        act.wait_ge(S(f"m_hp{q}"), t + 1)
                        act.copy(hid_t[:, q, :], pb[4 + q][:, 0:256]).then_inc(S(f"m_ht{q}"), 1)
                        act.wait_ge(S("m_free"), used + 6)
                        act.wait_ge(S(f"m_sc{q}"), (t + q) * KD + ps * (KD if q else 0))
                        act.copy(y_slot[:, q, 0:BANK], pb[6][:])
                        act.copy(y_slot[:, q, BANK:2 * BANK], pb[7][:]).then_inc(S(f"m_ye{q}"), 1)

            moe_act(0)
            act.wait_ge(*once("cap_ready"))
            count = act.value_load(most[0:1, 0:1], min_val=0, max_val=NP_)
            with act.If(count > CAP):
                with act.Fori(1, PASSES) as ps:
                    moe_act(ps)
            act.wait_ge(S("x2"), 1)
            square("norm_sq", ht[:, :, :], xt[:, :, :])
            root(3)
            scale_upper(3, M_SHF)
            for b in range(0, 12, 2):
                act.wait_ge(S("yo_ps"), b + 1)
                dst = (y_tok[:, b // 4, (b % 4) * BANK:(b % 4 + 1) * BANK] if b < 8 else
                       ys_tok[:, (b - 8) * BANK:(b - 7) * BANK])
                act.wait_ge(S("yo_evac"), b)
                act.copy(dst, pb[1 + b % 4][0:dst.shape[0], :]).then_inc(S("yo_evac"), 1)

        @block.vector
        def _(dve):
            link = Chain(dve, "dve_chain")
            dve.memset(c_row, 0.0).then_inc(once("c_zeroed")[0], 1)
            dve.wait_ge(S("iotas"), 2)
            link(dve.tensor_tensor(idx_x, idx_f, idx_p, ALU.bitwise_xor))
            dve.tensor_copy(xor_f, idx_x)
            link(dve.tensor_tensor(tri_f, idx_f, idx_p, ALU.is_gt))
            dve.tensor_scalar(lm[:, 7, :], xor_f, 0.0, None, ALU.is_equal)
            link(dve.tensor_tensor(tri_f, xor_f, tri_f, ALU.mult))
            for l in range(7):
                link(dve.tensor_scalar(ge_f, tri_f, float(2 ** l), None, ALU.is_ge))
                link(dve.scalar_tensor_tensor(out=lm[:, l, :], in0=tri_f, scalar=float(2 ** (l + 1)), in1=ge_f,
                                              op0=ALU.is_lt, op1=ALU.mult))
            dve.wait_ge(*once("cT_ps"))
            dve.tensor_copy(ct[:, :, :], pb[0][:].rearrange("p (k n) -> p k n", n=CPAD)).then_inc(once("cT_ready")[0], 1)
            dve.wait_ge(*once("vec_ps"))
            dve.tensor_copy(vecs[:], pb[1][:, 0:V_END]).then_inc(once("vecs_ready")[0], 1)
            dve.wait_ge(*once("vecs_ready"))

            def vec(at, n, m):
                return vecs[:, at:at + n].unsqueeze(2).to_broadcast([P, n, m])

            def rms_start(n):
                dve.wait_ge(S("ms_ps"), n)
                dve.tensor_scalar(rstd, pb[0][:, 0:NT], 1.0 / D, EPS, ALU.mult, ALU.add).then_inc(S("ms_sum"), 1)
                dve.wait_ge(S("rms_root"), n)
                link(dve.reciprocal(rstd, rstd))
                link(dve.tensor_tensor(ht[:, :, :], xt[:, :, :], rstd.unsqueeze(1).to_broadcast([P, KD, NT]), ALU.mult))

            def modulate(n, norm, sc, sh):
                dve.scalar_tensor_tensor(out=gscale[:, :, :], in0=mod[:, sc], scalar=1.0, in1=vec(norm, KD, COND),
                                         op0=ALU.add, op1=ALU.mult).then_inc(S("mod_g"), 1)
                dve.wait_ge(S("mod_g"), n)
                for k in range(8):
                    dve.tensor_scalar(ht[:, k, 0:NP_], ht[:, k, 0:NP_], gscale[:, k, 0:1], mod[:, sh, k, 0:1],
                                      ALU.mult, ALU.add)
                link(dve.tensor_tensor(ht[:, :, NP_:NT], ht[:, :, NP_:NT], gscale[:, :, 1:COND], ALU.mult))
                dve.tensor_tensor(ht[:, :, NP_:NT], ht[:, :, NP_:NT], mod[:, sh, :, 1:COND], ALU.add)\
                    .then_inc(S("h_dve"), 1)

            def ada(sec):
                n = sec
                dve.wait_ge(S("ada_tr"), n + 1)
                src = pb[6][:].rearrange("p (j g r) -> p g j r", j=4, g=4)[:, :, :, 0:COND]
                dst = mod[:, bass.ds(sec, 1)].rearrange("p o (g j) r -> p (o g) j r", g=4)
                b = vecs[:, bass.ds(sec * KD + V_ADA, KD)].rearrange("p (g j) -> p g j", g=4)
                dve.tensor_tensor(dst, src, b.unsqueeze(3).to_broadcast([P, 4, 4, COND]), ALU.add)\
                    .then_inc(S("ada_mod"), 1)

            rms_start(1)
            ada(M_SH1)
            ada(M_SC1)
            dve.wait_ge(S("ada_mod"), 2)
            modulate(1, V_NMIX, M_SC1, M_SH1)
            with dve.Fori(0, 6) as g:
                for t in range(1, 8, 2):
                    dve.wait_ge(S("ring_free"), g * 4 + IN_ROUND * 4 + t // 2 + 1)
                    dve.tensor_copy(pj[:, bass.ds(g * 8 + t, 1), :], pb[t % 4][:, 0:NT].rearrange("p (o n) -> p o n", o=1))\
                        .then_inc(S("in_evac_d"), 1)
            dve.wait_ge(S("in_small"), 1)
            dve.tensor_copy(pj[:, TWA, :], pb[0][:, 0:NT]).then_inc(S("in_small_d"), 1)
            dve.wait_ge(S("in_small"), 3)
            dve.tensor_copy(pj[0:GATE_RANK, TGL, :], pb[2][0:GATE_RANK, 0:NT]).then_inc(S("in_small_d"), 1)
            dve.wait_ge(*once("shs_ps"))
            dve.tensor_copy(shs, pb[5][:, 0:26 * NS].rearrange("p (t n) -> p t n", n=NS)).then_inc(once("shs_ready")[0], 1)
            dve.wait_ge(*once("shs_ready"))
            dve.wait_ge(S("in_evac_a"), 24)
            dve.wait_ge(S("in_evac_d"), 24)
            dve.wait_ge(*once("in_small_a"))
            dve.wait_ge(S("in_small_d"), 2)
            rp = pj[:, TR:TG7 + 1, :]
            dve.tensor_tensor(dl[:, :, 1:NP_], rp[:, :, 0:NP_ - 1], rp[:, :, 1:NP_], ALU.subtract)
            dve.tensor_scalar(dl[:, :, 0:1], rp[:, :, 0:1], -1.0, None, ALU.mult)
            link(dve.tensor_tensor(dl[:, :, NP_:NT], shs, rp[:, :, NP_:NT], ALU.subtract))
            link(dve.tensor_tensor(dl, dl, vec(V_MU, 26, NT), ALU.mult))
            dve.wait_ge(S("so_ps"), 7)
            dve.tensor_tensor(rp, rp, dl, ALU.add).then_inc(once("shift_mixed")[0], 1)
            dve.wait_ge(*once("shift_mixed"))
            dve.wait_ge(*once("gz_ps"))
            for h in range(GLA_H):
                last = dve.tensor_scalar(z4[:, h, :], pb[h][:, 0:NT], vecs[:, V_GB + h:V_GB + h + 1], None, ALU.add)
            last.then_inc(once("g_z")[0], 1)
            link(dve.tensor_scalar(pj[:, TQ:TQ + 4, :], pj[:, TQ:TQ + 4, :], GLA_DK ** -0.5, None, ALU.mult))
            ada(2)
            dve.memset(at0[:, :, 0:P], 0.0)
            link(dve.memset(at1, 0.0))
            dve.wait_ge(*once("g_ln"))
            link(dve.scalar_tensor_tensor(out=z4, in0=z4, scalar=0.0, in1=l4, op0=ALU.min, op1=ALU.subtract))
            dve.tensor_scalar(z4, z4, 1.0 / 16.0, None, ALU.mult).then_inc(once("g_log")[0], 1)
            dve.wait_ge(*once("g_log"))
            for h in range(GLA_H):
                last = dve.tensor_tensor_scan(cum4[:, h, :], ones[:, 0:1].to_broadcast([P, NP_]), z4[:, h, 0:NP_], 0.0,
                                              ALU.mult, ALU.add)
            link(last)
            dve.wait_ge(*once("eg"))

            def level_diff(l):
                b, ref = levels(cum, NP_ >> l)
                e, _ = levels(e_flat, NP_ >> l)
                dve.tensor_tensor(e, b, ref, ALU.subtract).then_inc(S("lv_d"), 1)

            level_diff(0)
            e4 = e_flat.rearrange("p (h n) -> p h n", n=NP_)
            for l in range(LEVELS + 1):
                if l < LEVELS:
                    dve.wait_ge(S("lv_e"), l + 1)
                    if l > 0:
                        dve.wait_ge(S("lv_ps"), l)
                    dve.tensor_tensor(q4, pj[:, TQ:TQ + 4, 0:NP_], e4, ALU.mult)
                    dve.tensor_tensor(k4, pj[:, TK:TK + 4, 0:NP_], e4, ALU.mult).then_inc(S("lv_qk"), 1)
                if l + 1 < LEVELS:
                    dve.wait_ge(S("lv_qk"), l + 1)
                    level_diff(l + 1)
                dve.wait_ge(S("lv_ps"), l + 1)
                b = 2 * (l % 2)
                src = [pb[b + i][:].rearrange("p (h n) -> p h n", n=P) for i in range(2)]
                if l == 0:
                    dve.tensor_copy(at0[:, :, P:NP_], src[0]).then_inc(S("lv_sel"), 1)
                    continue
                m = lm[:, 7 - l if l < LEVELS else 7, :].bitcast(I32).unsqueeze(1).to_broadcast([P, GLA_H, P])
                dve.wait_ge(S("lv_sel"), l)
                dve.copy_predicated(at0[:, :, 0:P], m, src[0])
                dve.copy_predicated(at1, m, src[1]).then_inc(S("lv_sel"), 1)
            ada(3)
            dve.wait_ge(*once("kd_e"))
            dve.wait_ge(S("lv_ps"), LEVELS + 1)
            dve.tensor_tensor(k4, pj[:, TK:TK + 4, 0:NP_], e4, ALU.mult).then_inc(once("kd")[0], 1)
            for h in range(GLA_H):
                if h == 0:
                    dve.wait_ge(*once("ks_evac"))
                    dve.wait_ge(*once("gst_evac"))
                if h > 0:
                    dve.wait_ge(S("gs_kv"), 4 * h)
                dve.tensor_tensor(kz, k_row[:, h * GLA_DK:(h + 1) * GLA_DK].unsqueeze(1).to_broadcast([NS, NS, GLA_DK]),
                                  ident[0:NS, 0:NS].unsqueeze(2).to_broadcast([NS, NS, GLA_DK]), ALU.mult)\
                    .then_inc(S("kz"), 1)
                dve.wait_ge(S(f"sgs_in{h % 2}"), 16 * (h // 2 + 1))
                for b in range(NS):
                    if b % 2 == 0:
                        dve.wait_ge(S("gs_kv"), 4 * h + b // 2 + 1)
                    last = dve.scalar_tensor_tensor(
                        out=gs[h % 2][:, b, :], in0=gs[h % 2][:, b, :], scalar=eg[:, h * NS + b:h * NS + b + 1],
                        in1=pb[b // 2][:, (b % 2) * GLA_DV:(b % 2 + 1) * GLA_DV], op0=ALU.mult, op1=ALU.add)
                last.then_inc(S("gs_s"), 1)
            dve.wait_ge(*once("gn_ps"))
            for h in range(GLA_H):
                last = dve.tensor_scalar(gla_r[:, h, :], pb[h][:, 0:NT], 1.0 / GLA_DV, GLA_EPS, ALU.mult, ALU.add)
            last.then_inc(once("gla_ms")[0], 1)
            dve.wait_ge(*once("gla_root"))
            link(dve.reciprocal(gla_r, gla_r))
            oh = o_gla.rearrange("p (h e) n -> p h e n", e=2)
            link(dve.tensor_tensor(oh, oh, gla_r.unsqueeze(2).to_broadcast([P, GLA_H, 2, NT]), ALU.mult))
            og = pj[:, TOG:TOG + 8, :].rearrange("p (h e) n -> p h e n", e=2)
            dve.wait_ge(*once("gates_act"))
            for e in range(2):
                last = dve.scalar_tensor_tensor(out=oh[:, :, e, :], in0=oh[:, :, e, :], scalar=vecs[:, V_GN + e:V_GN + e + 1],
                                                in1=og[:, :, e, :], op0=ALU.mult, op1=ALU.mult)
            last.then_inc(once("gla_done")[0], 1)
            dve.wait_ge(*once("gla_done"))
            dve.wait_ge(S("rs_evac"), 8)
            dve.tensor_scalar(t0, t0, -HALF_E, None, ALU.mult).then_inc(once("lw")[0], 1)
            dve.tensor_tensor(ra, rk, vec(V_KK, 8, NT), ALU.mult).then_inc(once("kk_raw")[0], 1)
            dve.wait_ge(*once("kk_raw"))
            dve.wait_ge(S("kn_evac"), 8)
            link(dve.tensor_scalar(t1, t1, 1e-12, None, ALU.max))
            link(dve.reciprocal(t1, t1))
            link(dve.tensor_tensor(ra, ra, t1, ALU.mult))
            dve.wait_ge(S("rs_evac"), 16)
            link(dve.scalar_tensor_tensor(out=t1, in0=rb, scalar=1.0, in1=vec(V_KA, 8, NT), op0=ALU.subtract, op1=ALU.mult))
            link(dve.scalar_tensor_tensor(out=rk, in0=t1, scalar=1.0, in1=rk, op0=ALU.add, op1=ALU.mult))
            link(dve.tensor_tensor(rb, rb, ra, ALU.mult))
            link(dve.tensor_tensor(t1, rr, rk, ALU.mult))
            dve.tensor_tensor(t1, t1, vec(V_RK, 8, NT), ALU.mult).then_inc(once("bonus_in")[0], 1)
            for v, src in ((0, rr), (2, rk), (3, rv), (4, ra), (5, rb)):
                last = dve.tensor_copy(sv[:, :, v, :], src[:, :, NP_:NT])
            last.then_inc(once("sv_rest")[0], 1)
            for t in range(8):
                dve.wait_ge(S("bonus_ps"), t + 1)
                dve.tensor_tensor(bonus[:, t, :], pb[2 + t % 2][:, 0:NT], rv[:, t, :], ALU.mult).then_inc(S("bonus_evac"), 1)
            dve.wait_ge(S("bonus_evac"), 8)
            keep = t2[:, 0, 0:NP_]
            dve.wait_ge(S("kn_ps"), 8)
            link(dve.memset(keep, 1.0))
            link(dve.memset(keep.rearrange("p (c n) -> p c n", n=CH)[:, :, 0:1], 0.0))
            for t in range(8):
                last = dve.tensor_tensor_scan(t1[:, t, 0:NP_], keep, t0[:, t, 0:NP_], 0.0, ALU.mult, ALU.add)
            link(last)
            dve.tensor_tensor(t2[:, :, 0:NP_], t1[:, :, 0:NP_], t0[:, :, 0:NP_], ALU.subtract).then_inc(S("cw_e"), 1)

            def pr(x):
                return x[:, :, 0:NP_]

            dve.wait_ge(S("cw_exp"), 1)
            link(dve.scalar_tensor_tensor(out=pr(ra), in0=pr(ra), scalar=-1.0, in1=pr(t2), op0=ALU.mult, op1=ALU.mult))
            dve.engine_nop().then_inc(S("cw_e"), 1)
            dve.wait_ge(S("cw_exp"), 2)
            dve.tensor_tensor(pr(rr), pr(rr), pr(t2), ALU.mult)
            link(dve.tensor_copy(wc, pr(t2).rearrange("p t (c n) -> p t c n", n=CH)[:, :, :, CH - 1]))
            dve.engine_nop().then_inc(S("cw_e"), 1)
            dve.wait_ge(S("cw_exp"), 3)
            dve.tensor_tensor(pr(rb), pr(rb), pr(t2), ALU.mult)
            link(dve.tensor_tensor(pr(rk), pr(rk), pr(t2), ALU.mult))
            dve.memset(ar, 0.0)
            dve.memset(bp, 0.0)
            dve.memset(kp, 0.0)
            dve.memset(vp, 0.0)
            dve.memset(st, 0.0).then_inc(once("ck_zero")[0], 1)
            dve.wait_ge(*once("ck_zero"))

            def masks(m, count):
                return m.unsqueeze(1).to_broadcast([P, count, m.shape[1]])

            with dve.Fori(0, NCH) as c:
                for hf in range(2):
                    n = c * 2 + hf
                    js = slice(4 * hf, 4 * hf + 4)
                    dve.wait_ge(S("ck_y"), n)
                    for h in range(2):
                        r = slice(CH * h, CH * h + CH)
                        dve.tensor_copy(ar[r, :, r], ra[r, js, bass.ds(c * CH, CH)])
                        dve.tensor_copy(bp[r, :, r], rb[r, js, bass.ds(c * CH, CH)])
                    dve.tensor_copy(ar[:, :, P:192], rr[:, js, bass.ds(c * CH, CH)]).then_inc(S("ck_pad_d"), 1)
                    dve.wait_ge(S("ck_g"), n + 1)
                    g = [pb[i][:, 0:384].rearrange("p (j n) -> p j n", n=192) for i in range(4)]
                    for i in range(2):
                        dve.tensor_tensor(ltm[:, 2 * i:2 * i + 2, :], g[i][:, :, 0:P], masks(mstrict[:], 2), ALU.mult)
                        dve.tensor_tensor(mtm[:, 2 * i:2 * i + 2, :], g[2 + i][:, :, 0:P], masks(mstrict[:], 2), ALU.mult)
                        dve.tensor_tensor(rbm[:, 2 * i:2 * i + 2, :], g[i][:, :, P:192], masks(mincl[:], 2), ALU.mult)
                        last = dve.tensor_tensor(rkm[:, 2 * i:2 * i + 2, :], g[2 + i][:, :, P:192], masks(mincl[:], 2),
                                                 ALU.mult)
                    last.then_inc(S("ck_m"), 1)
                    dve.wait_ge(S("ck_m"), n + 1)
                    dve.tensor_tensor(lo, ltm, masks(lm[:, 0, :], 4), ALU.mult).then_inc(S("ck_l0"), 1)
                    dve.wait_ge(S("ck_l0"), n + 1)
                    dve.tensor_tensor(tt, lo, masks(ident[:], 4), ALU.add).then_inc(S("ck_tt0"), 1)
                    dve.wait_ge(S("ck_tt0"), n + 1)
                    for l in range(1, 6):
                        if l > 1:
                            dve.wait_ge(S("iv_p"), n * 5 + l - 1)
                        dve.tensor_tensor(lo, ltm, masks(lm[:, l, :], 4), ALU.mult).then_inc(S("iv_lo"), 1)
                        if l > 1:
                            inverse_step(dve, n, l - 1)
                    inverse_step(dve, n, 5)
                    dve.wait_ge(S("ck_y"), n + 1)
                    dve.tensor_tensor(st[:, js, :], st[:, js, :], pb[3][:].rearrange("p (j n) -> p j n", n=P), ALU.add)\
                        .then_inc(S("ck_sadd"), 1)
                    dve.wait_ge(S("ck_sadd"), n + 1)
                    dve.tensor_tensor(st[:, js, :], st[:, js, :],
                                      wc[:, js, bass.ds(c, 1)].to_broadcast([P, 4, P]), ALU.mult).then_inc(S("ck_s"), 1)
                ada(c + 4)
            dve.wait_ge(S("rs_in"), 16)
            dve.wait_ge(S("sv_in"), 96)
            vr, vw, vk, vv, vkk, vb = (svt[:, i, :] for i in range(6))

            def over_i(x):
                return x.unsqueeze(1).to_broadcast([P, RD, RD])

            def over_j(x):
                return x.unsqueeze(2).to_broadcast([P, RD, RD])

            link(dve.tensor_tensor(rt, rs, over_i(vkk), ALU.mult))
            link(dve.tensor_reduce(sa_row, rt, axis=AX.X, op=ALU.add))
            link(dve.tensor_tensor(rt, over_j(sa_row), over_i(vb), ALU.mult))
            link(dve.tensor_tensor(rs, rs, over_i(vw), ALU.mult))
            link(dve.tensor_tensor(rs, rs, rt, ALU.subtract))
            link(dve.tensor_tensor(rt, over_j(vv), over_i(vk), ALU.mult))
            dve.tensor_tensor(rs, rs, rt, ALU.add).then_inc(once("rs_new")[0], 1)
            dve.wait_ge(*once("rs_new"))
            link(dve.tensor_tensor(rt, rs, over_i(vr), ALU.mult))
            dve.tensor_reduce(y_row, rt, axis=AX.X, op=ALU.add).then_inc(once("ys_row")[0], 1)
            dve.wait_ge(*once("ys_ps"))
            dve.wait_ge(S("ck_yev"), 2 * NCH)
            for h in range(2):
                last = dve.tensor_copy(y8[RD * h:RD * h + RD, :, NP_:NT],
                                       pb[2][0:RD, 0:P].rearrange("p (b t h) -> p h t b", b=NS, h=2)[:, h])
            last.then_inc(once("y_all")[0], 1)
            dve.wait_ge(*once("y_all"))
            for t in range(8):
                dve.wait_ge(S("mu_ps"), t + 1)
                last = dve.scalar_tensor_tensor(out=y8[:, t, :], in0=pb[t % 4][:, 0:NT], scalar=-1.0 / RD, in1=y8[:, t, :],
                                                op0=ALU.mult, op1=ALU.add)
                last.then_inc(S("mu_evac"), 1)
            dve.wait_ge(S("mu_evac"), 8)
            dve.engine_nop().then_inc(once("gn_c")[0], 1)
            for t in range(8):
                dve.wait_ge(S("var_ps"), t + 1)
                last = dve.tensor_scalar(rr[:, t, :], pb[t % 4][:, 0:NT], 1.0 / RD, GN_EPS, ALU.mult, ALU.add)
                last.then_inc(S("var_evac"), 1)
            dve.wait_ge(S("var_evac"), 8)
            dve.engine_nop().then_inc(once("gn_ms")[0], 1)
            dve.wait_ge(*once("gn_root"))
            link(dve.reciprocal(rr, rr))
            link(dve.tensor_tensor(y8, y8, rr, ALU.mult))
            link(dve.tensor_tensor(y8, y8, vec(V_GW, 8, NT), ALU.mult))
            link(dve.tensor_tensor(y8, y8, vec(V_GBI, 8, NT), ALU.add))
            link(dve.tensor_tensor(y8, y8, bonus, ALU.add))
            for t in range(8):
                dve.wait_ge(S("g_ps"), t + 1)
                dve.tensor_tensor(y8[:, t, :], y8[:, t, :], pb[t % 4][:, 0:NT], ALU.mult).then_inc(S("o_rwkv"), 1)
            for t in range(KD):
                dve.wait_ge(S("out_ps"), t + 1)
                b = pb[t % 4]
                dve.scalar_tensor_tensor(out=xt[:, t, 0:NP_], in0=b[:, 0:NP_], scalar=mod[:, M_GT1, t, 0:1],
                                         in1=xt[:, t, 0:NP_], op0=ALU.mult, op1=ALU.add)
                dve.wait_ge(S("x1"), t)
                link(dve.tensor_tensor(tmp_s, b[:, NP_:NT], mod[:, M_GT1, t, 1:COND], ALU.mult))
                dve.tensor_tensor(xt[:, t, NP_:NT], xt[:, t, NP_:NT], tmp_s, ALU.add).then_inc(S("x1"), 1)
            rms_start(2)
            modulate(2, V_NFFN, M_SC2, M_SH2)
            dve.wait_ge(S("rt_consts"), 4)
            dve.wait_ge(S("g_ps"), 8)
            link(dve.memset(lg, 0.0))
            link(dve.memset(slots, -1.0))
            link(dve.memset(comb, 0.0))
            dve.wait_ge(*once("lgt_ps"))
            dve.tensor_copy(lg[:, 0:TC, :], pb[2][:, 0:TC * 36].rearrange("p (c n) -> p c n", n=36))
            link(dve.tensor_copy(lg[0:NS, TC, :], pb[2][0:NS, TC * 36:3 * 36]))
            dve.wait_ge(S("h_dve"), 2)
            link(dve.tensor_copy(h2s, ht[:, :, NP_:NT]))

            def first_max(x, n, top, one_hot):
                link(dve.tensor_reduce(top, x, axis=AX.X, op=ALU.max))
                c = pick[:, :, 0:n]
                link(dve.tensor_tensor(c, x, top.unsqueeze(2).to_broadcast([P, 3, n]), ALU.is_equal))
                link(dve.scalar_tensor_tensor(out=c, in0=c, scalar=-64.0, in1=eight[:, 0:n].unsqueeze(1).to_broadcast([P, 3, n]),
                                              op0=ALU.mult, op1=ALU.add))
                link(dve.tensor_reduce(least, c, axis=AX.X, op=ALU.min))
                link(dve.tensor_tensor(one_hot, c, least.unsqueeze(2).to_broadcast([P, 3, n]), ALU.is_equal))

            first_max(lg[:, :, 0:NG], NG, top_g, oh_g)
            dve.tensor_tensor(g_exp, lg[:, :, 0:NG], top_g.unsqueeze(2).to_broadcast([P, 3, NG]), ALU.subtract)\
                .then_inc(once("rt_d1")[0], 1)
            le4 = lg[:, :, NG:].rearrange("p c (g e) -> p c g e", e=NE)
            by_g = oh_g.unsqueeze(3).to_broadcast([P, 3, NG, NE])
            link(dve.tensor_tensor(wide, le4, by_g, ALU.mult))
            link(dve.tensor_reduce(le, wide.rearrange("p c g e -> p c e g"), axis=AX.X, op=ALU.add))
            first_max(le, NE, top_1, oh_1)
            link(dve.scalar_tensor_tensor(out=le, in0=oh_1, scalar=-1e30, in1=le, op0=ALU.mult, op1=ALU.add))
            first_max(le, NE, top_2, oh_2)
            dve.tensor_tensor(e2, top_2, top_1, ALU.subtract).then_inc(once("rt_d2")[0], 1)
            dve.wait_ge(*once("rt_e1"))
            link(dve.tensor_reduce(w_1, g_exp, axis=AX.X, op=ALU.add))
            dve.wait_ge(*once("rt_e2"))
            link(dve.scalar_tensor_tensor(out=w_1, in0=e2, scalar=1.0, in1=w_1, op0=ALU.add, op1=ALU.mult))
            link(dve.reciprocal(w_1, w_1))
            link(dve.tensor_tensor(w_2, w_1, e2, ALU.mult))
            dve.tensor_tensor(le, oh_1, w_1.unsqueeze(2).to_broadcast([P, 3, NE]), ALU.mult)
            link(dve.tensor_tensor(pick, oh_2, w_2.unsqueeze(2).to_broadcast([P, 3, NE]), ALU.mult))
            link(dve.tensor_tensor(le, le, pick, ALU.add))
            link(dve.tensor_tensor(oh_1, oh_1, oh_2, ALU.add))
            c4 = comb[:, :, 0:NEXP].rearrange("p c (g e) -> p c g e", e=NE)
            dve.tensor_tensor(c4, le.unsqueeze(2).to_broadcast([P, 3, NG, NE]), by_g, ALU.mult)
            dve.tensor_tensor(wide, oh_1.unsqueeze(2).to_broadcast([P, 3, NG, NE]), by_g, ALU.mult).then_inc(once("routed")[0], 1)
            dve.wait_ge(*once("routed"))
            dve.wait_ge(*once("rk_ps"))
            sl = slots[:, :, 0:NEXP]
            link(dve.tensor_reduce(most_f, pb[1][:, 2 * NEXP:3 * NEXP], axis=AX.X, op=ALU.max))
            dve.tensor_copy(most[:, 0:1], most_f).then_inc(once("cap_ready")[0], 1)
            link(dve.scalar_tensor_tensor(out=sl, in0=pb[1][:, 0:2 * NEXP].rearrange("p (c e) -> p c e", e=NEXP),
                                          scalar=float(NS + 1), in1=wide.rearrange("p c g e -> p c (g e)")[:, 0:TC],
                                          op0=ALU.add, op1=ALU.mult))
            link(dve.tensor_scalar(sl, sl, -1.0, None, ALU.add))
            dve.wait_ge(S("h2t_ps"), 8)
            dve.wait_ge(*once("lg_ps"))
            dve.wait_ge(S("h_act"), 2 * (KD - 8))
            link(dve.memset(ht, 0.0))

            def moe_dispatch(n, t):
                dve.wait_ge(S("m_ga"), n * 4)
                for q in range(2):
                    for c in range(TC):
                        last = dve.tensor_scalar(disp[:, c, q * SLOT:(q + 1) * SLOT], slot_no[:, 0, :],
                                                 slots[:, c, bass.ds(t * 2 + q, 1)], None, ALU.is_equal)
                last.then_inc(S("m_dp"), 1)

            def moe_gather_out(n):
                for b in range(2, 4):
                    dve.wait_ge(S("m_ga"), n * 4 + (b + 1))
                    last = dve.tensor_copy(xg[:, :, 4 * b:4 * b + 4, :],
                                           pb[b][:].rearrange("p (k q s) -> p q k s", q=2, s=SLOT))
                last.then_inc(S("m_ga_d"), 1)
                dve.wait_ge(S("m_ga_a"), (n + 1) * 2)
                dve.wait_ge(S("m_ga_d"), n + 1)
                dve.tensor_copy(xg[:, :, :, 0:NS], h2s.unsqueeze(1).to_broadcast([P, 2, KD, NS])).then_inc(S("m_xg"), 1)

            def moe_add(q, n):
                for i in range(KD):
                    k = (i % 2) * 8 + i // 2
                    dve.wait_ge(S(f"m_sc{q}"), n * KD + (i + 1))
                    dve.tensor_tensor(ht[:, k, :], ht[:, k, :], pb[i % 4][:, 0:NT], ALU.add)\
                        .then_inc(S(f"m_add{q}"), 1)

            def moe_dve(ps):
                if not isinstance(ps, int):
                    dve.tensor_scalar(sl, sl, -float(CAP), None, ALU.add)
                    dve.memset(own_w, 0.0).then_inc(S("m_next"), 1)
                    dve.wait_ge(S("m_next"), ps)
                dve.wait_ge(S("m_sc1"), ps * (17 * KD))
                dve.memset(pwt[:, 1, :], 0.0)
                dve.memset(y_slot[:, 1, :], 0.0).then_inc(S("m_zero"), 1)
                moe_dispatch(ps * 17, 0)
                moe_gather_out(ps * 17)
                with dve.Fori(0, NEXP // 2) as i:
                    t = ps * 16 + i
                    for q in range(2):
                        dve.wait_ge(S(f"m_wt{q}"), t)
                        for c in range(TC):
                            dve.tensor_scalar(pw[:, q, c, :], slot_no.rearrange("p a s -> p (a s)"),
                                              slots[:, c, bass.ds(i * 2 + q, 1)], comb[:, c, bass.ds(i * 2 + q, 1)],
                                              ALU.is_equal, ALU.mult)
                        dve.tensor_scalar(pw[0:NS, q, TC, :], own_slot.rearrange("p a s -> p (a s)"),
                                          comb[0:NS, TC, bass.ds(i * 2 + q, 1)], None, ALU.mult)\
                            .then_inc(S(f"m_pw{q}"), 1)
                    moe_dispatch(ps * 17 + i + 1, i + 1)
                    for q in range(2):
                        dve.wait_ge(S(f"m_sg{q}"), t + 1)
                        dve.wait_ge(S("m_free"), (t * 2 + q) * MOE_SLOTS + 4)
                        dve.tensor_tensor(sg[:, q, :], sg[:, q, :], pb[4 + q][:, 256:512], ALU.mult)\
                            .then_inc(S(f"m_hid{q}"), 1)
                        moe_add(1 - q, ps * (17 if q == 0 else 16) + i)
                        if q == 1:
                            moe_gather_out(ps * 17 + i + 1)
                moe_add(1, ps * 17 + 16)
                dve.wait_ge(S("m_add1"), ps * (17 * KD) + 17 * KD)

            moe_dve(0)
            dve.wait_ge(*once("cap_ready"))
            count = dve.value_load(most[0:1, 0:1], min_val=0, max_val=NP_)
            with dve.If(count > CAP):
                with dve.Fori(1, PASSES) as ps:
                    moe_dve(ps)
            for k in range(KD):
                dve.scalar_tensor_tensor(out=xt[:, k, 0:NP_], in0=ht[:, k, 0:NP_], scalar=mod[:, M_GT2, k, 0:1],
                                         in1=xt[:, k, 0:NP_], op0=ALU.mult, op1=ALU.add)
            link(dve.tensor_tensor(ht[:, :, NP_:NT], ht[:, :, NP_:NT], mod[:, M_GT2, :, 1:COND], ALU.mult))
            dve.tensor_tensor(xt[:, :, NP_:NT], xt[:, :, NP_:NT], ht[:, :, NP_:NT], ALU.add).then_inc(S("x2"), 1)
            rms_start(3)
            modulate(3, V_NFIN, M_SCF, M_SHF)
            for b in range(1, 12, 2):
                dve.wait_ge(S("yo_ps"), b + 1)
                dst = (y_tok[:, b // 4, (b % 4) * BANK:(b % 4 + 1) * BANK] if b < 8 else
                       ys_tok[:, (b - 8) * BANK:(b - 7) * BANK])
                dve.wait_ge(S("yo_evac"), b)
                dve.tensor_copy(dst, pb[1 + b % 4][0:dst.shape[0], :]).then_inc(S("yo_evac"), 1)

        @block.tensor
        def _(pe):
            pe.wait_ge(S("consts"), N_CONSTS)
            pe.wait_ge(*once("c_silu"))
            for k in range(KD):
                last = pe.transpose(pb[0][:, k * CPAD:(k + 1) * CPAD], c_row[:, k * P:(k + 1) * P], ident[0:CPAD, 0:CPAD])
            last.then_inc(once("cT_ps")[0], 1)
            pe.wait_ge(S("vec_in"), 16 * N_VEC)
            for g, (at, n) in enumerate(((V_ADA, 128), (V_NMIX, 80), (V_W0, 56))):
                last = pe.transpose(pb[1][:, at:at + n], vec_rows[0:n, g, :], ident[0:n, 0:n])
            last.then_inc(once("vec_ps")[0], 1)
            pe.wait_ge(S("x_in"), 32)
            for k in range(KD):
                if k >= 4:
                    pe.wait_ge(S("xT_evac"), k - 3)
                bank = pb[2 + k % 4]
                for c in range(TC):
                    pe.transpose(bank[:, c * P:(c + 1) * P], x_tok[:, c, k * P:(k + 1) * P], ident[:])
                pe.transpose(bank[:, NP_:NT], x_row[:, k * P:(k + 1) * P], ident[0:NS, 0:NS]).then_inc(S("xT_ps"), 1)

            def sum_squares(n):
                pe.wait_ge(S("norm_sq"), n)
                for k in range(KD):
                    last = pe.matmul(pb[0][:, 0:NT], ones[:], ht[:, k, :], start=(k == 0), stop=(k == KD - 1))
                last.then_inc(S("ms_ps"), 1)

            pe.wait_ge(*once("cT_ready"))
            sum_squares(1)

            def ada(sec):
                n = sec
                pe.wait_ge(S("ada_evac"), n)
                for i in range(8):
                    rnd, s = ada_round(sec) + i // 4, i % 4
                    pe.wait_ge(S(f"ring_full{s}"), (rnd + 1) * 16)
                    w = slot(s).rearrange("p (k c) -> p k c", c=D)
                    for j in range(2):
                        k = 2 * i + j
                        for g in range(4):
                            last = pe.matmul(pb[7][g * CPAD:(g + 1) * CPAD, :], ct[:, k, :],
                                             w[:, j, g * BANK:(g + 1) * BANK], start=(k == 0), stop=(k == KD - 1))
                    last.then_inc(S("ring_free"), 1)
                pe.wait_ge(S("ada_evac"), n + 1)
                pe.wait_ge(S("ada_mod"), n)
                for j in range(4):
                    last = pe.transpose(pb[6][:, j * P:(j + 1) * P], ada_row[:, j * P:(j + 1) * P], ident[:])
                last.then_inc(S("ada_tr"), 1)

            ada(M_SH1)
            ada(M_SC1)
            pe.wait_ge(S("h_dve"), 1)
            pe.wait_ge(S("h_act"), 1 * (KD - 8))
            with pe.Fori(0, 6) as g:
                for s in range(4):
                    pe.wait_ge(S(f"ring_full{s}"), (g + IN_ROUND + 1) * 16)
                    w = slot(s).rearrange("p (k c) -> p k c", c=256)
                    for m in range(2):
                        t = 2 * s + m
                        if t >= 4:
                            pe.wait_ge(S("in_evac_d" if t % 2 else "in_evac_a"), g * 4 + (t - 4) // 2 + 1)
                        else:
                            pe.wait_ge(S("in_evac_d" if t % 2 else "in_evac_a"), g * 4)
                        for k in range(KD):
                            last = pe.matmul(pb[t % 4][:, 0:NT], w[:, k, m * P:(m + 1) * P], ht[:, k, :],
                                             start=(k == 0), stop=(k == KD - 1))
                        last.then_inc(S("ring_free" if m else "in_ps"), 1)
            pe.wait_ge(S("small_w_in"), 64)
            pe.wait_ge(S("in_evac_a"), 24)
            pe.wait_ge(S("in_evac_d"), 24)
            for i, (at, n) in enumerate(((0, P), (P, P), (2 * P, GATE_RANK))):
                for k in range(KD):
                    last = pe.matmul(pb[i][0:n, 0:NT], small_w[:, k, at:at + n], ht[:, k, :],
                                     start=(k == 0), stop=(k == KD - 1))
                last.then_inc(S("in_small"), 1)
            for b in range(7):
                if b >= 2:
                    pe.wait_ge(S("so_evac"), b - 1)
                if b == 0:
                    pe.wait_ge(*once("in_small_a"))
                    pe.wait_ge(S("in_small_d"), 1)
                for j in range(4 if b < 6 else 2):
                    last = pe.transpose(pb[3 + b % 2][0:COND, j * P:(j + 1) * P], pj[:, TR + 4 * b + j, NP_ - 1:NT],
                                        ident[:])
                last.then_inc(S("so_ps"), 1)
            pe.wait_ge(S("shift_in"), 16 * len(SHIFT_PARTS))
            for t in range(26):
                last = pe.transpose(pb[5][:, t * NS:(t + 1) * NS], shift_row[:, t * P:(t + 1) * P], ident[0:NS, 0:NS])
            last.then_inc(once("shs_ps")[0], 1)
            pe.wait_ge(S("in_small_d"), 2)
            pe.wait_ge(S("so_evac"), 7)
            for c in range(TC):
                for t in range(8):
                    last = pe.transpose(pb[2 * c + t // 4][:, (t % 4) * P:(t % 4 + 1) * P],
                                        pj[:, TV + t, c * P:(c + 1) * P], ident[:])
                    if t % 4 == 3:
                        last.then_inc(S("vt_ps"), 1)
            pe.wait_ge(*once("shs_ready"))
            for t in range(8):
                last = pe.transpose(pb[4 + t // 4][0:NS, (t % 4) * P:(t % 4 + 1) * P], pj[:, TV + t, NP_:NT], ident[:])
            last.then_inc(once("vs_ps")[0], 1)
            pe.wait_ge(S("vt_evac"), 1)
            for t in range(4):
                last = pe.transpose(pb[0][0:NS, t * P:(t + 1) * P], pj[:, TK + t, NP_:NT], ident[:])
            last.then_inc(once("ks_ps")[0], 1)
            ada(2)
            pe.wait_ge(S("low_rank_in"), 48)
            pe.wait_ge(*once("ks_evac"))
            pe.wait_ge(S("vt_evac"), 4)
            for h in range(GLA_H):
                last = pe.matmul(pb[h][:, 0:NT], gw2[:, h * GLA_DK:(h + 1) * GLA_DK], pj[0:GATE_RANK, TGL, :],
                                 start=True, stop=True)
            last.then_inc(once("gz_ps")[0], 1)
            pe.wait_ge(*once("g_z"))
            for l in range(LEVELS + 1):
                if l < LEVELS:
                    pe.wait_ge(S("lv_qk"), l + 1)
                if l >= 2:
                    pe.wait_ge(S("lv_sel"), l - 1)
                q, k = (q4, k4) if l < LEVELS else (pj[:, TQ:TQ + 4, :], pj[:, TK:TK + 4, :])
                for i in range(1 if l == 0 else 2):
                    for h in range(GLA_H):
                        ks, qs = (0, 1) if l == 0 else (i, i)
                        last = pe.matmul(pb[2 * (l % 2) + i][:, h * P:(h + 1) * P], k[:, h, ks * P:(ks + 1) * P],
                                         q[:, h, qs * P:(qs + 1) * P], start=True, stop=True)
                last.then_inc(S("lv_ps"), 1)
            ada(3)
            pe.wait_ge(*once("kd"))
            pe.wait_ge(S("vs_evac"), 2)
            for c in range(TC):
                for h in range(GLA_H):
                    last = pe.transpose(pb[4 + c][:, h * P:(h + 1) * P], k4[:, h, c * P:(c + 1) * P], ident[:])
            last.then_inc(once("kd_ps")[0], 1)
            pe.wait_ge(S("lv_sel"), LEVELS + 1)
            for t in range(8):
                h, b = t // 2, pb[t // 2]
                o = (t % 2) * NP_
                v0, v1 = (v_tok[:, c, t * P:(t + 1) * P] for c in range(TC))
                pe.matmul(b[:, o:o + P], v0, at0[:, h, 0:P], start=True, stop=True)
                pe.matmul(b[:, o + P:o + NP_], v0, at0[:, h, P:NP_], start=True, stop=False)
                last = pe.matmul(b[:, o + P:o + NP_], v1, at1[:, h, :], start=False, stop=True)
                if t % 2:
                    last.then_inc(S("go_ps"), 1)
            pe.wait_ge(S("kd_evac"), 2)
            for h in range(GLA_H):
                for c in range(TC):
                    last = pe.matmul(pb[4 + h // 2][:, (h % 2) * GLA_DV:(h % 2 + 1) * GLA_DV],
                                     kd_tok[:, c, h * GLA_DK:(h + 1) * GLA_DK], v_tok[:, c, h * GLA_DV:(h + 1) * GLA_DV],
                                     start=(c == 0), stop=(c == TC - 1))
            last.then_inc(once("gst_ps")[0], 1)
            pe.wait_ge(*once("gst_evac"))
            for h in range(GLA_H):
                pe.wait_ge(S("kz"), h + 1)
                if h == 0:
                    pe.wait_ge(S("go_evac"), 4)
                else:
                    pe.wait_ge(S("gs_s"), h)
                for b in range(NS):
                    last = pe.matmul(pb[b // 2][:, (b % 2) * GLA_DV:(b % 2 + 1) * GLA_DV], kz[:, b, :],
                                     v_row[:, h * GLA_DV:(h + 1) * GLA_DV], start=True, stop=True)
                    if b % 2:
                        last.then_inc(S("gs_kv"), 1)
                pe.wait_ge(S("gs_s"), h + 1)
                for e in range(2):
                    for b in range(NS):
                        at = (2 * h + e) * NS + b
                        last = pe.matmul(pb[4][:, at:at + 1], gs[h % 2][:, b, e * P:(e + 1) * P],
                                         pj[:, TQ + h, NP_ + b:NP_ + b + 1], start=True, stop=True)
                last.then_inc(S("gs_o"), 1)
            pe.wait_ge(*once("gla_sq"))
            for h in range(GLA_H):
                for e in range(2):
                    last = pe.matmul(pb[h][:, 0:NT], ones[:], gla_sq[:, 2 * h + e, :], start=(e == 0), stop=(e == 1))
            last.then_inc(once("gn_ps")[0], 1)
            pe.wait_ge(*once("gates_act"))
            pe.wait_ge(*once("gla_ms"))
            for i in range(16):
                r = slice(RD * (i // 8), RD * (i // 8) + RD)
                if i >= 4:
                    pe.wait_ge(S("rs_evac"), i - 3)
                pe.matmul(pb[i % 4][:, 0:NT], wa2[r, (i % 8) * P:(i % 8 + 1) * P], pj[r, TWA, :], start=True, stop=True)\
                    .then_inc(S("rs_ps"), 1)

            def head_sums(src, ps_sem, free_sem, base=0, banks=(0, 1, 2, 3)):
                n = len(banks)
                for t in range(8):
                    if t >= n:
                        pe.wait_ge(S(free_sem), base + t - n + 1)
                    pe.matmul(pb[banks[t % n]][:, 0:NT], bones[:], src[:, t, :], start=True, stop=True)\
                        .then_inc(S(ps_sem), 1)

            pe.wait_ge(*once("kk_sq"))
            pe.wait_ge(S("rs_evac"), 16)
            head_sums(t2, "kn_ps", "kn_evac")
            pe.wait_ge(*once("bonus_in"))
            pe.wait_ge(S("kn_evac"), 8)
            head_sums(t1, "bonus_ps", "bonus_evac", banks=(2, 3))
            pe.wait_ge(*once("sv_rest"))
            pe.wait_ge(*once("sv_w"))
            for t in range(8):
                last = pe.transpose(pb[t // 4][0:48, (t % 4) * P:(t % 4 + 1) * P],
                                    sv[:, t].rearrange("p v b -> p (v b)"), ident[:])
                if t % 4 == 3:
                    last.then_inc(S("sv_ps"), 1)
            pe.wait_ge(S("sv_evac"), 2)
            pe.wait_ge(S("bonus_evac"), 8)
            with pe.Fori(0, NCH) as c:
                for hf in range(2):
                    n = c * 2 + hf
                    pe.wait_ge(S("ck_pad_d"), n + 1)
                    pe.wait_ge(S("ck_pad_a"), n + 1)
                    pe.wait_ge(S("ck_s"), n)
                    pe.wait_ge(S("ck_yev"), n)
                    for i, x in enumerate((bp, kp)):
                        for j in range(4):
                            last = pe.matmul(pb[2 * i + j // 2][:, (j % 2) * 192:(j % 2 + 1) * 192], x[:, j, :], ar[:, j, :],
                                             start=True, stop=True)
                    last.then_inc(S("ck_g"), 1)
                    for i, x in enumerate((bp, kp)):
                        for j in range(4):
                            last = pe.transpose(pb[4 + i][:, j * P:(j + 1) * P], x[:, j, :], ident[:])
                    last.then_inc(S("ck_t1"), 1)
                    pe.wait_ge(S("ck_m"), n + 1)
                    for j in range(4):
                        last = pe.transpose(pb[0][:, j * P:(j + 1) * P], vp[:, j, :], ident[:])
                    last.then_inc(S("ck_t2"), 1)
                    pe.wait_ge(S("ck_tt0"), n + 1)
                    for j in range(4):
                        last = pe.transpose(pb[1][:, j * P:(j + 1) * P], tt[:, j, :], ident[:])
                    last.then_inc(S("ck_t0"), 1)
                    pe.wait_ge(S("ck_t1e"), n + 1)
                    pe.wait_ge(S("ck_t2e"), n + 1)
                    for j in range(4):
                        o = pb[5][:, j * P:(j + 1) * P]
                        pe.matmul(o, ar[:, j, 0:P], st[:, 4 * hf + j, :], start=True, stop=False)
                        last = pe.matmul(o, mtm[:, j, :], vp[:, j, :], start=False, stop=True)
                    last.then_inc(S("ck_u"), 1)
                    pe.wait_ge(S("ck_t0e"), n + 1)
                    for l in range(1, 6):
                        pe.wait_ge(S("iv_lo"), n * 5 + l)
                        pe.wait_ge(S("iv_tn"), n * 5 + l - 1)
                        for j in range(4):
                            last = pe.matmul(pb[2][:, j * P:(j + 1) * P], lo[:, j, :], tm[:, j, :], start=True, stop=True)
                        last.then_inc(S("iv_p"), 1)
                        pe.wait_ge(S("iv_pe"), n * 5 + l)
                        for j in range(4):
                            last = pe.matmul(pb[3][:, j * P:(j + 1) * P], pm[:, j, :], tt[:, j, :], start=True, stop=True)
                        if l < 5:
                            for j in range(4):
                                last = pe.matmul(pb[4][:, j * P:(j + 1) * P], tt[:, j, :], pm[:, j, :], start=True,
                                                 stop=True)
                        last.then_inc(S("iv_t"), 1)
                    pe.wait_ge(S("iv_tn"), n * 5 + 5)
                    pe.wait_ge(S("ck_ue"), n + 1)
                    for j in range(4):
                        last = pe.matmul(pb[1][:, j * P:(j + 1) * P], tt[:, j, :], um[:, j, :], start=True, stop=True)
                    last.then_inc(S("ck_sa"), 1)
                    pe.wait_ge(S("ck_sae"), n + 1)
                    for j in range(4):
                        o = pb[2][:, j * CH:(j + 1) * CH]
                        pe.matmul(o, st[:, 4 * hf + j, :], ar[:, j, P:192], start=True, stop=False)
                        pe.matmul(o, tm[:, j, :], rbm[:, j, :], start=False, stop=False)
                        pe.matmul(o, vp[:, j, :], rkm[:, j, :], start=False, stop=True)
                        o = pb[3][:, j * P:(j + 1) * P]
                        pe.matmul(o, bp[:, j, :], tm[:, j, :], start=True, stop=False)
                        last = pe.matmul(o, kp[:, j, :], vp[:, j, :], start=False, stop=True)
                    last.then_inc(S("ck_y"), 1)
                ada(c + 4)
            pe.wait_ge(S("ck_s"), 2 * NCH)
            pe.wait_ge(S("ck_yev"), 2 * NCH)
            for t in range(8):
                last = pe.transpose(pb[t // 4][:, (t % 4) * P:(t % 4 + 1) * P], st[:, t, :], ident[:])
            last.then_inc(once("sr_ps")[0], 1)
            pe.wait_ge(*once("ys_row"))
            pe.transpose(pb[2][0:RD, 0:P], y_row, ident[:]).then_inc(once("ys_ps")[0], 1)
            pe.wait_ge(S("sr_evac"), 2)
            pe.wait_ge(*once("y_all"))
            head_sums(y8, "mu_ps", "mu_evac")
            pe.wait_ge(*once("gn_sq"))
            head_sums(ra, "var_ps", "var_evac")
            pe.wait_ge(S("g2_in"), 16)
            for t in range(8):
                pe.wait_ge(S("var_evac"), min(8, t + 5))
                if t >= 4:
                    pe.wait_ge(S("o_rwkv"), t - 3)
                pe.matmul(pb[t % 4][:, 0:NT], g2[:, t * P:(t + 1) * P], pj[:, TG7, :], start=True, stop=True)\
                    .then_inc(S("g_ps"), 1)
            pe.wait_ge(S("o_rwkv"), 8)
            for t in range(KD):
                i = t // 2
                rnd, s = OUT_ROUND + i // 4, i % 4
                pe.wait_ge(S(f"ring_full{s}"), 16 * (rnd + 1))
                if t >= 4:
                    pe.wait_ge(S("x1"), t - 3)
                w = slot(s).rearrange("p (k c) -> p k c", c=256)
                for k in range(KD):
                    last = pe.matmul(pb[t % 4][:, 0:NT], w[:, k, (t % 2) * P:(t % 2 + 1) * P], ht[:, k, :],
                                     start=(k == 0), stop=(k == KD - 1))
                last.then_inc(S("out_ps"), 1)
            pe.wait_ge(S("x1"), KD)
            sum_squares(2)
            pe.wait_ge(S("rt_in"), 32)
            pe.wait_ge(S("h_dve"), 2)
            pe.wait_ge(S("h_act"), 2 * (KD - 8))
            for k in range(KD):
                last = pe.matmul(pb[1][0:NG + NEXP, 0:NT], w_rt[:, k, :], ht[:, k, :], start=(k == 0), stop=(k == KD - 1))
            last.then_inc(once("lg_ps")[0], 1)
            for b in range(8):
                if b >= 4:
                    pe.wait_ge(S("h2t_evac"), b - 3)
                if b == 1:
                    pe.wait_ge(*once("lg_evac"))
                    for c in range(3):
                        m = P if c < TC else NS
                        last = pe.transpose(pb[2][0:m, c * 36:(c + 1) * 36], lg_t[:, c * P:c * P + m], ident[0:36, 0:36])
                    last.then_inc(once("lgt_ps")[0], 1)
                for j in range(4):
                    k = 4 * (b % 4) + j
                    last = pe.transpose(pb[3 + b % 4][:, j * P:(j + 1) * P], ht[:, k, (b // 4) * P:(b // 4 + 1) * P],
                                        ident[:])
                last.then_inc(S("h2t_ps"), 1)
            pe.wait_ge(*once("routed"))
            m = [wide[:, c].rearrange("p g e -> p (g e)") for c in range(TC)]
            pe.matmul(pb[1][:, 0:NEXP], mstrict[:], m[0], start=True, stop=True)
            pe.matmul(pb[1][:, NEXP:2 * NEXP], ones[:], m[0], start=True, stop=False)
            pe.matmul(pb[1][:, NEXP:2 * NEXP], mstrict[:], m[1], start=False, stop=True)
            pe.matmul(pb[1][:, 2 * NEXP:3 * NEXP], ones[:], m[0], start=True, stop=False)
            pe.matmul(pb[1][:, 2 * NEXP:3 * NEXP], ones[:], m[1], start=False, stop=True).then_inc(once("rk_ps")[0], 1)
            pe.wait_ge(S("h2t_evac"), 8)
            pe.wait_ge(*once("cap_ready"))

            def moe_gather(n):
                pe.wait_ge(S("m_dp"), n + 1)
                for b in range(4):
                    for j in range(4):
                        k = 4 * b + j
                        for c in range(TC):
                            last = pe.matmul(pb[b][:, j * P:(j + 1) * P], h_tok[:, c, k * P:(k + 1) * P], disp[:, c, :],
                                             start=(c == 0), stop=(c == TC - 1))
                    last.then_inc(S("m_ga"), 1)

            def moe_scatter(q, n):
                for i in range(KD):
                    k = (i % 2) * 8 + i // 2
                    r = slice(SLOT * (i % 2), SLOT * (i % 2) + SLOT)
                    if i >= 4:
                        pe.wait_ge(S(f"m_add{q}"), n * KD + (i - 3))
                    pe.matmul(pb[i % 4][:, 0:NT], y_slot[r, q, (k % 8) * P:(k % 8 + 1) * P], pwt[r, q, :],
                              start=True, stop=True).then_inc(S(f"m_sc{q}"), 1)

            def moe_pe(ps):
                pe.wait_ge(S("m_zero"), ps + 1)
                pe.wait_ge(S("m_add1"), ps * (17 * KD))
                moe_gather(ps * 17)
                with pe.Fori(0, NEXP // 2) as i:
                    t = ps * 16 + i
                    for q in range(2):
                        pe.wait_ge(S(f"m_pw{q}"), t + 1)
                        bank = pb[5 - q]
                        pe.wait_ge(S(f"m_ht{1 - q}"), t + q)
                        for c in range(3):
                            m = P if c < TC else NS
                            last = pe.transpose(bank[:, c * P:c * P + m], pw[0:m, q, c, :], ident[0:m, 0:m])
                        last.then_inc(S(f"m_wt{q}"), 1)
                        if q == 0:
                            pe.wait_ge(S("m_wte1"), t)
                            pe.wait_ge(S("m_xg"), ps * 17 + i + 1)
                        else:
                            pe.wait_ge(S("m_wte0"), t + 1)
                        for s in range(4):
                            pe.wait_ge(S(f"m_full{s}"), (t * 2 + q + 1) * 16)
                            w = slot(s).rearrange("p (k f) -> p k f", f=FF)
                            o = (s // 2) * 256
                            for j in range(8):
                                k = (s % 2) * 8 + j
                                for h in range(2):
                                    last = pe.matmul(pb[4 + q][SLOT * h:SLOT * h + SLOT, o:o + 256], xg[:, q, k, :],
                                                     w[:, j, h * 256:(h + 1) * 256], start=(k == 0), stop=(k == KD - 1))
                            last.then_inc(S("m_free"), 1)
                        if q == 0:
                            pe.wait_ge(S("m_ye1"), t)
                            moe_scatter(1, ps * 17 + i)
                        else:
                            pe.wait_ge(S("m_ye0"), t + 1)
                            pe.wait_ge(S("m_add1"), ps * (17 * KD) + (i + 1) * KD)
                            moe_scatter(0, t)
                            pe.wait_ge(S("m_add0"), (t + 1) * KD)
                            moe_gather(ps * 17 + i + 1)
                        pe.wait_ge(S(f"m_hid{q}"), t + 1)
                        for j in range(2):
                            last = pe.transpose(pb[4 + q][:, j * P:(j + 1) * P], sg[:, q, j * P:(j + 1) * P], ident[:])
                        last.then_inc(S(f"m_hp{q}"), 1)
                        pe.wait_ge(S(f"m_ht{q}"), t + 1)
                        pe.wait_ge(S(f"m_ye{1 - q}"), t + q)
                        for s in range(4, MOE_SLOTS):
                            pe.wait_ge(S(f"m_full{s}"), (t * 2 + q + 1) * 16)
                            w = slot(s).rearrange("p (k f) -> p k f", f=D)
                            for j in range(2):
                                fc = (s - 4) * 2 + j
                                x = hid_t[:, q, (fc % 2) * P + (fc // 2) * SLOT:(fc % 2) * P + (fc // 2 + 1) * SLOT]
                                for n in range(2):
                                    for h in range(2):
                                        at = h * 1024 + n * BANK
                                        last = pe.matmul(pb[6 + n][SLOT * h:SLOT * h + SLOT, :], x, w[:, j, at:at + BANK],
                                                         start=(fc == 0), stop=(fc == 3))
                            last.then_inc(S("m_free"), 1)
                pe.wait_ge(S("m_ye1"), ps * 16 + 16)
                pe.wait_ge(S("m_xg"), ps * 17 + 17)
                moe_scatter(1, ps * 17 + 16)

            moe_pe(0)
            count = pe.value_load(most[0:1, 0:1], min_val=0, max_val=NP_)
            with pe.If(count > CAP):
                with pe.Fori(1, PASSES) as ps:
                    moe_pe(ps)
            pe.wait_ge(S("x2"), 1)
            sum_squares(3)
            pe.wait_ge(S("h_dve"), 3)
            pe.wait_ge(S("h_act"), 3 * (KD - 8))
            for b in range(12):
                if b >= 4:
                    pe.wait_ge(S("yo_evac"), b - 3)
                m = P if b < 8 else NS
                at = (b // 4) * P
                for j in range(4):
                    k = 4 * (b % 4) + j
                    last = pe.transpose(pb[1 + b % 4][0:m, j * P:(j + 1) * P], ht[:, k, at:at + m], ident[:])
                last.then_inc(S("yo_ps"), 1)


N_VEC = 2 + 11 + 7
N_CONSTS = 9

_OUTS = [("y_prompt", (1, NP_, D)), ("y_sample", (NS, 1, D)), ("sg_prompt", (1, 1, GLA_H, GLA_DK, GLA_DV)),
         ("sr_prompt", (1, 1, RH, RD, RD)), ("ss_prompt", (1, 1, RCOLS)), ("sg_sample", (1, NS, GLA_H, GLA_DK, GLA_DV)),
         ("sr_sample", (1, NS, RH, RD, RD)), ("ss_sample", (1, NS, RCOLS))]


def kernel(**inputs):
    import concourse.bacc as bacc
    from concourse.bass_utils import run_bass_kernel_spmd

    nc = bacc.Bacc("TRN2", target_bir_lowering=False, num_devices=1)
    arrays, args = {}, {}
    for name, value in inputs.items():
        a = np.ascontiguousarray(value)
        arrays[f"in_{name}"] = a
        args[name] = nc.dram_tensor(f"in_{name}", a.shape, mybir.dt.from_np(a.dtype), kind="ExternalInput").ap()
    for name, shape in _OUTS:
        args[name] = nc.dram_tensor(f"out_{name}", shape, F32, kind="ExternalOutput").ap()
    args["scratch"] = nc.dram_tensor("vector_scratch", (48, 1024), F32, kind="Internal").ap()
    hymba_layer(nc, **args)
    r = run_bass_kernel_spmd(nc, [arrays], core_ids=[0])
    return tuple(r.results[0][f"out_{name}"] for name, _ in _OUTS)
```

```python
from contextlib import ExitStack

import numpy as np

import concourse.bass as bass
from concourse import mybir

F32 = mybir.dt.float32
I32 = mybir.dt.int32
ALU = mybir.AluOpType
ACT = mybir.ActivationFunctionType
AX = mybir.AxisListType

P = 128
D = 2048
KD = D // P
NP_ = 256
NS = 8
NT = NP_ + NS
TC = NP_ // P
COND = 1 + NS
CPAD = 32
BANK = 512
GLA_H, GLA_DK, GLA_DV = 4, 128, 256
GATE_RANK = 16
RH, RD = 16, 64
NPAIR = RH // 2
CH = 64
NCH = NP_ // CH
RCOLS = 3328
GCOLS = 3088
NG, NE, FF = 4, 8, 512
NEXP = NG * NE
SLOT = 64
CAP = SLOT - NS
PASSES = -(-NP_ // CAP)
RING = 4096
MIX_SLOTS, MOE_SLOTS = 4, 6
EPS, GLA_EPS, GN_EPS = 1e-6, 1e-5, 64e-5
HALF_E = float(np.exp(-0.5))
TQ, TK, TV, TOG, TR, TK7, TV7, TWA, TG7, TGL, NTILE = 0, 4, 8, 16, 24, 32, 40, 48, 49, 50, 51
SHIFT_PARTS = [(0, 0, 0, 1024), (8, 0, 1088, 1024), (16, 0, 2112, 1024), (24, 0, 1024, 64), (24, 64, 3136, 64),
               (25, 0, 3200, 128)]
V_ADA, V_NMIX, V_NFFN, V_NFIN, V_MU, V_GB, V_GN = 0, 128, 144, 160, 176, 202, 206
V_W0, V_A0, V_KK, V_KA, V_RK, V_GW, V_GBI, V_END = 208, 216, 224, 232, 240, 248, 256, 264
M_SH1, M_SC1, M_GT1, M_SH2, M_SC2, M_GT2, M_SHF, M_SCF = range(8)


def hymba_layer(nc, x_prompt, x_sample, state_gla, state_rwkv, state_shift, c_prompt, c_sample,
                w_ada, b_ada, norm_mix, norm_ffn, w_in, gla_gate_w2, gla_gate_b, gla_norm,
                rwkv_mu, rwkv_w0, rwkv_w2, rwkv_a0, rwkv_a2, rwkv_g2, rwkv_k_k, rwkv_k_a, rwkv_r_k,
                rwkv_gn_w, rwkv_gn_b, w_out, w_router_group, w_router_expert,
                w_exp_gate, w_exp_up, w_exp_down, norm_final, w_ada_final, b_ada_final,
                y_prompt, y_sample, sg_prompt, sr_prompt, ss_prompt, sg_sample, sr_sample, ss_sample, scratch):
    ctx = ExitStack()
    with ctx:
        sems = {}

        def S(name):
            if name not in sems:
                sems[name] = ctx.enter_context(nc.semaphore(name))
            return sems[name]

        ONCE = {
            "pe_step": (
                "cT_ps vec_ps shs_ps vs_ps ks_ps gz_ps kd_ps gst_ps gs_o os_ps gn_ps sv_ps "
                "sr_ps ys_ps lg_ps lgt_ps rk_ps "),
            "act_step": (
                "c_silu in_small_a vs_evac ks_evac g_ln eg kd_e kd_evac gst_evac_a gst_evac gates_act or_evac "
                "gos_evac gla_sq gla_root kk_sq sv_w sv_evac sr_evac gn_sq gn_root lg_evac rt_e1 "
                "rt_e2 "),
            "dve_step": (
                "c_zeroed cT_ready vecs_ready shs_ready g_z g_log kd gla_ms "
                "gla_done lw kk_raw bonus_in sv_rest ck_zero y_all "
                "gn_c gn_ms rt_d1 rt_d2 routed cap_ready "),
        }

        def once(name):
            for sem, steps in ONCE.items():
                if name in steps.split():
                    return S(sem), steps.split().index(name) + 1
            raise KeyError(name)

        def sb(name, cols, rows=P, dt=F32):
            return ctx.enter_context(nc.sbuf_tensor(name, [rows, cols], dt))

        ring = sb("ring", MOE_SLOTS * RING)
        ta = ring[:, MIX_SLOTS * RING:MOE_SLOTS * RING]
        tb = ring[:, 2 * RING:MIX_SLOTS * RING]
        xt = sb("xt", KD * NT)[:].rearrange("p (k n) -> p k n", n=NT)
        ht_flat = sb("ht", KD * NT)
        ht = ht_flat[:].rearrange("p (k n) -> p k n", n=NT)
        pj_flat = sb("pj", NTILE * NT)
        pj = pj_flat[:].rearrange("p (k n) -> p k n", n=NT)
        mod = sb("mod", 8 * KD * COND)[:].rearrange("p (s k n) -> p s k n", s=8, n=COND)
        vecs = sb("vecs", V_END)
        ident = sb("ident", P)
        ones = sb("ones", P)
        bones = sb("bones", P)
        ct = sb("ct", KD * CPAD)[:].rearrange("p (k n) -> p k n", n=CPAD)
        lm = sb("lm", 8 * P)[:].rearrange("p (l n) -> p l n", n=P)
        mstrict = sb("mstrict", P)
        mincl = sb("mincl", CH)
        wa2 = ht_flat[:, 2112:3136]
        g2 = sb("g2", 1024)
        gw2, kz = g2[0:GATE_RANK, 0:512], g2[0:NS, :].rearrange("p (b d) -> p b d", d=GLA_DK)
        misc = sb("misc", 1040)
        ada_row = sb("ada_row", BANK)
        rstd = sb("rstd", NT)[:]
        tmp_s = sb("tmp_s", NS)[:]
        gscale = sb("gscale", KD * COND)[:].rearrange("p (k n) -> p k n", n=COND)
        shs = misc[:, 0:26 * NS].rearrange("p (t n) -> p t n", n=NS)
        pb = [ctx.enter_context(nc.psum_tensor(f"pb{i}", [P, BANK], F32)) for i in range(8)]

        x_tok = ta[:, 0:TC * D].rearrange("p (c d) -> p c d", d=D)
        x_row = ta[0:NS, TC * D:TC * D + D]
        c_row = ta[0:CPAD, TC * D + D:TC * D + 2 * D]
        small_w = ta[:, 0:KD * 272].rearrange("p (k c) -> p k c", c=272)
        shift_row = ta[0:NS, KD * 272:KD * 272 + RCOLS]
        vec_rows = pj_flat[:, 0:3 * P].rearrange("p (g c) -> p g c", c=P)
        idx_f = pj_flat[:, 512:640].bitcast(I32)
        idx_p = pj_flat[:, 640:768].bitcast(I32)
        idx_x = pj_flat[:, 768:896].bitcast(I32)
        xor_f = pj_flat[:, 896:1024]
        tri_f = pj_flat[:, 1024:1152]
        ge_f = pj_flat[:, 1152:1280]

        dl = tb[:, 0:26 * NT].rearrange("p (t n) -> p t n", n=NT)
        shift_out = ht_flat[0:COND, 0:RCOLS]
        cum = ta[:, 0:1024]
        cum4 = cum.rearrange("p (h n) -> p h n", n=NP_)
        e_flat = ta[:, 1024:2048]
        z4 = ta[:, 1024:2080].rearrange("p (h n) -> p h n", n=NT)
        l4 = ta[:, 2080:3136].rearrange("p (h n) -> p h n", n=NT)
        q4 = ta[:, 2080:3104].rearrange("p (h n) -> p h n", n=NP_)
        k4 = ta[:, 3104:4128].rearrange("p (h n) -> p h n", n=NP_)
        kd_tok = ta[:, 2080:3104].rearrange("p (c d) -> p c d", d=GLA_H * GLA_DK)
        v_tok = ta[:, 4128:6176].rearrange("p (c d) -> p c d", d=GLA_H * GLA_DV)
        at0 = ta[:, 6176:7200].rearrange("p (h n) -> p h n", n=NP_)
        at1 = ta[:, 7200:7712].rearrange("p (h n) -> p h n", n=P)
        sg_new = ta[:, 0:1024].rearrange("p (h e) -> p h e", e=GLA_DV)
        k_row, v_row = ht_flat[0:NS, 3648:4160], misc[0:NS, 0:1024]
        eg = rstd[:, 0:GLA_H * NS]
        gs = [tb[:, i * 2048:(i + 1) * 2048].rearrange("p (b e) -> p b e", e=GLA_DV) for i in range(GLA_H)]
        o_rows = ta[:, 2080:4128].rearrange("p (a f) -> p a f", a=2)
        gla_sq = ta[:, 5152:7264].rearrange("p (t n) -> p t n", n=NT)
        gla_r = pj[:, TQ:TQ + GLA_H, :]
        o_gla = ht[:, 0:8, :]
        W8 = NPAIR * NT

        def tiles8(flat):
            return flat.rearrange("p (t n) -> p t n", n=NT)

        ra, rb, bonus = (tiles8(pj_flat[:, i * W8:(i + 1) * W8]) for i in range(3))
        t0, t1, t2 = (tiles8(ta[:, i * W8:(i + 1) * W8]) for i in range(3))
        rr, rk, rv = pj[:, TR:TR + 8, :], pj[:, TK7:TK7 + 8, :], pj[:, TV7:TV7 + 8, :]
        sv = misc[:, 0:384].rearrange("p (t v b) -> p t v b", v=6, b=NS)
        svt = misc[:, 384:768].rearrange("p (v d) -> p v d", d=RD)
        sv_row = ht_flat[0:48, 2112:3136]
        wc = misc[:, 768:800].rearrange("p (t c) -> p t c", c=NCH)
        y8 = ht[:, 8:16, :]
        ar = [x[:, 0:768].rearrange("p (j n) -> p j n", n=192) for x in (ta, tb)]
        bufs = [[x[:, 768 + i * 512:768 + (i + 1) * 512].rearrange("p (j n) -> p j n", n=P) for x in (ta, tb)]
                for i in range(10)]
        bp, kp, vp, ltm, mtm, lo, tm, tt, pm, um = bufs
        rbm = [x[:, 5888:6144].rearrange("p (j n) -> p j n", n=CH) for x in (ta, tb)]
        rkm = [x[:, 6144:6400].rearrange("p (j n) -> p j n", n=CH) for x in (ta, tb)]
        st = ta[:, 6400:7424].rearrange("p (t n) -> p t n", n=P)
        sr_new = pj_flat[:, W8:W8 + 1024].rearrange("p (t n) -> p t n", n=P)
        SI = 8
        rs = [tb[:, 6400 + i * 512:6912 + i * 512].rearrange("p (i j) -> p i j", j=RD) for i in range(2)]
        rt = tb[:, 7424:7936].rearrange("p (i j) -> p i j", j=RD)
        sa_row, y_row = misc[:, 800:808], misc[:, 864:928]

        at = [0]

        def room(cols):
            at[0] += cols
            return pj_flat[:, at[0] - cols:at[0]]

        w_rt = room(KD * 36).rearrange("p (k c) -> p k c", c=NG + NEXP)
        lg_t = room(NT)[0:NG + NEXP]
        lg = room(3 * 36).rearrange("p (c n) -> p c n", n=36)
        comb = room(3 * 34).rearrange("p (c e) -> p c e", e=NEXP + 2)
        slots = room(TC * 34).rearrange("p (c e) -> p c e", e=NEXP + 2)
        wide = room(3 * NEXP).rearrange("p (c g e) -> p c g e", g=NG, e=NE)
        pick, le, oh_1, oh_2 = (room(3 * NE).rearrange("p (c e) -> p c e", e=NE) for _ in range(4))
        g_exp, oh_g = (room(3 * NG).rearrange("p (c g) -> p c g", g=NG) for _ in range(2))
        top_g, top_1, top_2, least, e2, w_1, w_2 = (room(3) for _ in range(7))
        most_f, most = room(1), room(1).bitcast(I32)
        h_tok = room(TC * D).rearrange("p (c d) -> p c d", d=D)
        xg = room(2 * KD * SLOT).rearrange("p (q k s) -> p q k s", q=2, s=SLOT)
        y_slot = room(2 * 1024).rearrange("p (q d) -> p q d", q=2)
        sg = room(512).rearrange("p (q f) -> p q f", q=2)
        hid_t = room(512).rearrange("p (q f) -> p q f", q=2)
        pw = room(2 * 3 * P).rearrange("p (q c s) -> p q c s", q=2, c=3)
        disp = room(TC * P).rearrange("p (c s) -> p c s", c=TC)
        pwt = room(2 * NT).rearrange("p (q n) -> p q n", q=2)
        assert at[0] <= NTILE * NT
        h2s = misc[:, 0:KD * NS].rearrange("p (k n) -> p k n", n=NS)
        slot_no = misc[:, 128:256].rearrange("p (a s) -> p a s", a=2)
        own_slot = misc[0:NS, 256:384].rearrange("p (a s) -> p a s", a=2)
        own_w = comb[:, TC, :]
        eight = misc[:, 384:392]
        y_tok, ys_tok = h_tok, xg.rearrange("p q k s -> p (q k s)")[0:NS]

        def slot(s):
            return ring[:, s * RING:(s + 1) * RING]

        def ada_src(sec):
            return (w_ada[0, :, sec * D:(sec + 1) * D] if sec < 6 else
                    w_ada_final[:, (sec - 6) * D:(sec - 5) * D]).rearrange("(k p) c -> p k c", p=P)

        IN_ROUND = 4

        block = ctx.enter_context(nc.Block())

        class Chain:

            def __init__(self, eng, name):
                self.eng, self.sem, self.n = eng, S(name), 0

            def __call__(self, ins):
                self.n += 1
                ins.then_inc(self.sem, 1)
                self.eng.wait_ge(self.sem, self.n)

        def levels(flat, size):
            v = flat.rearrange("p (b n) -> p b n", n=size)
            return v, v[:, :, size // 2 - 1:size // 2].to_broadcast([P, GLA_H * NP_ // size, size])

        G_BANKS = ((0, 1, 2, 6), (3, 4, 5, 6))
        LEVELS = 8

        @block.sync
        def _(sp):
            def ada_load(sec):
                src = ada_src(sec)
                for i in range(8):
                    rnd, s = 2 * sec + i // 4, i % 4
                    if rnd > 0:
                        sp.wait_ge(S("ring_free"), MIX_SLOTS * (rnd - 1) + s + 1)
                    sp.dma_start(slot(s).rearrange("p (k c) -> p k c", c=D), src[:, 2 * i:2 * i + 2, :])\
                        .then_inc(S(f"ring_full{s}"), 16)

            ada_load(M_SH1)
            ada_load(M_SC1)
            for pair in range(3):
                skip = (0, GATE_RANK, GATE_RANK + RD)[pair]
                with sp.Fori(2 * pair, 2 * pair + 2) as g:
                    for s in range(4):
                        sp.wait_ge(S("ring_free"), (g + IN_ROUND - 1) * 4 + s + 1)
                        src = w_in[0, :, bass.ds(g * 1024 + skip + s * 256, 256)]
                        sp.dma_start(slot(s).rearrange("p (k c) -> p k c", c=256),
                                     src.rearrange("(k p) c -> p k c", p=P)).then_inc(S(f"ring_full{s}"), 16)
            def ada_load2(weights, sec, at, peeled=0):
                for i in range(8):
                    s = i % 2
                    if i < peeled:
                        sp.wait_ge(S("ring_free"), (IN_ROUND + 5) * 4 + s + 1)
                    else:
                        sp.wait_ge(S("r2_free"), (sec - 2) * 8 + (i - 1))
                    src = weights[:, bass.ds(at * D, D)].rearrange("(k p) c -> p k c", p=P)
                    sp.dma_start(slot(s).rearrange("p (k c) -> p k c", c=D), src[:, 2 * i:2 * i + 2, :])\
                        .then_inc(S(f"r2_full{s}"), 16)

            ada_load2(w_ada[0], 2, 2, peeled=2)
            with sp.Fori(3, 6) as sec:
                ada_load2(w_ada[0], sec, sec)
            with sp.Fori(6, 8) as sec:
                ada_load2(w_ada_final, sec, sec - 6)
            for i in range(8):
                s = i % 4
                if i >= 4:
                    sp.wait_ge(S("out_ps"), 2 * s + 2)
                elif s < 2:
                    sp.wait_ge(S("r2_free"), 47 + s)
                else:
                    sp.wait_ge(S("ck_y"), 2 * NCH)
                    sp.wait_ge(S("ck_yev"), 2 * NCH)
                    sp.wait_ge(S("rs_out"), 16 * RD // SI)
                    sp.wait_ge(S("ys_row"), RD // SI)
                sp.dma_start(slot(s).rearrange("p (k c) -> p k c", c=256),
                             w_out[0, :, i * 256:(i + 1) * 256].rearrange("(k p) c -> p k c", p=P))\
                    .then_inc(S(f"wo_full{s}"), 16)
            sp.wait_ge(*once("sr_ps"))
            sp.wait_ge(S("ck_s"), 2 * NCH)

            def expert_load(expert, before=None):
                for s in range(MOE_SLOTS):
                    if before is not None:
                        sp.wait_ge(S("m_free"), before + (s + 1))
                    elif s < MIX_SLOTS:
                        sp.wait_ge(S("out_ps"), 8 + 2 * s + 2)
                    half, w = s % 2, (w_exp_gate, w_exp_up, w_exp_down)[s // 2]
                    src = w[0].rearrange("g e a b -> (g e) a b")[bass.ds(expert, 1)]
                    if s < 4:
                        src = src.rearrange("o (k p) f -> p (o k) f", p=P)[:, 8 * half:8 * half + 8, :]
                    else:
                        src = src.rearrange("o (k p) f -> p (o k) f", p=P)[:, 2 * half:2 * half + 2, :]
                    sp.dma_start(slot(s).rearrange("p (k f) -> p k f", f=src.shape[2]), src)\
                        .then_inc(S(f"m_full{s}"), 16)

            expert_load(0)
            with sp.Fori(1, NEXP) as e:
                expert_load(e, (e - 1) * MOE_SLOTS)
            sp.wait_ge(*once("cap_ready"))
            count = sp.value_load(most[0:1, 0:1], min_val=0, max_val=NP_)
            with sp.If(count > CAP):
                with sp.Fori(1, PASSES) as ps:
                    with sp.Fori(0, NEXP) as e:
                        expert_load(e, ps * (NEXP * MOE_SLOTS) + e * MOE_SLOTS - MOE_SLOTS)
            for c in range(TC):
                sp.wait_ge(S("yo_evac"), 4 * c + 4)
                sp.dma_start(y_prompt[0, c * P:(c + 1) * P, :], y_tok[:, c, :]).then_inc(S("y_out"), 16)
            sp.wait_ge(S("yo_evac"), 12)
            sp.dma_start(y_sample[:, 0, :], ys_tok).then_inc(S("y_out"), 16)
            sp.wait_ge(S("y_out"), 48)

        @block.gpsimd
        def _(pool):
            link = Chain(pool, "consts")
            link(pool.memset(ident[:], 0.0))
            link(pool.memset(bones[:], 0.0))
            link(pool.memset(ones[:], 1.0))
            pool.iota(idx_f, pattern=[[1, P]], base=0, channel_multiplier=0).then_inc(S("iotas"), 1)
            pool.iota(idx_p, pattern=[[0, P]], base=0, channel_multiplier=1).then_inc(S("iotas"), 1)
            link(pool.affine_select(out=ident[:], in_=ident[:], compare_op=ALU.not_equal, fill=1.0, base=0,
                                    pattern=[[-1, P]], channel_multiplier=1))
            link(pool.affine_select(out=mstrict[:], in_=ones[:], compare_op=ALU.is_gt, fill=0.0, base=0,
                                    pattern=[[1, P]], channel_multiplier=-1))
            for h in range(2):
                r = slice(RD * h, RD * h + RD)
                link(pool.memset(bones[r, r], 1.0))
                link(pool.affine_select(out=mincl[r, :], in_=ones[r, 0:CH], compare_op=ALU.is_ge, fill=0.0, base=0,
                                        pattern=[[1, CH]], channel_multiplier=-1))
            assert link.n == N_CONSTS
            pool.wait_ge(S("xT_ps"), KD)
            pool.wait_ge(*once("cT_ready"))
            for tile, part, col, width in SHIFT_PARTS:
                at = tile * P + part
                pool.dma_start(shift_row[:, at:at + width], state_shift[0, :, col:col + width])\
                    .then_inc(S("shift_in"), 16)
            cols = [(0, GCOLS + 1024, RD), (RD, GCOLS + 3136, RD), (2 * RD, GCOLS + 3200, P), (4 * RD, 2048, GATE_RANK)]
            for at, col, width in cols:
                pool.dma_start(small_w[:, :, at:at + width],
                               w_in[0, :, col:col + width].rearrange("(k p) c -> p k c", p=P))\
                    .then_inc(S("small_w_in"), 16)
            pool.wait_ge(S("ring_free"), (IN_ROUND + 6) * 4)
            pool.wait_ge(S("in_evac_a"), 24)
            pool.wait_ge(S("in_evac_d"), 24)
            pool.wait_ge(*once("in_small_a"))
            pool.wait_ge(S("in_small_d"), 2)
            pool.wait_ge(*once("shs_ready"))
            pool.wait_ge(S("so_ps"), 7)
            mix = Chain(pool, "mix_chain")
            rp = pj[:, TR:TG7 + 1, :]
            mix(pool.tensor_tensor(dl[:, :, NP_:NT], shs, rp[:, :, NP_:NT], ALU.subtract))
            pool.tensor_scalar(dl[:, :, 0:1], rp[:, :, 0:1], -1.0, None, ALU.mult)
            mix(pool.tensor_tensor(dl[:, :, 1:NP_], rp[:, :, 0:NP_ - 1], rp[:, :, 1:NP_], ALU.subtract))
            mu = vecs[:, V_MU:V_MU + 26].unsqueeze(2).to_broadcast([P, 26, NT])
            mix(pool.tensor_tensor(dl, dl, mu, ALU.mult))
            pool.tensor_tensor(rp, rp, dl, ALU.add).then_inc(S("shift_mixed"), 1)
            pool.wait_ge(S("shift_mixed"), 1)
            pool.wait_ge(S("so_evac"), 7)
            for tile, part, col, width in SHIFT_PARTS:
                at = tile * P + part
                pool.dma_start(ss_prompt[0, :, col:col + width], shift_out[0:1, at:at + width]).then_inc(S("ss_out"), 16)
                pool.dma_start(ss_sample[0, :, col:col + width], shift_out[1:COND, at:at + width])\
                    .then_inc(S("ss_out"), 16)
            pool.wait_ge(S("ss_out"), 16 * 2 * len(SHIFT_PARTS))
            pool.dma_start(wa2[0:RD, :], rwkv_w2[0]).then_inc(S("low_rank_in"), 16)
            pool.dma_start(wa2[RD:P, :], rwkv_a2[0]).then_inc(S("low_rank_in"), 16)
            for h in range(GLA_H):
                pool.dma_start(gs[h], state_gla[0, :, h].rearrange("b k v -> k b v")).then_inc(S(f"sgs_in{h}"), 16)
            pool.wait_ge(*once("gst_evac"))
            pool.dma_start(sg_prompt[0, 0].rearrange("h k v -> k h v"), sg_new).then_inc(S("sg_out"), 16)
            pool.wait_ge(S("sg_out"), 16)
            for h in range(GLA_H):
                pool.wait_ge(S("gs_s"), h + 1)
                pool.dma_start(sg_sample[0, :, h].rearrange("b k v -> k b v"), gs[h]).then_inc(S("sgs_out"), 16)
            pool.dma_start(g2[:], rwkv_g2[0]).then_inc(S("g2_in"), 16)
            pool.wait_ge(S("sgs_out"), 16 * GLA_H)
            pool.wait_ge(*once("sv_evac"))
            pool.dma_start(scratch, sv_row).then_inc(S("sv_store"), 16)
            pool.wait_ge(S("sv_store"), 16)
            for v in range(6):
                pool.dma_start(svt[:, v, :], scratch[v * NS:(v + 1) * NS, :].rearrange("b (h d) -> (b h) d", d=RD))\
                    .then_inc(S("sv_in"), 16)
            pool.wait_ge(S("sv_in"), 96)
            vr, vw, vk, vv, vkk, vb = (svt[:, i, :] for i in range(6))

            def over_i(x):
                return x.unsqueeze(1).to_broadcast([P, SI, RD])

            def over_j(x):
                return x.unsqueeze(2).to_broadcast([P, SI, RD])

            state_in = state_rwkv[0].rearrange("b h i j -> (b h) i j")
            state_out = sr_sample[0].rearrange("b h i j -> (b h) i j")
            STEPS = 20
            rs_link = Chain(pool, "rs_chain")

            def sum_keys(x):
                w = RD
                while w > 1:
                    w //= 2
                    rs_link(pool.tensor_tensor(x[:, :, 0:w], x[:, :, 0:w], x[:, :, w:2 * w], ALU.add))

            for n in range(RD // SI):
                rows = slice(n * SI, (n + 1) * SI)
                s_ = rs[n % 2]
                if n == 0:
                    for q in range(2):
                        pool.dma_start(rs[q], state_in[:, q * SI:(q + 1) * SI, :]).then_inc(S(f"rs_in{q}"), 16)
                pool.wait_ge(S(f"rs_in{n % 2}"), (n // 2 + 1) * 16)
                rs_link(pool.tensor_tensor(rt, s_, over_i(vkk), ALU.mult))
                sum_keys(rt)
                rs_link(pool.tensor_copy(sa_row.unsqueeze(2), rt[:, :, 0:1]))
                rs_link(pool.tensor_tensor(s_, s_, over_i(vw), ALU.mult))
                rs_link(pool.tensor_tensor(rt, over_j(sa_row), over_i(vb), ALU.mult))
                rs_link(pool.tensor_tensor(s_, s_, rt, ALU.subtract))
                rs_link(pool.tensor_tensor(rt, over_j(vv[:, rows]), over_i(vk), ALU.mult))
                rs_link(pool.tensor_tensor(s_, s_, rt, ALU.add))
                pool.dma_start(state_out[:, rows, :], s_).then_inc(S("rs_out"), 16)
                rs_link(pool.tensor_tensor(rt, s_, over_i(vr), ALU.mult))
                sum_keys(rt)
                pool.tensor_copy(y_row[:, rows].unsqueeze(2), rt[:, :, 0:1]).then_inc(S("ys_row"), 1)
                pool.wait_ge(S("ys_row"), n + 1)
                if n + 2 < RD // SI:
                    pool.wait_ge(S("rs_out"), (n + 1) * 16)
                    pool.dma_start(s_, state_in[:, (n + 2) * SI:(n + 3) * SI, :]).then_inc(S(f"rs_in{n % 2}"), 16)
            pool.wait_ge(S("rs_out"), 16 * RD // SI)
            pool.wait_ge(*once("sr_evac"))
            for h in range(2):
                r = slice(RD * h, RD * h + RD)
                pool.dma_start(sr_prompt[0, 0].rearrange("(p h) i j -> h i p j", h=2)[h], sr_new[r, :, r])\
                    .then_inc(S("sr_out"), 16)
            pool.wait_ge(S("sr_out"), 32)
            pool.wait_ge(S("o_rwkv"), 8)
            pool.dma_start(w_rt[:, :, 0:NG], w_router_group[0].rearrange("(k p) c -> p k c", p=P)).then_inc(S("rt_in"), 16)
            pool.dma_start(w_rt[:, :, NG:NG + NEXP], w_router_expert[0].rearrange("(k p) c -> p k c", p=P))\
                .then_inc(S("rt_in"), 16)
            rlink = Chain(pool, "rt_consts")
            rlink(pool.iota(slot_no, pattern=[[0, 2], [1, SLOT]], base=0, channel_multiplier=0,
                            allow_small_or_imprecise_dtypes=True))
            rlink(pool.memset(slot_no[:, :, 0:NS], -4096.0))
            rlink(pool.iota(eight, pattern=[[1, NE]], base=0, channel_multiplier=0, allow_small_or_imprecise_dtypes=True))
            rlink(pool.memset(own_slot, 0.0))
            rlink(pool.tensor_copy(own_slot[:, :, 0:NS], ident[0:NS, 0:NS].unsqueeze(1).to_broadcast([NS, 2, NS])))

        @block.scalar
        def _(act):
            act.wait_ge(*once("c_zeroed"))
            act.dma_start(c_row[0:1, :], c_prompt).then_inc(S("c_in"), 16)
            act.dma_start(c_row[1:COND, :], c_sample).then_inc(S("c_in"), 16)
            act.dma_start(x_tok, x_prompt[0].rearrange("(c p) d -> p c d", p=P)).then_inc(S("x_in"), 16)
            act.dma_start(x_row, x_sample[:, 0, :]).then_inc(S("x_in"), 16)
            act.wait_ge(S("c_in"), 32)
            act.activation(c_row, c_row, ACT.Silu).then_inc(once("c_silu")[0], 1)
            rows = [[b_ada[0], b_ada_final],
                    [norm_mix[0], norm_ffn[0], norm_final, rwkv_mu[0, 0:1024], rwkv_mu[0, 1088:2112],
                     rwkv_mu[0, 2112:3136], (rwkv_mu[0, 1024:1088], 0), (rwkv_mu[0, 3136:3200], RD),
                     rwkv_mu[0, 3200:3328], gla_gate_b[0], gla_norm[0]],
                    [rwkv_w0[0], rwkv_a0[0], rwkv_k_k[0], rwkv_k_a[0], rwkv_r_k[0].rearrange("h d -> (h d)"),
                     rwkv_gn_w[0], rwkv_gn_b[0]]]
            n_vec = 0
            for g, group in enumerate(rows):
                at = 0
                for v in group:
                    if isinstance(v, tuple):
                        v, c = v
                        act.dma_start(vec_rows[at:at + 1, g, c:c + RD], v.rearrange("(r c) -> r c", c=RD))\
                            .then_inc(S("vec_in"), 16)
                        at += c // RD
                    else:
                        n = v.shape[0] // P
                        act.dma_start(vec_rows[at:at + n, g, :], v.rearrange("(r c) -> r c", c=P))\
                            .then_inc(S("vec_in"), 16)
                        at += n
                    n_vec += 1
            assert n_vec == N_VEC
            act.dma_start(gw2, gla_gate_w2[0]).then_inc(S("gate_w_in"), 16)
            for k in range(KD):
                act.wait_ge(S("xT_ps"), k + 1)
                act.copy(xt[:, k, :], pb[2 + k % 4][:, 0:NT]).then_inc(S("xT_evac"), 1)

            def square(sem, out, in_):
                act.activation(out, in_, ACT.Square).then_inc(S(sem), 1)

            def root(n):
                act.wait_ge(S("ms_sum"), n)
                act.activation(rstd, rstd, ACT.Sqrt).then_inc(S("rms_root"), 1)

            act.wait_ge(S("xT_evac"), KD)
            square("norm_sq", ht[:, :, :], xt[:, :, :])
            root(1)

            def ada(sec):
                n = sec
                if isinstance(sec, int) and sec < 2:
                    act.wait_ge(S("ring_free"), (2 * sec + 2) * 4)
                else:
                    act.wait_ge(S("r2_free"), (sec - 2) * 8 + 8)
                act.wait_ge(S("ada_tr"), n)
                act.copy(ada_row[:], pb[7][:]).then_inc(S("ada_evac"), 1)

            ada(M_SH1)
            ada(M_SC1)
            for k in range(8, KD):
                act.wait_ge(S("mod_g"), 1)
                act.activation(ht[:, k, 0:NP_], ht[:, k, 0:NP_], ACT.Identity, bias=mod[:, M_SH1, k, 0:1],
                               scale=gscale[:, k, 0:1]).then_inc(S("h_act"), 1)
            with act.Fori(0, 6) as g:
                for t in range(0, 8, 2):
                    act.wait_ge(S("in_ps"), g * 4 + t // 2 + 1)
                    act.copy(pj[:, bass.ds(g * 8 + t, 1), :], pb[t % 4][:, 0:NT].rearrange("p (o n) -> p o n", o=1))\
                        .then_inc(S("in_evac_a"), 1)
            act.wait_ge(S("in_small"), 2)
            act.copy(pj[:, TG7, :], pb[1][:, 0:NT]).then_inc(once("in_small_a")[0], 1)
            for b in range(7):
                act.wait_ge(S("so_ps"), b + 1)
                n = min(BANK, RCOLS - b * BANK)
                act.copy(shift_out[:, b * BANK:b * BANK + n], pb[3 + b % 2][0:COND, 0:n]).then_inc(S("so_evac"), 1)
            act.wait_ge(*once("shs_ps"))
            for b in range(4):
                act.wait_ge(S("vt_ps"), b + 1)
                act.copy(v_tok[:, b // 2, (b % 2) * BANK:(b % 2 + 1) * BANK], pb[b][:]).then_inc(S("vt_evac"), 1)
            act.wait_ge(*once("vs_ps"))
            act.wait_ge(S("mix_chain"), 1)
            for b in range(2):
                last = act.copy(v_row[:, b * BANK:(b + 1) * BANK], pb[4 + b][0:NS, :])
            last.then_inc(once("vs_evac")[0], 1)
            act.wait_ge(*once("ks_ps"))
            act.copy(k_row, pb[0][0:NS, :]).then_inc(once("ks_evac")[0], 1)
            act.wait_ge(*once("g_z"))
            link = Chain(act, "act_chain")
            link(act.activation(l4, z4, ACT.Abs))
            link(act.activation(l4, l4, ACT.Exp, scale=-1.0))
            act.activation(l4, l4, ACT.Ln, bias=1.0).then_inc(once("g_ln")[0], 1)
            act.wait_ge(*once("g_log"))
            act.activation(eg.rearrange("p (h b) -> p h b", b=NS), z4[:, :, NP_:NT], ACT.Exp).then_inc(once("eg")[0], 1)
            for l in range(LEVELS):
                act.wait_ge(S("lv_d"), l + 1)
                link(act.activation(e_flat, e_flat, ACT.Abs))
                act.activation(e_flat, e_flat, ACT.Exp, scale=-1.0).then_inc(S("lv_e"), 1)
            act.wait_ge(S("lv_qk"), LEVELS)
            for h in range(GLA_H):
                last = act.activation(e_flat[:, h * NP_:(h + 1) * NP_], cum4[:, h, :], ACT.Exp, scale=-1.0,
                                      bias=cum4[:, h, NP_ - 1:NP_])
            last.then_inc(once("kd_e")[0], 1)
            act.wait_ge(*once("kd_ps"))
            for c in range(TC):
                last = act.copy(kd_tok[:, c, :], pb[4 + c][:])
            last.then_inc(once("kd_evac")[0], 1)
            ada(2)
            act.wait_ge(S("ss_out"), 16 * 2 * len(SHIFT_PARTS))
            for b in range(4):
                act.wait_ge(S("go_ps"), b + 1)
                act.copy(ht[:, 2 * b:2 * b + 2, 0:NP_], pb[b][:].rearrange("p (t n) -> p t n", n=NP_))\
                    .then_inc(S("go_evac"), 1)
            act.wait_ge(*once("gst_ps"))
            act.wait_ge(*once("kd_e"))
            act.copy(sg_new[:, 0:2, :], pb[4][:].rearrange("p (h e) -> p h e", e=GLA_DV)).then_inc(once("gst_evac_a")[0], 1)
            act.wait_ge(*once("gst_evac_a"))
            act.copy(sg_new[:, 2:4, :], pb[5][:].rearrange("p (h e) -> p h e", e=GLA_DV)).then_inc(once("gst_evac")[0], 1)
            act.wait_ge(S("shift_mixed"), 1)
            link(act.activation(pj[:, TOG:TOG + 8, :], pj[:, TOG:TOG + 8, :], ACT.Silu))
            link(act.activation(pj[0:RD, TWA, :], pj[0:RD, TWA, :], ACT.Tanh))
            act.activation(pj[:, TG7, :], pj[:, TG7, :], ACT.Sigmoid).then_inc(once("gates_act")[0], 1)
            act.wait_ge(*once("gs_o"))
            for b in range(4):
                last = act.copy(o_rows[:, b // 2, (b % 2) * BANK:(b % 2 + 1) * BANK], pb[b][:])
            last.then_inc(once("or_evac")[0], 1)
            ada(3)
            act.wait_ge(*once("os_ps"))
            for a in range(2):
                for i in range(2):
                    last = act.copy(ht[:, 4 * i:4 * i + 4, NP_ + 4 * a:NP_ + 4 * a + 4],
                                    pb[2 * a + i][:].rearrange("p (t g r) -> p t g r", g=4, r=CPAD)[:, :, :, CPAD - 1])
            last.then_inc(once("gos_evac")[0], 1)
            act.wait_ge(*once("gos_evac"))
            act.wait_ge(S("go_evac"), 4)
            act.activation(gla_sq, o_gla, ACT.Square).then_inc(once("gla_sq")[0], 1)
            act.wait_ge(*once("gla_ms"))
            act.activation(gla_r, gla_r, ACT.Sqrt).then_inc(once("gla_root")[0], 1)
            act.wait_ge(S("sgs_out"), 16 * GLA_H)
            act.wait_ge(*once("gla_done"))
            for i in range(16):
                t = i % 8
                act.wait_ge(S("rs_ps"), i + 1)
                dst, at = ((t0, V_W0), (rb, V_A0))[i // 8]
                act.activation(dst[:, t, :], pb[i % 4][:, 0:NT], ACT.Sigmoid, bias=vecs[:, at + t:at + t + 1])\
                    .then_inc(S("rs_evac"), 1)
            act.wait_ge(*once("kk_raw"))
            act.activation(t2, ra, ACT.Square).then_inc(once("kk_sq")[0], 1)
            for t in range(8):
                act.wait_ge(S("kn_ps"), t + 1)
                act.activation(t1[:, t, :], pb[t % 4][:, 0:NT], ACT.Sqrt).then_inc(S("kn_evac"), 1)
            act.wait_ge(*once("lw"))
            act.activation(sv[:, :, 1, :], t0[:, :, NP_:NT], ACT.Exp).then_inc(once("sv_w")[0], 1)
            act.wait_ge(*once("sv_ps"))
            for b in range(2):
                last = act.copy(sv_row[:, b * BANK:(b + 1) * BANK], pb[b][0:48, :])
            last.then_inc(once("sv_evac")[0], 1)
            for i, scale in enumerate((1.0, 1.0, -1.0)):
                act.wait_ge(S("cw_e"), i + 1)
                src = t2 if i == 0 else t1
                act.activation(t2[:, :, 0:NP_], src[:, :, 0:NP_], ACT.Exp, scale=scale).then_inc(S("cw_exp"), 1)

            act.wait_ge(S("sv_store"), 16)

            def tiles(bank):
                return pb[bank][:].rearrange("p (j n) -> p j n", n=P)

            with act.Fori(0, NCH) as c:
                for hf in range(2):
                    js = slice(4 * hf, 4 * hf + 4)
                    act.wait_ge(S("ck_y"), c * 2)
                    act.wait_ge(*once("ck_zero"))
                    for h in range(2):
                        r = slice(CH * h, CH * h + CH)
                        act.copy(kp[hf][r, :, r], rk[r, js, bass.ds(c * CH, CH)])
                        last = act.copy(vp[hf][r, :, r], rv[r, js, bass.ds(c * CH, CH)])
                    last.then_inc(S("ck_pad_a"), 1)
                for hf in range(2):
                    act.wait_ge(S("ck_t1"), c * 2 + (hf + 1))
                    for i, x in enumerate((bp, kp, vp)):
                        last = act.copy(x[hf], tiles(3 * hf + i))
                    last.then_inc(S("ck_t1e"), 1)
                for hf in range(2):
                    act.wait_ge(S("ck_t0"), c * 2 + (hf + 1))
                    act.copy(tm[hf], tiles(3 * hf)).then_inc(S("ck_t0e"), 1)
                    act.wait_ge(S("ck_u"), c * 2 + (hf + 1))
                    act.copy(um[hf], tiles(3 * hf + 1)).then_inc(S("ck_ue"), 1)
                for l in range(1, 6):
                    for hf in range(2):
                        act.wait_ge(S("iv_p"), c * 10 + (2 * l - 1 + hf))
                        act.copy(pm[hf], tiles(3 * hf + 2)).then_inc(S("iv_pe"), 1)
                for hf in range(2):
                    act.wait_ge(S("ck_sa"), c * 2 + (hf + 1))
                    act.copy(tm[hf], tiles(3 * hf + 2)).then_inc(S("ck_sae"), 1)
                ada(c + 4)
                for hf in range(2):
                    act.wait_ge(S("ck_y"), c * 2 + (hf + 1))
                    act.copy(y8[:, 4 * hf:4 * hf + 4, bass.ds(c * CH, CH)], tiles(3 * hf)[:, :, 0:CH])\
                        .then_inc(S("ck_yev"), 1)
            act.wait_ge(*once("sr_ps"))
            for b in range(2):
                last = act.copy(sr_new[:, 4 * b:4 * b + 4, :], pb[b][:].rearrange("p (j n) -> p j n", n=P))
            last.then_inc(once("sr_evac")[0], 1)
            act.wait_ge(*once("gn_c"))
            act.activation(ra, y8, ACT.Square).then_inc(once("gn_sq")[0], 1)
            act.wait_ge(*once("gn_ms"))
            act.activation(rr, rr, ACT.Sqrt).then_inc(once("gn_root")[0], 1)

            def scale_upper(n, sh):
                for k in range(8, KD):
                    act.wait_ge(S("mod_g"), n)
                    act.activation(ht[:, k, 0:NP_], ht[:, k, 0:NP_], ACT.Identity, bias=mod[:, sh, k, 0:1],
                                   scale=gscale[:, k, 0:1]).then_inc(S("h_act"), 1)

            act.wait_ge(S("x1"), KD)
            square("norm_sq", ht[:, :, :], xt[:, :, :])
            root(2)
            scale_upper(2, M_SH2)
            act.wait_ge(*once("lg_ps"))
            act.copy(lg_t, pb[1][0:NG + NEXP, 0:NT]).then_inc(once("lg_evac")[0], 1)
            for b in range(8):
                act.wait_ge(S("h2t_ps"), b + 1)
                act.copy(h_tok[:, b // 4, (b % 4) * BANK:(b % 4 + 1) * BANK], pb[3 + b % 4][:]).then_inc(S("h2t_evac"), 1)
            act.wait_ge(*once("rt_d1"))
            act.activation(g_exp, g_exp, ACT.Exp).then_inc(once("rt_e1")[0], 1)
            act.wait_ge(*once("rt_d2"))
            act.activation(e2, e2, ACT.Exp).then_inc(once("rt_e2")[0], 1)

            def moe_gather_out(n):
                for b in range(2):
                    act.wait_ge(S("m_ga"), n * 4 + (b + 1))
                    act.copy(xg[:, :, 4 * b:4 * b + 4, :], pb[b][:].rearrange("p (k q s) -> p q k s", q=2, s=SLOT))\
                        .then_inc(S("m_ga_a"), 1)

            def moe_act(ps):
                moe_gather_out(ps * 17)
                with act.Fori(0, NEXP // 2) as i:
                    t = ps * 16 + i
                    for q in range(2):
                        used = (t * 2 + q) * MOE_SLOTS
                        act.wait_ge(S(f"m_wt{q}"), t + 1)
                        act.copy(pwt[:, q, :], pb[5 - q][:, 0:NT]).then_inc(S(f"m_wte{q}"), 1)
                        act.wait_ge(S("m_free"), used + 4)
                        act.activation(sg[:, q, :], pb[4 + q][:, 0:256], ACT.Silu).then_inc(S(f"m_sg{q}"), 1)
                        if q == 1:
                            moe_gather_out(ps * 17 + i + 1)
                        act.wait_ge(S(f"m_hp{q}"), t + 1)
                        act.copy(hid_t[:, q, :], pb[4 + q][:, 0:256]).then_inc(S(f"m_ht{q}"), 1)
                        act.wait_ge(S("m_free"), used + 6)
                        act.wait_ge(S(f"m_sc{q}"), (t + q) * KD + ps * (KD if q else 0))
                        act.copy(y_slot[:, q, 0:BANK], pb[6][:])
                        act.copy(y_slot[:, q, BANK:2 * BANK], pb[7][:]).then_inc(S(f"m_ye{q}"), 1)

            moe_act(0)
            act.wait_ge(*once("cap_ready"))
            count = act.value_load(most[0:1, 0:1], min_val=0, max_val=NP_)
            with act.If(count > CAP):
                with act.Fori(1, PASSES) as ps:
                    moe_act(ps)
            act.wait_ge(S("x2"), 1)
            square("norm_sq", ht[:, :, :], xt[:, :, :])
            root(3)
            scale_upper(3, M_SHF)
            for b in range(0, 12, 2):
                act.wait_ge(S("yo_ps"), b + 1)
                dst = (y_tok[:, b // 4, (b % 4) * BANK:(b % 4 + 1) * BANK] if b < 8 else
                       ys_tok[:, (b - 8) * BANK:(b - 7) * BANK])
                act.wait_ge(S("yo_evac"), b)
                act.copy(dst, pb[1 + b % 4][0:dst.shape[0], :]).then_inc(S("yo_evac"), 1)

        @block.vector
        def _(dve):
            link = Chain(dve, "dve_chain")
            dve.memset(c_row, 0.0).then_inc(once("c_zeroed")[0], 1)
            dve.wait_ge(S("iotas"), 2)
            link(dve.tensor_tensor(idx_x, idx_f, idx_p, ALU.bitwise_xor))
            dve.tensor_copy(xor_f, idx_x)
            link(dve.tensor_tensor(tri_f, idx_f, idx_p, ALU.is_gt))
            dve.tensor_scalar(lm[:, 7, :], xor_f, 0.0, None, ALU.is_equal)
            link(dve.tensor_tensor(tri_f, xor_f, tri_f, ALU.mult))
            for l in range(7):
                link(dve.tensor_scalar(ge_f, tri_f, float(2 ** l), None, ALU.is_ge))
                link(dve.scalar_tensor_tensor(out=lm[:, l, :], in0=tri_f, scalar=float(2 ** (l + 1)), in1=ge_f,
                                              op0=ALU.is_lt, op1=ALU.mult))
            dve.wait_ge(*once("cT_ps"))
            dve.tensor_copy(ct[:, :, :], pb[0][:].rearrange("p (k n) -> p k n", n=CPAD)).then_inc(once("cT_ready")[0], 1)
            dve.wait_ge(*once("vec_ps"))
            dve.tensor_copy(vecs[:], pb[1][:, 0:V_END]).then_inc(once("vecs_ready")[0], 1)
            dve.wait_ge(*once("vecs_ready"))

            def vec(at, n, m):
                return vecs[:, at:at + n].unsqueeze(2).to_broadcast([P, n, m])

            def rms_start(n):
                dve.wait_ge(S("ms_ps"), n)
                dve.tensor_scalar(rstd, pb[0][:, 0:NT], 1.0 / D, EPS, ALU.mult, ALU.add).then_inc(S("ms_sum"), 1)
                dve.wait_ge(S("rms_root"), n)
                link(dve.reciprocal(rstd, rstd))
                link(dve.tensor_tensor(ht[:, :, :], xt[:, :, :], rstd.unsqueeze(1).to_broadcast([P, KD, NT]), ALU.mult))

            def modulate(n, norm, sc, sh):
                dve.scalar_tensor_tensor(out=gscale[:, :, :], in0=mod[:, sc], scalar=1.0, in1=vec(norm, KD, COND),
                                         op0=ALU.add, op1=ALU.mult).then_inc(S("mod_g"), 1)
                dve.wait_ge(S("mod_g"), n)
                for k in range(8):
                    dve.tensor_scalar(ht[:, k, 0:NP_], ht[:, k, 0:NP_], gscale[:, k, 0:1], mod[:, sh, k, 0:1],
                                      ALU.mult, ALU.add)
                link(dve.tensor_tensor(ht[:, :, NP_:NT], ht[:, :, NP_:NT], gscale[:, :, 1:COND], ALU.mult))
                dve.tensor_tensor(ht[:, :, NP_:NT], ht[:, :, NP_:NT], mod[:, sh, :, 1:COND], ALU.add)\
                    .then_inc(S("h_dve"), 1)

            def ada(sec):
                n = sec
                dve.wait_ge(S("ada_tr"), n + 1)
                src = pb[6][:].rearrange("p (j g r) -> p g j r", j=4, g=4)[:, :, :, 0:COND]
                dst = mod[:, bass.ds(sec, 1)].rearrange("p o (g j) r -> p (o g) j r", g=4)
                b = vecs[:, bass.ds(sec * KD + V_ADA, KD)].rearrange("p (g j) -> p g j", g=4)
                dve.tensor_tensor(dst, src, b.unsqueeze(3).to_broadcast([P, 4, 4, COND]), ALU.add)\
                    .then_inc(S("ada_mod"), 1)

            rms_start(1)
            ada(M_SH1)
            ada(M_SC1)
            dve.wait_ge(S("ada_mod"), 2)
            modulate(1, V_NMIX, M_SC1, M_SH1)
            with dve.Fori(0, 6) as g:
                for t in range(1, 8, 2):
                    dve.wait_ge(S("ring_free"), g * 4 + IN_ROUND * 4 + t // 2 + 1)
                    dve.tensor_copy(pj[:, bass.ds(g * 8 + t, 1), :], pb[t % 4][:, 0:NT].rearrange("p (o n) -> p o n", o=1))\
                        .then_inc(S("in_evac_d"), 1)
            dve.wait_ge(S("in_small"), 1)
            dve.tensor_copy(pj[:, TWA, :], pb[0][:, 0:NT]).then_inc(S("in_small_d"), 1)
            dve.wait_ge(S("in_small"), 3)
            dve.tensor_copy(pj[0:GATE_RANK, TGL, :], pb[2][0:GATE_RANK, 0:NT]).then_inc(S("in_small_d"), 1)
            dve.wait_ge(*once("shs_ps"))
            dve.tensor_copy(shs, pb[5][:, 0:26 * NS].rearrange("p (t n) -> p t n", n=NS)).then_inc(once("shs_ready")[0], 1)
            dve.wait_ge(*once("gz_ps"))
            for h in range(GLA_H):
                last = dve.tensor_scalar(z4[:, h, :], pb[h][:, 0:NT], vecs[:, V_GB + h:V_GB + h + 1], None, ALU.add)
            last.then_inc(once("g_z")[0], 1)
            link(dve.tensor_scalar(pj[:, TQ:TQ + 4, :], pj[:, TQ:TQ + 4, :], GLA_DK ** -0.5, None, ALU.mult))
            dve.memset(at0[:, :, 0:P], 0.0)
            link(dve.memset(at1, 0.0))
            dve.wait_ge(*once("g_ln"))
            link(dve.scalar_tensor_tensor(out=z4, in0=z4, scalar=0.0, in1=l4, op0=ALU.min, op1=ALU.subtract))
            dve.tensor_scalar(z4, z4, 1.0 / 16.0, None, ALU.mult).then_inc(once("g_log")[0], 1)
            dve.wait_ge(*once("g_log"))
            for h in range(GLA_H):
                last = dve.tensor_tensor_scan(cum4[:, h, :], ones[:, 0:1].to_broadcast([P, NP_]), z4[:, h, 0:NP_], 0.0,
                                              ALU.mult, ALU.add)
            link(last)
            dve.wait_ge(*once("eg"))

            def level_diff(l):
                b, ref = levels(cum, NP_ >> l)
                e, _ = levels(e_flat, NP_ >> l)
                dve.tensor_tensor(e, b, ref, ALU.subtract).then_inc(S("lv_d"), 1)

            level_diff(0)
            e4 = e_flat.rearrange("p (h n) -> p h n", n=NP_)
            for l in range(LEVELS + 1):
                if l < LEVELS:
                    dve.wait_ge(S("lv_e"), l + 1)
                    if l > 0:
                        dve.wait_ge(S("lv_ps"), l)
                    dve.tensor_tensor(q4, pj[:, TQ:TQ + 4, 0:NP_], e4, ALU.mult)
                    dve.tensor_tensor(k4, pj[:, TK:TK + 4, 0:NP_], e4, ALU.mult).then_inc(S("lv_qk"), 1)
                if l + 1 < LEVELS:
                    dve.wait_ge(S("lv_qk"), l + 1)
                    level_diff(l + 1)
                dve.wait_ge(S("lv_ps"), l + 1)
                b = 2 * (l % 2)
                src = [pb[b + i][:].rearrange("p (h n) -> p h n", n=P) for i in range(2)]
                if l == 0:
                    dve.tensor_copy(at0[:, :, P:NP_], src[0]).then_inc(S("lv_sel"), 1)
                    continue
                m = lm[:, 7 - l if l < LEVELS else 7, :].bitcast(I32).unsqueeze(1).to_broadcast([P, GLA_H, P])
                dve.wait_ge(S("lv_sel"), l)
                dve.copy_predicated(at0[:, :, 0:P], m, src[0])
                dve.copy_predicated(at1, m, src[1]).then_inc(S("lv_sel"), 1)
            dve.wait_ge(*once("kd_e"))
            dve.wait_ge(S("lv_ps"), LEVELS + 1)
            dve.tensor_tensor(k4, pj[:, TK:TK + 4, 0:NP_], e4, ALU.mult).then_inc(once("kd")[0], 1)
            ada(2)
            for h in range(GLA_H):
                if h == 0:
                    dve.wait_ge(*once("ks_evac"))
                    dve.wait_ge(*once("gst_evac"))
                else:
                    dve.wait_ge(S("gs_kv"), 4 * h)
                dve.tensor_tensor(kz, k_row[:, h * GLA_DK:(h + 1) * GLA_DK].unsqueeze(1).to_broadcast([NS, NS, GLA_DK]),
                                  ident[0:NS, 0:NS].unsqueeze(2).to_broadcast([NS, NS, GLA_DK]), ALU.mult)\
                    .then_inc(S("kz"), 1)
                dve.wait_ge(S(f"sgs_in{h}"), 16)
                for b in range(NS):
                    if b % 2 == 0:
                        dve.wait_ge(S("gs_kv"), 4 * h + b // 2 + 1)
                    last = dve.scalar_tensor_tensor(
                        out=gs[h][:, b, :], in0=gs[h][:, b, :], scalar=eg[:, h * NS + b:h * NS + b + 1],
                        in1=pb[b // 2][:, (b % 2) * GLA_DV:(b % 2 + 1) * GLA_DV], op0=ALU.mult, op1=ALU.add)
                last.then_inc(S("gs_s"), 1)
            ada(3)
            dve.wait_ge(*once("gn_ps"))
            for h in range(GLA_H):
                last = dve.tensor_scalar(gla_r[:, h, :], pb[h][:, 0:NT], 1.0 / GLA_DV, GLA_EPS, ALU.mult, ALU.add)
            last.then_inc(once("gla_ms")[0], 1)
            dve.wait_ge(*once("gla_root"))
            link(dve.reciprocal(gla_r, gla_r))
            oh = o_gla.rearrange("p (h e) n -> p h e n", e=2)
            link(dve.tensor_tensor(oh, oh, gla_r.unsqueeze(2).to_broadcast([P, GLA_H, 2, NT]), ALU.mult))
            og = pj[:, TOG:TOG + 8, :].rearrange("p (h e) n -> p h e n", e=2)
            dve.wait_ge(*once("gates_act"))
            for e in range(2):
                last = dve.scalar_tensor_tensor(out=oh[:, :, e, :], in0=oh[:, :, e, :], scalar=vecs[:, V_GN + e:V_GN + e + 1],
                                                in1=og[:, :, e, :], op0=ALU.mult, op1=ALU.mult)
            last.then_inc(once("gla_done")[0], 1)
            dve.wait_ge(*once("gla_done"))
            dve.wait_ge(S("rs_evac"), 8)
            dve.tensor_scalar(t0, t0, -HALF_E, None, ALU.mult).then_inc(once("lw")[0], 1)
            dve.tensor_tensor(ra, rk, vec(V_KK, 8, NT), ALU.mult).then_inc(once("kk_raw")[0], 1)
            dve.wait_ge(*once("kk_raw"))
            dve.wait_ge(S("kn_evac"), 8)
            link(dve.tensor_scalar(t1, t1, 1e-12, None, ALU.max))
            link(dve.reciprocal(t1, t1))
            link(dve.tensor_tensor(ra, ra, t1, ALU.mult))
            dve.wait_ge(S("rs_evac"), 16)
            link(dve.scalar_tensor_tensor(out=t1, in0=rb, scalar=1.0, in1=vec(V_KA, 8, NT), op0=ALU.subtract, op1=ALU.mult))
            link(dve.scalar_tensor_tensor(out=rk, in0=t1, scalar=1.0, in1=rk, op0=ALU.add, op1=ALU.mult))
            link(dve.tensor_tensor(rb, rb, ra, ALU.mult))
            link(dve.tensor_tensor(t1, rr, rk, ALU.mult))
            dve.tensor_tensor(t1, t1, vec(V_RK, 8, NT), ALU.mult).then_inc(once("bonus_in")[0], 1)
            for v, src in ((0, rr), (2, rk), (3, rv), (4, ra), (5, rb)):
                last = dve.tensor_copy(sv[:, :, v, :], src[:, :, NP_:NT])
            last.then_inc(once("sv_rest")[0], 1)
            for t in range(8):
                dve.wait_ge(S("bonus_ps"), t + 1)
                dve.tensor_tensor(bonus[:, t, :], pb[2 + t % 2][:, 0:NT], rv[:, t, :], ALU.mult).then_inc(S("bonus_evac"), 1)
            dve.wait_ge(S("bonus_evac"), 8)
            keep = t2[:, 0, 0:NP_]
            dve.wait_ge(S("kn_ps"), 8)
            link(dve.memset(keep, 1.0))
            link(dve.memset(keep.rearrange("p (c n) -> p c n", n=CH)[:, :, 0:1], 0.0))
            for t in range(8):
                last = dve.tensor_tensor_scan(t1[:, t, 0:NP_], keep, t0[:, t, 0:NP_], 0.0, ALU.mult, ALU.add)
            link(last)
            dve.tensor_tensor(t2[:, :, 0:NP_], t1[:, :, 0:NP_], t0[:, :, 0:NP_], ALU.subtract).then_inc(S("cw_e"), 1)

            def pr(x):
                return x[:, :, 0:NP_]

            dve.wait_ge(S("cw_exp"), 1)
            link(dve.scalar_tensor_tensor(out=pr(ra), in0=pr(ra), scalar=-1.0, in1=pr(t2), op0=ALU.mult, op1=ALU.mult))
            dve.engine_nop().then_inc(S("cw_e"), 1)
            dve.wait_ge(S("cw_exp"), 2)
            dve.tensor_tensor(pr(rr), pr(rr), pr(t2), ALU.mult)
            link(dve.tensor_copy(wc, pr(t2).rearrange("p t (c n) -> p t c n", n=CH)[:, :, :, CH - 1]))
            dve.engine_nop().then_inc(S("cw_e"), 1)
            dve.wait_ge(S("cw_exp"), 3)
            dve.tensor_tensor(pr(rb), pr(rb), pr(t2), ALU.mult)
            link(dve.tensor_tensor(pr(rk), pr(rk), pr(t2), ALU.mult))
            dve.wait_ge(S("sgs_out"), 16 * GLA_H)
            for x in (ar, bp, kp, vp):
                for hf in range(2):
                    dve.memset(x[hf], 0.0)
            dve.memset(st, 0.0).then_inc(once("ck_zero")[0], 1)
            dve.wait_ge(*once("ck_zero"))

            def masks(m, count):
                return m.unsqueeze(1).to_broadcast([P, count, m.shape[1]])

            def tiles(bank):
                return pb[bank][:].rearrange("p (j n) -> p j n", n=P)

            with dve.Fori(0, NCH) as c:
                for hf in range(2):
                    js = slice(4 * hf, 4 * hf + 4)
                    dve.wait_ge(S("ck_y"), c * 2)
                    for h in range(2):
                        r = slice(CH * h, CH * h + CH)
                        dve.tensor_copy(ar[hf][r, :, r], ra[r, js, bass.ds(c * CH, CH)])
                        dve.tensor_copy(bp[hf][r, :, r], rb[r, js, bass.ds(c * CH, CH)])
                    dve.tensor_copy(ar[hf][:, :, P:192], rr[:, js, bass.ds(c * CH, CH)]).then_inc(S("ck_pad_d"), 1)
                for hf in range(2):
                    n = c * 2 + hf
                    dve.wait_ge(S("ck_g"), n + 1)
                    g = [pb[i][:, 0:384].rearrange("p (j n) -> p j n", n=192) for i in G_BANKS[hf]]
                    for i in range(2):
                        s2 = slice(2 * i, 2 * i + 2)
                        dve.tensor_tensor(ltm[hf][:, s2, :], g[i][:, :, 0:P], masks(mstrict[:], 2), ALU.mult)
                        dve.tensor_tensor(mtm[hf][:, s2, :], g[2 + i][:, :, 0:P], masks(mstrict[:], 2), ALU.mult)
                        dve.tensor_tensor(rbm[hf][:, s2, :], g[i][:, :, P:192], masks(mincl[:], 2), ALU.mult)
                        last = dve.tensor_tensor(rkm[hf][:, s2, :], g[2 + i][:, :, P:192], masks(mincl[:], 2), ALU.mult)
                    last.then_inc(S("ck_m"), 1)
                for hf in range(2):
                    n = c * 2 + hf
                    dve.wait_ge(S("ck_m"), n + 1)
                    dve.tensor_tensor(lo[hf], ltm[hf], masks(lm[:, 0, :], 4), ALU.mult).then_inc(S("ck_l0"), 1)
                    dve.wait_ge(S("ck_l0"), n + 1)
                    dve.tensor_tensor(tt[hf], lo[hf], masks(ident[:], 4), ALU.add).then_inc(S("ck_tt0"), 1)
                    dve.wait_ge(S("ck_tt0"), n + 1)
                    dve.tensor_tensor(lo[hf], ltm[hf], masks(lm[:, 1, :], 4), ALU.mult).then_inc(S("iv_lo"), 1)
                for l in range(1, 6):
                    for hf in range(2):
                        if l < 5:
                            dve.wait_ge(S("iv_p"), c * 10 + (2 * l - 1 + hf))
                            dve.tensor_tensor(lo[hf], ltm[hf], masks(lm[:, l + 1, :], 4), ALU.mult)\
                                .then_inc(S("iv_lo"), 1)
                    for hf in range(2):
                        dve.wait_ge(S("iv_t"), c * 10 + (2 * l - 1 + hf))
                        last = dve.tensor_tensor(tt[hf], tt[hf], tiles(3 * hf), ALU.add)
                        if l < 5:
                            last = dve.tensor_tensor(tm[hf], tm[hf], tiles(3 * hf + 1), ALU.add)
                        last.then_inc(S("iv_tn"), 1)
                for hf in range(2):
                    n = c * 2 + hf
                    js = slice(4 * hf, 4 * hf + 4)
                    dve.wait_ge(S("ck_y"), n + 1)
                    dve.tensor_tensor(st[:, js, :], st[:, js, :], tiles(3 * hf + 1), ALU.add).then_inc(S("ck_sadd"), 1)
                    dve.wait_ge(S("ck_sadd"), n + 1)
                    dve.tensor_tensor(st[:, js, :], st[:, js, :],
                                      wc[:, js, bass.ds(c, 1)].to_broadcast([P, 4, P]), ALU.mult).then_inc(S("ck_s"), 1)
                ada(c + 4)
            dve.wait_ge(*once("ys_ps"))
            dve.wait_ge(S("ck_yev"), 2 * NCH)
            for h in range(2):
                last = dve.tensor_copy(y8[RD * h:RD * h + RD, :, NP_:NT],
                                       pb[2][0:RD, 0:P].rearrange("p (b t h) -> p h t b", b=NS, h=2)[:, h])
            last.then_inc(once("y_all")[0], 1)
            dve.wait_ge(*once("y_all"))
            for t in range(8):
                dve.wait_ge(S("mu_ps"), t + 1)
                last = dve.scalar_tensor_tensor(out=y8[:, t, :], in0=pb[t % 4][:, 0:NT], scalar=-1.0 / RD, in1=y8[:, t, :],
                                                op0=ALU.mult, op1=ALU.add)
                last.then_inc(S("mu_evac"), 1)
            dve.wait_ge(S("mu_evac"), 8)
            dve.engine_nop().then_inc(once("gn_c")[0], 1)
            for t in range(8):
                dve.wait_ge(S("var_ps"), t + 1)
                last = dve.tensor_scalar(rr[:, t, :], pb[t % 4][:, 0:NT], 1.0 / RD, GN_EPS, ALU.mult, ALU.add)
                last.then_inc(S("var_evac"), 1)
            dve.wait_ge(S("var_evac"), 8)
            dve.engine_nop().then_inc(once("gn_ms")[0], 1)
            dve.wait_ge(*once("gn_root"))
            link(dve.reciprocal(rr, rr))
            link(dve.tensor_tensor(y8, y8, rr, ALU.mult))
            link(dve.tensor_tensor(y8, y8, vec(V_GW, 8, NT), ALU.mult))
            link(dve.tensor_tensor(y8, y8, vec(V_GBI, 8, NT), ALU.add))
            link(dve.tensor_tensor(y8, y8, bonus, ALU.add))
            for t in range(8):
                dve.wait_ge(S("g_ps"), t + 1)
                dve.tensor_tensor(y8[:, t, :], y8[:, t, :], pb[t % 4][:, 0:NT], ALU.mult).then_inc(S("o_rwkv"), 1)
            for t in range(KD):
                dve.wait_ge(S("out_ps"), t + 1)
                b = pb[t % 4]
                dve.scalar_tensor_tensor(out=xt[:, t, 0:NP_], in0=b[:, 0:NP_], scalar=mod[:, M_GT1, t, 0:1],
                                         in1=xt[:, t, 0:NP_], op0=ALU.mult, op1=ALU.add)
                dve.wait_ge(S("x1"), t)
                link(dve.tensor_tensor(tmp_s, b[:, NP_:NT], mod[:, M_GT1, t, 1:COND], ALU.mult))
                dve.tensor_tensor(xt[:, t, NP_:NT], xt[:, t, NP_:NT], tmp_s, ALU.add).then_inc(S("x1"), 1)
            rms_start(2)
            modulate(2, V_NFFN, M_SC2, M_SH2)
            dve.wait_ge(S("rt_consts"), 5)
            dve.wait_ge(S("g_ps"), 8)
            link(dve.memset(lg, 0.0))
            link(dve.memset(slots, -1.0))
            link(dve.memset(comb, 0.0))
            dve.wait_ge(*once("lgt_ps"))
            dve.tensor_copy(lg[:, 0:TC, :], pb[2][:, 0:TC * 36].rearrange("p (c n) -> p c n", n=36))
            link(dve.tensor_copy(lg[0:NS, TC, :], pb[2][0:NS, TC * 36:3 * 36]))
            dve.wait_ge(S("h_dve"), 2)
            link(dve.tensor_copy(h2s, ht[:, :, NP_:NT]))

            def first_max(x, n, top, one_hot):
                link(dve.tensor_reduce(top, x, axis=AX.X, op=ALU.max))
                c = pick[:, :, 0:n]
                link(dve.tensor_tensor(c, x, top.unsqueeze(2).to_broadcast([P, 3, n]), ALU.is_equal))
                link(dve.scalar_tensor_tensor(out=c, in0=c, scalar=-64.0, in1=eight[:, 0:n].unsqueeze(1).to_broadcast([P, 3, n]),
                                              op0=ALU.mult, op1=ALU.add))
                link(dve.tensor_reduce(least, c, axis=AX.X, op=ALU.min))
                link(dve.tensor_tensor(one_hot, c, least.unsqueeze(2).to_broadcast([P, 3, n]), ALU.is_equal))

            first_max(lg[:, :, 0:NG], NG, top_g, oh_g)
            dve.tensor_tensor(g_exp, lg[:, :, 0:NG], top_g.unsqueeze(2).to_broadcast([P, 3, NG]), ALU.subtract)\
                .then_inc(once("rt_d1")[0], 1)
            le4 = lg[:, :, NG:].rearrange("p c (g e) -> p c g e", e=NE)
            by_g = oh_g.unsqueeze(3).to_broadcast([P, 3, NG, NE])
            link(dve.tensor_tensor(wide, le4, by_g, ALU.mult))
            link(dve.tensor_reduce(le, wide.rearrange("p c g e -> p c e g"), axis=AX.X, op=ALU.add))
            first_max(le, NE, top_1, oh_1)
            link(dve.scalar_tensor_tensor(out=le, in0=oh_1, scalar=-1e30, in1=le, op0=ALU.mult, op1=ALU.add))
            first_max(le, NE, top_2, oh_2)
            dve.tensor_tensor(e2, top_2, top_1, ALU.subtract).then_inc(once("rt_d2")[0], 1)
            dve.wait_ge(*once("rt_e1"))
            link(dve.tensor_reduce(w_1, g_exp, axis=AX.X, op=ALU.add))
            dve.wait_ge(*once("rt_e2"))
            link(dve.scalar_tensor_tensor(out=w_1, in0=e2, scalar=1.0, in1=w_1, op0=ALU.add, op1=ALU.mult))
            link(dve.reciprocal(w_1, w_1))
            link(dve.tensor_tensor(w_2, w_1, e2, ALU.mult))
            dve.tensor_tensor(le, oh_1, w_1.unsqueeze(2).to_broadcast([P, 3, NE]), ALU.mult)
            link(dve.tensor_tensor(pick, oh_2, w_2.unsqueeze(2).to_broadcast([P, 3, NE]), ALU.mult))
            link(dve.tensor_tensor(le, le, pick, ALU.add))
            link(dve.tensor_tensor(oh_1, oh_1, oh_2, ALU.add))
            c4 = comb[:, :, 0:NEXP].rearrange("p c (g e) -> p c g e", e=NE)
            dve.tensor_tensor(c4, le.unsqueeze(2).to_broadcast([P, 3, NG, NE]), by_g, ALU.mult)
            dve.tensor_tensor(wide, oh_1.unsqueeze(2).to_broadcast([P, 3, NG, NE]), by_g, ALU.mult).then_inc(once("routed")[0], 1)
            dve.wait_ge(*once("routed"))
            dve.wait_ge(*once("rk_ps"))
            sl = slots[:, :, 0:NEXP]
            link(dve.tensor_reduce(most_f, pb[1][:, 2 * NEXP:3 * NEXP], axis=AX.X, op=ALU.max))
            dve.tensor_copy(most[:, 0:1], most_f).then_inc(once("cap_ready")[0], 1)
            link(dve.scalar_tensor_tensor(out=sl, in0=pb[1][:, 0:2 * NEXP].rearrange("p (c e) -> p c e", e=NEXP),
                                          scalar=float(NS + 1), in1=wide.rearrange("p c g e -> p c (g e)")[:, 0:TC],
                                          op0=ALU.add, op1=ALU.mult))
            link(dve.tensor_scalar(sl, sl, -1.0, None, ALU.add))
            dve.wait_ge(S("h2t_ps"), 8)
            dve.wait_ge(*once("lg_ps"))
            dve.wait_ge(S("h_act"), 2 * (KD - 8))
            link(dve.memset(ht, 0.0))

            def moe_dispatch(n, t):
                dve.wait_ge(S("m_ga"), n * 4)
                for q in range(2):
                    for c in range(TC):
                        last = dve.tensor_scalar(disp[:, c, q * SLOT:(q + 1) * SLOT], slot_no[:, 0, :],
                                                 slots[:, c, bass.ds(t * 2 + q, 1)], None, ALU.is_equal)
                last.then_inc(S("m_dp"), 1)

            def moe_gather_out(n):
                for b in range(2, 4):
                    dve.wait_ge(S("m_ga"), n * 4 + (b + 1))
                    last = dve.tensor_copy(xg[:, :, 4 * b:4 * b + 4, :],
                                           pb[b][:].rearrange("p (k q s) -> p q k s", q=2, s=SLOT))
                last.then_inc(S("m_ga_d"), 1)
                dve.wait_ge(S("m_ga_a"), (n + 1) * 2)
                dve.wait_ge(S("m_ga_d"), n + 1)
                dve.tensor_copy(xg[:, :, :, 0:NS], h2s.unsqueeze(1).to_broadcast([P, 2, KD, NS])).then_inc(S("m_xg"), 1)

            def moe_add(q, n):
                for i in range(KD):
                    k = (i % 2) * 8 + i // 2
                    dve.wait_ge(S(f"m_sc{q}"), n * KD + (i + 1))
                    dve.tensor_tensor(ht[:, k, :], ht[:, k, :], pb[i % 4][:, 0:NT], ALU.add)\
                        .then_inc(S(f"m_add{q}"), 1)

            def moe_dve(ps):
                if not isinstance(ps, int):
                    dve.tensor_scalar(sl, sl, -float(CAP), None, ALU.add)
                    dve.memset(own_w, 0.0).then_inc(S("m_next"), 1)
                    dve.wait_ge(S("m_next"), ps)
                dve.wait_ge(S("m_sc1"), ps * (17 * KD))
                dve.memset(pwt[:, 1, :], 0.0)
                dve.memset(y_slot[:, 1, :], 0.0).then_inc(S("m_zero"), 1)
                moe_dispatch(ps * 17, 0)
                moe_gather_out(ps * 17)
                with dve.Fori(0, NEXP // 2) as i:
                    t = ps * 16 + i
                    for q in range(2):
                        dve.wait_ge(S(f"m_wt{q}"), t)
                        for c in range(TC):
                            dve.tensor_scalar(pw[:, q, c, :], slot_no.rearrange("p a s -> p (a s)"),
                                              slots[:, c, bass.ds(i * 2 + q, 1)], comb[:, c, bass.ds(i * 2 + q, 1)],
                                              ALU.is_equal, ALU.mult)
                        dve.tensor_scalar(pw[0:NS, q, TC, :], own_slot.rearrange("p a s -> p (a s)"),
                                          comb[0:NS, TC, bass.ds(i * 2 + q, 1)], None, ALU.mult)\
                            .then_inc(S(f"m_pw{q}"), 1)
                    moe_dispatch(ps * 17 + i + 1, i + 1)
                    for q in range(2):
                        dve.wait_ge(S(f"m_sg{q}"), t + 1)
                        dve.wait_ge(S("m_free"), (t * 2 + q) * MOE_SLOTS + 4)
                        dve.tensor_tensor(sg[:, q, :], sg[:, q, :], pb[4 + q][:, 256:512], ALU.mult)\
                            .then_inc(S(f"m_hid{q}"), 1)
                        moe_add(1 - q, ps * (17 if q == 0 else 16) + i)
                        if q == 1:
                            moe_gather_out(ps * 17 + i + 1)
                moe_add(1, ps * 17 + 16)
                dve.wait_ge(S("m_add1"), ps * (17 * KD) + 17 * KD)

            moe_dve(0)
            dve.wait_ge(*once("cap_ready"))
            count = dve.value_load(most[0:1, 0:1], min_val=0, max_val=NP_)
            with dve.If(count > CAP):
                with dve.Fori(1, PASSES) as ps:
                    moe_dve(ps)
            for k in range(KD):
                dve.scalar_tensor_tensor(out=xt[:, k, 0:NP_], in0=ht[:, k, 0:NP_], scalar=mod[:, M_GT2, k, 0:1],
                                         in1=xt[:, k, 0:NP_], op0=ALU.mult, op1=ALU.add)
            link(dve.tensor_tensor(ht[:, :, NP_:NT], ht[:, :, NP_:NT], mod[:, M_GT2, :, 1:COND], ALU.mult))
            dve.tensor_tensor(xt[:, :, NP_:NT], xt[:, :, NP_:NT], ht[:, :, NP_:NT], ALU.add).then_inc(S("x2"), 1)
            rms_start(3)
            modulate(3, V_NFIN, M_SCF, M_SHF)
            for b in range(1, 12, 2):
                dve.wait_ge(S("yo_ps"), b + 1)
                dst = (y_tok[:, b // 4, (b % 4) * BANK:(b % 4 + 1) * BANK] if b < 8 else
                       ys_tok[:, (b - 8) * BANK:(b - 7) * BANK])
                dve.wait_ge(S("yo_evac"), b)
                dve.tensor_copy(dst, pb[1 + b % 4][0:dst.shape[0], :]).then_inc(S("yo_evac"), 1)

        @block.tensor
        def _(pe):
            pe.wait_ge(S("consts"), N_CONSTS)
            pe.wait_ge(*once("c_silu"))
            for k in range(KD):
                last = pe.transpose(pb[0][:, k * CPAD:(k + 1) * CPAD], c_row[:, k * P:(k + 1) * P], ident[0:CPAD, 0:CPAD])
            last.then_inc(once("cT_ps")[0], 1)
            pe.wait_ge(S("vec_in"), 16 * N_VEC)
            for g, (at, n) in enumerate(((V_ADA, 128), (V_NMIX, 80), (V_W0, 56))):
                last = pe.transpose(pb[1][:, at:at + n], vec_rows[0:n, g, :], ident[0:n, 0:n])
            last.then_inc(once("vec_ps")[0], 1)
            pe.wait_ge(S("x_in"), 32)
            for k in range(KD):
                if k >= 4:
                    pe.wait_ge(S("xT_evac"), k - 3)
                bank = pb[2 + k % 4]
                for c in range(TC):
                    pe.transpose(bank[:, c * P:(c + 1) * P], x_tok[:, c, k * P:(k + 1) * P], ident[:])
                pe.transpose(bank[:, NP_:NT], x_row[:, k * P:(k + 1) * P], ident[0:NS, 0:NS]).then_inc(S("xT_ps"), 1)

            def sum_squares(n):
                pe.wait_ge(S("norm_sq"), n)
                for k in range(KD):
                    last = pe.matmul(pb[0][:, 0:NT], ones[:], ht[:, k, :], start=(k == 0), stop=(k == KD - 1))
                last.then_inc(S("ms_ps"), 1)

            pe.wait_ge(*once("cT_ready"))
            sum_squares(1)

            def ada_piece(sec, i):
                if i == 0:
                    pe.wait_ge(S("ada_evac"), sec)
                if isinstance(sec, int) and sec < 2:
                    s, full, free = i % 4, "ring_full", "ring_free"
                    pe.wait_ge(S(f"ring_full{s}"), (2 * sec + i // 4 + 1) * 16)
                else:
                    s, full, free = i % 2, "r2_full", "r2_free"
                    pe.wait_ge(S(f"r2_full{s}"), (sec - 2) * 64 + (i // 2 + 1) * 16)
                w = slot(s).rearrange("p (k c) -> p k c", c=D)
                for j in range(2):
                    k = 2 * i + j
                    for g in range(4):
                        last = pe.matmul(pb[7][g * CPAD:(g + 1) * CPAD, :], ct[:, k, :],
                                         w[:, j, g * BANK:(g + 1) * BANK], start=(k == 0), stop=(k == KD - 1))
                last.then_inc(S(free), 1)

            def ada_turn(sec):
                pe.wait_ge(S("ada_evac"), sec + 1)
                pe.wait_ge(S("ada_mod"), sec)
                for j in range(4):
                    last = pe.transpose(pb[6][:, j * P:(j + 1) * P], ada_row[:, j * P:(j + 1) * P], ident[:])
                last.then_inc(S("ada_tr"), 1)

            for sec in (M_SH1, M_SC1):
                for i in range(8):
                    ada_piece(sec, i)
                ada_turn(sec)
            pe.wait_ge(S("h_dve"), 1)
            pe.wait_ge(S("h_act"), 1 * (KD - 8))
            with pe.Fori(0, 6) as g:
                for s in range(4):
                    pe.wait_ge(S(f"ring_full{s}"), (g + IN_ROUND + 1) * 16)
                    w = slot(s).rearrange("p (k c) -> p k c", c=256)
                    for m in range(2):
                        t = 2 * s + m
                        if t >= 4:
                            pe.wait_ge(S("in_evac_d" if t % 2 else "in_evac_a"), g * 4 + (t - 4) // 2 + 1)
                        else:
                            pe.wait_ge(S("in_evac_d" if t % 2 else "in_evac_a"), g * 4)
                        for k in range(KD):
                            last = pe.matmul(pb[t % 4][:, 0:NT], w[:, k, m * P:(m + 1) * P], ht[:, k, :],
                                             start=(k == 0), stop=(k == KD - 1))
                        last.then_inc(S("ring_free" if m else "in_ps"), 1)
            pe.wait_ge(S("small_w_in"), 64)
            pe.wait_ge(S("in_evac_a"), 24)
            pe.wait_ge(S("in_evac_d"), 24)
            for i, (at, n) in enumerate(((0, P), (P, P), (2 * P, GATE_RANK))):
                for k in range(KD):
                    last = pe.matmul(pb[i][0:n, 0:NT], small_w[:, k, at:at + n], ht[:, k, :],
                                     start=(k == 0), stop=(k == KD - 1))
                last.then_inc(S("in_small"), 1)
            for b in range(7):
                if b >= 2:
                    pe.wait_ge(S("so_evac"), b - 1)
                if b == 0:
                    pe.wait_ge(*once("in_small_a"))
                    pe.wait_ge(S("in_small_d"), 1)
                for j in range(4 if b < 6 else 2):
                    last = pe.transpose(pb[3 + b % 2][0:COND, j * P:(j + 1) * P], pj[:, TR + 4 * b + j, NP_ - 1:NT],
                                        ident[:])
                last.then_inc(S("so_ps"), 1)
            pe.wait_ge(S("shift_in"), 16 * len(SHIFT_PARTS))
            for t in range(26):
                last = pe.transpose(pb[5][:, t * NS:(t + 1) * NS], shift_row[:, t * P:(t + 1) * P], ident[0:NS, 0:NS])
            last.then_inc(once("shs_ps")[0], 1)
            pe.wait_ge(S("in_small_d"), 2)
            pe.wait_ge(S("so_evac"), 7)
            for c in range(TC):
                for t in range(8):
                    last = pe.transpose(pb[2 * c + t // 4][:, (t % 4) * P:(t % 4 + 1) * P],
                                        pj[:, TV + t, c * P:(c + 1) * P], ident[:])
                    if t % 4 == 3:
                        last.then_inc(S("vt_ps"), 1)
            pe.wait_ge(*once("shs_ready"))
            for t in range(8):
                last = pe.transpose(pb[4 + t // 4][0:NS, (t % 4) * P:(t % 4 + 1) * P], pj[:, TV + t, NP_:NT], ident[:])
            last.then_inc(once("vs_ps")[0], 1)
            pe.wait_ge(S("vt_evac"), 1)
            for t in range(4):
                last = pe.transpose(pb[0][0:NS, t * P:(t + 1) * P], pj[:, TK + t, NP_:NT], ident[:])
            last.then_inc(once("ks_ps")[0], 1)
            pe.wait_ge(S("gate_w_in"), 16)
            pe.wait_ge(*once("ks_evac"))
            pe.wait_ge(S("vt_evac"), 4)
            for h in range(GLA_H):
                last = pe.matmul(pb[h][:, 0:NT], gw2[:, h * GLA_DK:(h + 1) * GLA_DK], pj[0:GATE_RANK, TGL, :],
                                 start=True, stop=True)
            last.then_inc(once("gz_ps")[0], 1)
            pe.wait_ge(*once("g_z"))
            for l in range(LEVELS + 1):
                if l < LEVELS:
                    pe.wait_ge(S("lv_qk"), l + 1)
                if l >= 2:
                    pe.wait_ge(S("lv_sel"), l - 1)
                q, k = (q4, k4) if l < LEVELS else (pj[:, TQ:TQ + 4, :], pj[:, TK:TK + 4, :])
                for i in range(1 if l == 0 else 2):
                    for h in range(GLA_H):
                        ks, qs = (0, 1) if l == 0 else (i, i)
                        last = pe.matmul(pb[2 * (l % 2) + i][:, h * P:(h + 1) * P], k[:, h, ks * P:(ks + 1) * P],
                                         q[:, h, qs * P:(qs + 1) * P], start=True, stop=True)
                last.then_inc(S("lv_ps"), 1)
                if l < LEVELS:
                    ada_piece(2, l)
            pe.wait_ge(*once("kd"))
            pe.wait_ge(*once("vs_evac"))
            for c in range(TC):
                for h in range(GLA_H):
                    last = pe.transpose(pb[4 + c][:, h * P:(h + 1) * P], k4[:, h, c * P:(c + 1) * P], ident[:])
            last.then_inc(once("kd_ps")[0], 1)
            ada_turn(2)
            pe.wait_ge(S("lv_sel"), LEVELS + 1)
            for t in range(8):
                h, b = t // 2, pb[t // 2]
                o = (t % 2) * NP_
                v0, v1 = (v_tok[:, c, t * P:(t + 1) * P] for c in range(TC))
                pe.matmul(b[:, o:o + P], v0, at0[:, h, 0:P], start=True, stop=True)
                pe.matmul(b[:, o + P:o + NP_], v0, at0[:, h, P:NP_], start=True, stop=False)
                last = pe.matmul(b[:, o + P:o + NP_], v1, at1[:, h, :], start=False, stop=True)
                if t % 2:
                    last.then_inc(S("go_ps"), 1)
            pe.wait_ge(*once("kd_evac"))
            for h in range(GLA_H):
                for c in range(TC):
                    last = pe.matmul(pb[4 + h // 2][:, (h % 2) * GLA_DV:(h % 2 + 1) * GLA_DV],
                                     kd_tok[:, c, h * GLA_DK:(h + 1) * GLA_DK], v_tok[:, c, h * GLA_DV:(h + 1) * GLA_DV],
                                     start=(c == 0), stop=(c == TC - 1))
            last.then_inc(once("gst_ps")[0], 1)
            pe.wait_ge(*once("gst_evac"))
            for h in range(GLA_H):
                pe.wait_ge(S("kz"), h + 1)
                if h == 0:
                    pe.wait_ge(S("go_evac"), 4)
                else:
                    pe.wait_ge(S("gs_s"), h)
                for b in range(NS):
                    last = pe.matmul(pb[b // 2][:, (b % 2) * GLA_DV:(b % 2 + 1) * GLA_DV], kz[:, b, :],
                                     v_row[:, h * GLA_DV:(h + 1) * GLA_DV], start=True, stop=True)
                    if b % 2:
                        last.then_inc(S("gs_kv"), 1)
                ada_piece(3, 2 * h)
                ada_piece(3, 2 * h + 1)
            pe.wait_ge(S("gs_s"), GLA_H)
            for a in range(2):
                for h in range(GLA_H):
                    for g in range(4):
                        b = 4 * a + g
                        last = pe.matmul(pb[2 * a + h // 2][g * CPAD:(g + 1) * CPAD, (h % 2) * GLA_DV:(h % 2 + 1) * GLA_DV],
                                         pj[:, TQ + h, NP_ + b - CPAD + 1:NP_ + b + 1], gs[h][:, b, :],
                                         start=True, stop=True)
            last.then_inc(once("gs_o")[0], 1)
            ada_turn(3)
            pe.wait_ge(*once("or_evac"))
            for a in range(2):
                for t in range(8):
                    last = pe.transpose(pb[2 * a + t // 4][:, (t % 4) * P:(t % 4 + 1) * P],
                                        o_rows[:, a, t * P:(t + 1) * P], ident[:])
            last.then_inc(once("os_ps")[0], 1)
            pe.wait_ge(*once("gos_evac"))
            pe.wait_ge(*once("gla_sq"))
            for h in range(GLA_H):
                for e in range(2):
                    last = pe.matmul(pb[h][:, 0:NT], ones[:], gla_sq[:, 2 * h + e, :], start=(e == 0), stop=(e == 1))
            last.then_inc(once("gn_ps")[0], 1)
            pe.wait_ge(S("low_rank_in"), 32)
            pe.wait_ge(*once("gates_act"))
            pe.wait_ge(*once("gla_ms"))
            for i in range(16):
                r = slice(RD * (i // 8), RD * (i // 8) + RD)
                if i >= 4:
                    pe.wait_ge(S("rs_evac"), i - 3)
                pe.matmul(pb[i % 4][:, 0:NT], wa2[r, (i % 8) * P:(i % 8 + 1) * P], pj[r, TWA, :], start=True, stop=True)\
                    .then_inc(S("rs_ps"), 1)

            def head_sums(src, ps_sem, free_sem, base=0, banks=(0, 1, 2, 3)):
                n = len(banks)
                for t in range(8):
                    if t >= n:
                        pe.wait_ge(S(free_sem), base + t - n + 1)
                    pe.matmul(pb[banks[t % n]][:, 0:NT], bones[:], src[:, t, :], start=True, stop=True)\
                        .then_inc(S(ps_sem), 1)

            pe.wait_ge(*once("kk_sq"))
            pe.wait_ge(S("rs_evac"), 16)
            head_sums(t2, "kn_ps", "kn_evac")
            pe.wait_ge(*once("bonus_in"))
            pe.wait_ge(S("kn_evac"), 8)
            head_sums(t1, "bonus_ps", "bonus_evac", banks=(2, 3))
            pe.wait_ge(*once("sv_rest"))
            pe.wait_ge(*once("sv_w"))
            for t in range(8):
                last = pe.transpose(pb[t // 4][0:48, (t % 4) * P:(t % 4 + 1) * P],
                                    sv[:, t].rearrange("p v b -> p (v b)"), ident[:])
            last.then_inc(once("sv_ps")[0], 1)
            pe.wait_ge(*once("sv_evac"))
            pe.wait_ge(S("bonus_evac"), 8)
            def four(bank, lhs, rhs, start=True, stop=True):
                for j in range(4):
                    last = pe.matmul(pb[bank][:, j * P:(j + 1) * P], lhs[:, j, :], rhs[:, j, :], start=start, stop=stop)
                return last

            def turn(bank, x):
                for j in range(4):
                    last = pe.transpose(pb[bank][:, j * P:(j + 1) * P], x[:, j, :], ident[:])
                return last

            def twice(x):
                return x.unsqueeze(1).to_broadcast([P, 2, CH])

            with pe.Fori(0, NCH) as c:
                for hf in range(2):
                    n = c * 2 + hf
                    pe.wait_ge(S("ck_pad_d"), n + 1)
                    pe.wait_ge(S("ck_pad_a"), n + 1)
                    pe.wait_ge(S("ck_s"), c * 2)
                    pe.wait_ge(S("ck_yev"), c * 2)
                    if hf == 0:
                        pe.wait_ge(S("ada_mod"), c + 4)
                    else:
                        pe.wait_ge(S("ck_m"), n)
                    for i, x in enumerate((bp, kp)):
                        for j in range(4):
                            last = pe.matmul(pb[G_BANKS[hf][2 * i + j // 2]][:, (j % 2) * 192:(j % 2 + 1) * 192],
                                             x[hf][:, j, :], ar[hf][:, j, :], start=True, stop=True)
                    last.then_inc(S("ck_g"), 1)
                    ada_piece(c + 4, hf)
                for hf in range(2):
                    pe.wait_ge(S("ck_m"), c * 2 + (hf + 1))
                    for i, x in enumerate((bp, kp, vp)):
                        last = turn(3 * hf + i, x[hf])
                    last.then_inc(S("ck_t1"), 1)
                for hf in range(2):
                    n = c * 2 + hf
                    pe.wait_ge(S("ck_tt0"), n + 1)
                    pe.wait_ge(S("ck_t1e"), n + 1)
                    turn(3 * hf, tt[hf]).then_inc(S("ck_t0"), 1)
                    for j in range(4):
                        o = pb[3 * hf + 1][:, j * P:(j + 1) * P]
                        pe.matmul(o, ar[hf][:, j, 0:P], st[:, 4 * hf + j, :], start=True, stop=False)
                        last = pe.matmul(o, mtm[hf][:, j, :], vp[hf][:, j, :], start=False, stop=True)
                    last.then_inc(S("ck_u"), 1)
                for l in range(1, 6):
                    for hf in range(2):
                        if l == 1:
                            pe.wait_ge(S("ck_t0e"), c * 2 + (hf + 1))
                            pe.wait_ge(S("ck_ue"), c * 2 + (hf + 1))
                        else:
                            pe.wait_ge(S("iv_tn"), c * 10 + (2 * l - 3 + hf))
                        pe.wait_ge(S("iv_lo"), c * 10 + (2 * l - 1 + hf))
                        four(3 * hf + 2, lo[hf], tm[hf]).then_inc(S("iv_p"), 1)
                    ada_piece(c + 4, 1 + l)
                    for hf in range(2):
                        pe.wait_ge(S("iv_pe"), c * 10 + (2 * l - 1 + hf))
                        last = four(3 * hf, pm[hf], tt[hf])
                        if l < 5:
                            last = four(3 * hf + 1, tt[hf], pm[hf])
                        last.then_inc(S("iv_t"), 1)
                ada_piece(c + 4, 7)
                for hf in range(2):
                    pe.wait_ge(S("iv_tn"), c * 10 + (9 + hf))
                    four(3 * hf + 2, tt[hf], um[hf]).then_inc(S("ck_sa"), 1)
                for hf in range(2):
                    pe.wait_ge(S("ck_sae"), c * 2 + (hf + 1))
                    for j in range(4):
                        o = pb[3 * hf][:, j * P:(j + 1) * P]
                        pe.matmul(o, st[:, 4 * hf + j, :], twice(ar[hf][:, j, P:192]), start=True, stop=False)
                        pe.matmul(o, tm[hf][:, j, :], twice(rbm[hf][:, j, :]), start=False, stop=False)
                        pe.matmul(o, vp[hf][:, j, :], twice(rkm[hf][:, j, :]), start=False, stop=True)
                        o = pb[3 * hf + 1][:, j * P:(j + 1) * P]
                        pe.matmul(o, bp[hf][:, j, :], tm[hf][:, j, :], start=True, stop=False)
                        last = pe.matmul(o, kp[hf][:, j, :], vp[hf][:, j, :], start=False, stop=True)
                    last.then_inc(S("ck_y"), 1)
                ada_turn(c + 4)
            pe.wait_ge(S("ck_s"), 2 * NCH)
            pe.wait_ge(S("ck_yev"), 2 * NCH)
            for t in range(8):
                last = pe.transpose(pb[t // 4][:, (t % 4) * P:(t % 4 + 1) * P], st[:, t, :], ident[:])
            last.then_inc(once("sr_ps")[0], 1)
            pe.wait_ge(S("ys_row"), RD // SI)
            pe.transpose(pb[2][0:RD, 0:P], y_row, ident[:]).then_inc(once("ys_ps")[0], 1)
            pe.wait_ge(*once("sr_evac"))
            pe.wait_ge(*once("y_all"))
            head_sums(y8, "mu_ps", "mu_evac")
            pe.wait_ge(*once("gn_sq"))
            head_sums(ra, "var_ps", "var_evac")
            pe.wait_ge(S("g2_in"), 16)
            for t in range(8):
                pe.wait_ge(S("var_evac"), min(8, t + 5))
                if t >= 4:
                    pe.wait_ge(S("o_rwkv"), t - 3)
                pe.matmul(pb[t % 4][:, 0:NT], g2[:, t * P:(t + 1) * P], pj[:, TG7, :], start=True, stop=True)\
                    .then_inc(S("g_ps"), 1)
            pe.wait_ge(S("o_rwkv"), 8)
            for t in range(KD):
                i = t // 2
                s = i % 4
                pe.wait_ge(S(f"wo_full{s}"), 16 * (i // 4 + 1))
                if t >= 4:
                    pe.wait_ge(S("x1"), t - 3)
                w = slot(s).rearrange("p (k c) -> p k c", c=256)
                for k in range(KD):
                    last = pe.matmul(pb[t % 4][:, 0:NT], w[:, k, (t % 2) * P:(t % 2 + 1) * P], ht[:, k, :],
                                     start=(k == 0), stop=(k == KD - 1))
                last.then_inc(S("out_ps"), 1)
            pe.wait_ge(S("x1"), KD)
            sum_squares(2)
            pe.wait_ge(S("rt_in"), 32)
            pe.wait_ge(S("h_dve"), 2)
            pe.wait_ge(S("h_act"), 2 * (KD - 8))
            for k in range(KD):
                last = pe.matmul(pb[1][0:NG + NEXP, 0:NT], w_rt[:, k, :], ht[:, k, :], start=(k == 0), stop=(k == KD - 1))
            last.then_inc(once("lg_ps")[0], 1)
            for b in range(8):
                if b >= 4:
                    pe.wait_ge(S("h2t_evac"), b - 3)
                if b == 1:
                    pe.wait_ge(*once("lg_evac"))
                    for c in range(3):
                        m = P if c < TC else NS
                        last = pe.transpose(pb[2][0:m, c * 36:(c + 1) * 36], lg_t[:, c * P:c * P + m], ident[0:36, 0:36])
                    last.then_inc(once("lgt_ps")[0], 1)
                for j in range(4):
                    k = 4 * (b % 4) + j
                    last = pe.transpose(pb[3 + b % 4][:, j * P:(j + 1) * P], ht[:, k, (b // 4) * P:(b // 4 + 1) * P],
                                        ident[:])
                last.then_inc(S("h2t_ps"), 1)
            pe.wait_ge(*once("routed"))
            m = [wide[:, c].rearrange("p g e -> p (g e)") for c in range(TC)]
            pe.matmul(pb[1][:, 0:NEXP], mstrict[:], m[0], start=True, stop=True)
            pe.matmul(pb[1][:, NEXP:2 * NEXP], ones[:], m[0], start=True, stop=False)
            pe.matmul(pb[1][:, NEXP:2 * NEXP], mstrict[:], m[1], start=False, stop=True)
            pe.matmul(pb[1][:, 2 * NEXP:3 * NEXP], ones[:], m[0], start=True, stop=False)
            pe.matmul(pb[1][:, 2 * NEXP:3 * NEXP], ones[:], m[1], start=False, stop=True).then_inc(once("rk_ps")[0], 1)
            pe.wait_ge(S("h2t_evac"), 8)
            pe.wait_ge(*once("cap_ready"))

            def moe_gather(n):
                pe.wait_ge(S("m_dp"), n + 1)
                for b in range(4):
                    for j in range(4):
                        k = 4 * b + j
                        for c in range(TC):
                            last = pe.matmul(pb[b][:, j * P:(j + 1) * P], h_tok[:, c, k * P:(k + 1) * P], disp[:, c, :],
                                             start=(c == 0), stop=(c == TC - 1))
                    last.then_inc(S("m_ga"), 1)

            def moe_scatter(q, n):
                for i in range(KD):
                    k = (i % 2) * 8 + i // 2
                    r = slice(SLOT * (i % 2), SLOT * (i % 2) + SLOT)
                    if i >= 4:
                        pe.wait_ge(S(f"m_add{q}"), n * KD + (i - 3))
                    pe.matmul(pb[i % 4][:, 0:NT], y_slot[r, q, (k % 8) * P:(k % 8 + 1) * P], pwt[r, q, :],
                              start=True, stop=True).then_inc(S(f"m_sc{q}"), 1)

            def moe_pe(ps):
                pe.wait_ge(S("m_zero"), ps + 1)
                pe.wait_ge(S("m_add1"), ps * (17 * KD))
                moe_gather(ps * 17)
                with pe.Fori(0, NEXP // 2) as i:
                    t = ps * 16 + i
                    for q in range(2):
                        pe.wait_ge(S(f"m_pw{q}"), t + 1)
                        bank = pb[5 - q]
                        pe.wait_ge(S(f"m_ht{1 - q}"), t + q)
                        for c in range(3):
                            m = P if c < TC else NS
                            last = pe.transpose(bank[:, c * P:c * P + m], pw[0:m, q, c, :], ident[0:m, 0:m])
                        last.then_inc(S(f"m_wt{q}"), 1)
                        if q == 0:
                            pe.wait_ge(S("m_wte1"), t)
                            pe.wait_ge(S("m_xg"), ps * 17 + i + 1)
                        else:
                            pe.wait_ge(S("m_wte0"), t + 1)
                        for s in range(4):
                            pe.wait_ge(S(f"m_full{s}"), (t * 2 + q + 1) * 16)
                            w = slot(s).rearrange("p (k f) -> p k f", f=FF)
                            o = (s // 2) * 256
                            for j in range(8):
                                k = (s % 2) * 8 + j
                                for h in range(2):
                                    last = pe.matmul(pb[4 + q][SLOT * h:SLOT * h + SLOT, o:o + 256], xg[:, q, k, :],
                                                     w[:, j, h * 256:(h + 1) * 256], start=(k == 0), stop=(k == KD - 1))
                            last.then_inc(S("m_free"), 1)
                        if q == 0:
                            pe.wait_ge(S("m_ye1"), t)
                            moe_scatter(1, ps * 17 + i)
                        else:
                            pe.wait_ge(S("m_ye0"), t + 1)
                            pe.wait_ge(S("m_add1"), ps * (17 * KD) + (i + 1) * KD)
                            moe_scatter(0, t)
                            pe.wait_ge(S("m_add0"), (t + 1) * KD)
                            moe_gather(ps * 17 + i + 1)
                        pe.wait_ge(S(f"m_hid{q}"), t + 1)
                        for j in range(2):
                            last = pe.transpose(pb[4 + q][:, j * P:(j + 1) * P], sg[:, q, j * P:(j + 1) * P], ident[:])
                        last.then_inc(S(f"m_hp{q}"), 1)
                        pe.wait_ge(S(f"m_ht{q}"), t + 1)
                        pe.wait_ge(S(f"m_ye{1 - q}"), t + q)
                        for s in range(4, MOE_SLOTS):
                            pe.wait_ge(S(f"m_full{s}"), (t * 2 + q + 1) * 16)
                            w = slot(s).rearrange("p (k f) -> p k f", f=D)
                            for j in range(2):
                                fc = (s - 4) * 2 + j
                                x = hid_t[:, q, (fc % 2) * P + (fc // 2) * SLOT:(fc % 2) * P + (fc // 2 + 1) * SLOT]
                                for n in range(2):
                                    for h in range(2):
                                        at = h * 1024 + n * BANK
                                        last = pe.matmul(pb[6 + n][SLOT * h:SLOT * h + SLOT, :], x, w[:, j, at:at + BANK],
                                                         start=(fc == 0), stop=(fc == 3))
                            last.then_inc(S("m_free"), 1)
                pe.wait_ge(S("m_ye1"), ps * 16 + 16)
                pe.wait_ge(S("m_xg"), ps * 17 + 17)
                moe_scatter(1, ps * 17 + 16)

            moe_pe(0)
            count = pe.value_load(most[0:1, 0:1], min_val=0, max_val=NP_)
            with pe.If(count > CAP):
                with pe.Fori(1, PASSES) as ps:
                    moe_pe(ps)
            pe.wait_ge(S("x2"), 1)
            sum_squares(3)
            pe.wait_ge(S("h_dve"), 3)
            pe.wait_ge(S("h_act"), 3 * (KD - 8))
            for b in range(12):
                if b >= 4:
                    pe.wait_ge(S("yo_evac"), b - 3)
                m = P if b < 8 else NS
                at = (b // 4) * P
                for j in range(4):
                    k = 4 * (b % 4) + j
                    last = pe.transpose(pb[1 + b % 4][0:m, j * P:(j + 1) * P], ht[:, k, at:at + m], ident[:])
                last.then_inc(S("yo_ps"), 1)


N_VEC = 2 + 11 + 7
N_CONSTS = 9

_OUTS = [("y_prompt", (1, NP_, D)), ("y_sample", (NS, 1, D)), ("sg_prompt", (1, 1, GLA_H, GLA_DK, GLA_DV)),
         ("sr_prompt", (1, 1, RH, RD, RD)), ("ss_prompt", (1, 1, RCOLS)), ("sg_sample", (1, NS, GLA_H, GLA_DK, GLA_DV)),
         ("sr_sample", (1, NS, RH, RD, RD)), ("ss_sample", (1, NS, RCOLS))]


def kernel(**inputs):
    import concourse.bacc as bacc
    from concourse.bass_utils import run_bass_kernel_spmd

    nc = bacc.Bacc("TRN2", target_bir_lowering=False, num_devices=1)
    arrays, args = {}, {}
    for name, value in inputs.items():
        a = np.ascontiguousarray(value)
        arrays[f"in_{name}"] = a
        args[name] = nc.dram_tensor(f"in_{name}", a.shape, mybir.dt.from_np(a.dtype), kind="ExternalInput").ap()
    for name, shape in _OUTS:
        args[name] = nc.dram_tensor(f"out_{name}", shape, F32, kind="ExternalOutput").ap()
    args["scratch"] = nc.dram_tensor("vector_scratch", (48, 1024), F32, kind="Internal").ap()
    hymba_layer(nc, **args)
    r = run_bass_kernel_spmd(nc, [arrays], core_ids=[0])
    return tuple(r.results[0][f"out_{name}"] for name, _ in _OUTS)
```

```python
from contextlib import ExitStack

import numpy as np

import concourse.bass as bass
from concourse import mybir

F32 = mybir.dt.float32
F32R = mybir.dt.float32r
I32 = mybir.dt.int32
ALU = mybir.AluOpType
ACT = mybir.ActivationFunctionType
AX = mybir.AxisListType

P = 128
D = 2048
KD = D // P
NP_ = 256
NS = 8
NT = NP_ + NS
TC = NP_ // P
COND = 1 + NS
CPAD = 32
BANK = 512
GLA_H, GLA_DK, GLA_DV = 4, 128, 256
GATE_RANK = 16
RH, RD = 16, 64
NPAIR = RH // 2
CH = 64
NCH = NP_ // CH
RCOLS = 3328
GCOLS = 3088
NG, NE, FF = 4, 8, 512
NEXP = NG * NE
SLOT = 64
CAP = SLOT - NS
PASSES = -(-NP_ // CAP)
RING = 4096
MIX_SLOTS, MOE_SLOTS = 4, 6
EPS, GLA_EPS, GN_EPS = 1e-6, 1e-5, 64e-5
HALF_E = float(np.exp(-0.5))
TQ, TK, TV, TOG, TR, TK7, TV7, TWA, TG7, TGL, NTILE = 0, 4, 8, 16, 24, 32, 40, 48, 49, 50, 51
SHIFT_PARTS = [(0, 0, 0, 1024), (8, 0, 1088, 1024), (16, 0, 2112, 1024), (24, 0, 1024, 64), (24, 64, 3136, 64),
               (25, 0, 3200, 128)]
V_ADA, V_NMIX, V_NFFN, V_NFIN, V_MU, V_GB, V_GN = 0, 128, 144, 160, 176, 202, 206
V_W0, V_A0, V_KK, V_KA, V_RK, V_GW, V_GBI, V_END = 208, 216, 224, 232, 240, 248, 256, 264
M_SH1, M_SC1, M_GT1, M_SH2, M_SC2, M_GT2, M_SHF, M_SCF = range(8)


def hymba_layer(nc, x_prompt, x_sample, state_gla, state_rwkv, state_shift, c_prompt, c_sample,
                w_ada, b_ada, norm_mix, norm_ffn, w_in, gla_gate_w2, gla_gate_b, gla_norm,
                rwkv_mu, rwkv_w0, rwkv_w2, rwkv_a0, rwkv_a2, rwkv_g2, rwkv_k_k, rwkv_k_a, rwkv_r_k,
                rwkv_gn_w, rwkv_gn_b, w_out, w_router_group, w_router_expert,
                w_exp_gate, w_exp_up, w_exp_down, norm_final, w_ada_final, b_ada_final,
                y_prompt, y_sample, sg_prompt, sr_prompt, ss_prompt, sg_sample, sr_sample, ss_sample, scratch):
    ctx = ExitStack()
    with ctx:
        sems = {}

        def S(name):
            if name not in sems:
                sems[name] = ctx.enter_context(nc.semaphore(name))
            return sems[name]

        ONCE = {
            "pe_step": (
                "cT_ps vec_ps shs_ps gl_ps vs_ps ks_ps gz_ps kd_ps gst_ps gs_o os_ps gn_ps kn_ps sv_ps "
                "sr_ps ys_ps lg_ps lgt_ps rk_ps "),
            "act_step": (
                "c_silu h_hi0 h_hi1 gl_hi vs_evac ks_evac g_ln eg kd_e kd_evac gst_evac_a gst_evac gates_act or_evac "
                "gos_evac gla_sq gla_root kk_sq kn_root rate sv_w sv_evac bonus_in sr_evac o_hi0 gn_sq gn_root o_hi1 o_hi2 lg_evac rt_e1 "
                "rt_e2 "),
            "dve_step": (
                "c_zeroed cT_ready vecs_ready shs_ready h_lo0 h_lo1 gl_lo gl_ready g_z g_log kd gla_ms "
                "gla_done kk_raw kn_inv cw kk_done rb_done sv_rest ck_zero y_all "
                "gn_c gn_ms rt_d1 rt_d2 routed cap_ready "),
        }

        def once(name):
            for sem, steps in ONCE.items():
                if name in steps.split():
                    return S(sem), steps.split().index(name) + 1
            raise KeyError(name)

        def sb(name, cols, rows=P, dt=F32):
            return ctx.enter_context(nc.sbuf_tensor(name, [rows, cols], dt))

        sizes = (("ring", (MOE_SLOTS - 1) * RING + KD * NT), ("ht", KD * NT), ("g2", 1024))
        with ExitStack() as parts:
            ring_r, ht_r, g2_r = (parts.enter_context(nc.sbuf_tensor(f"{name}_parts", [P, cols], F32R))
                                  for name, cols in sizes)
        ring, ht_flat, g2 = (sb(name, cols) for name, cols in sizes)
        ta = ring[:, MIX_SLOTS * RING:MOE_SLOTS * RING]
        tb = ring[:, 2 * RING:MIX_SLOTS * RING]
        xt = sb("xt", KD * NT)[:].rearrange("p (k n) -> p k n", n=NT)
        ht = ht_flat[:].rearrange("p (k n) -> p k n", n=NT)
        pj_flat = sb("pj", NTILE * NT)
        pj = pj_flat[:].rearrange("p (k n) -> p k n", n=NT)
        mod = sb("mod", 8 * KD * COND)[:].rearrange("p (s k n) -> p s k n", s=8, n=COND)
        vecs = sb("vecs", V_END)
        ident = sb("ident", P)
        ones = sb("ones", P)
        bones = sb("bones", P)
        ct = sb("ct", KD * CPAD)[:].rearrange("p (k n) -> p k n", n=CPAD)
        lm = sb("lm", 8 * P)[:].rearrange("p (l n) -> p l n", n=P)
        mstrict = sb("mstrict", P)
        mincl = sb("mincl", CH)
        wa2 = ht_flat[:, 2112:3136]
        gw2, kz = g2[0:GATE_RANK, 0:512], g2[0:NS, :].rearrange("p (b d) -> p b d", d=GLA_DK)
        misc = sb("misc", 1040)
        head_at = sb("head_at", 30)
        om_ka = sb("om_ka", 8)
        ada_row = sb("ada_row", BANK)
        rstd = sb("rstd", NT)[:]
        tmp_s = sb("tmp_s", NS)[:]
        gscale = sb("gscale", KD * COND)[:].rearrange("p (k n) -> p k n", n=COND)
        shs = misc[:, 0:26 * NS].rearrange("p (t n) -> p t n", n=NS)
        pb = [ctx.enter_context(nc.psum_tensor(f"pb{i}", [P, BANK], F32)) for i in range(8)]

        x_tok = ta[:, 0:TC * D].rearrange("p (c d) -> p c d", d=D)
        x_row = ta[0:NS, TC * D:TC * D + D]
        c_row = ta[0:COND, TC * D + D:TC * D + 2 * D]
        w_hi = ring_r[:, MIX_SLOTS * RING:(MIX_SLOTS + 1) * RING].rearrange("p (m k c) -> p m k c", m=2, c=P)
        ht_hi = ring_r[:, (MOE_SLOTS - 1) * RING:].rearrange("p (k n) -> p k n", n=NT)
        ht_lo = ht_r[:].rearrange("p (k n) -> p k n", n=NT)
        gl_w = g2[:, 512:768].rearrange("p (k c) -> p k c", c=GATE_RANK)
        gl_lo, gl_hi = (g2_r[:, at:at + 256].rearrange("p (k c) -> p k c", c=GATE_RANK) for at in (512, 768))
        shift_row = pj_flat[0:NS, 1280:1280 + RCOLS]
        vec_rows = pj_flat[:, 0:3 * P].rearrange("p (g c) -> p g c", c=P)
        idx_f = pj_flat[:, 512:640].bitcast(I32)
        idx_p = pj_flat[:, 640:768].bitcast(I32)
        idx_x = pj_flat[:, 768:896].bitcast(I32)
        xor_f = pj_flat[:, 896:1024]
        tri_f = pj_flat[:, 1024:1152]
        ge_f = pj_flat[:, 1152:1280]

        dl = tb[:, 0:26 * NT].rearrange("p (t n) -> p t n", n=NT)
        shift_out = ht_flat[0:COND, 0:RCOLS]
        cum = ta[:, 0:1024]
        cum4 = cum.rearrange("p (h n) -> p h n", n=NP_)
        e_flat = ta[:, 1024:2048]
        z4 = ta[:, 1024:2080].rearrange("p (h n) -> p h n", n=NT)
        l4 = ta[:, 2080:3136].rearrange("p (h n) -> p h n", n=NT)
        q4 = ta[:, 2080:3104].rearrange("p (h n) -> p h n", n=NP_)
        k4 = ta[:, 3104:4128].rearrange("p (h n) -> p h n", n=NP_)
        kd_tok = ta[:, 2080:3104].rearrange("p (c d) -> p c d", d=GLA_H * GLA_DK)
        v_tok = ta[:, 4128:6176].rearrange("p (c d) -> p c d", d=GLA_H * GLA_DV)
        at0 = ta[:, 6176:7200].rearrange("p (h n) -> p h n", n=NP_)
        at1 = ta[:, 7200:7712].rearrange("p (h n) -> p h n", n=P)
        sg_new = ta[:, 0:1024].rearrange("p (h e) -> p h e", e=GLA_DV)
        k_row, v_row = ht_flat[0:NS, 3648:4160], misc[0:NS, 0:1024]
        eg = rstd[:, 0:GLA_H * NS]
        gs = [tb[:, i * 2048:(i + 1) * 2048].rearrange("p (b e) -> p b e", e=GLA_DV) for i in range(GLA_H)]
        o_rows = ta[:, 2080:4128].rearrange("p (a f) -> p a f", a=2)
        gla_sq = ta[:, 5152:7264].rearrange("p (t n) -> p t n", n=NT)
        gla_r = pj[:, TQ:TQ + GLA_H, :]
        o_gla = ht[:, 0:8, :]
        W8 = NPAIR * NT

        def tiles8(flat):
            return flat.rearrange("p (t n) -> p t n", n=NT)

        ra, rb, bonus = (tiles8(pj_flat[:, i * W8:(i + 1) * W8]) for i in range(3))
        t0, t1, t2 = (tiles8(ta[:, i * W8:(i + 1) * W8]) for i in range(3))
        rr, rk, rv = pj[:, TR:TR + 8, :], pj[:, TK7:TK7 + 8, :], pj[:, TV7:TV7 + 8, :]
        sv = misc[:, 0:384].rearrange("p (t v b) -> p t v b", v=6, b=NS)
        svt = misc[:, 384:768].rearrange("p (v d) -> p v d", d=RD)
        sv_row = ht_flat[0:48, 2112:3136]
        wc = misc[:, 768:800].rearrange("p (t c) -> p t c", c=NCH)
        y8 = ht[:, 8:16, :]
        ar = [x[:, 0:768].rearrange("p (j n) -> p j n", n=192) for x in (ta, tb)]
        bufs = [[x[:, 768 + i * 512:768 + (i + 1) * 512].rearrange("p (j n) -> p j n", n=P) for x in (ta, tb)]
                for i in range(10)]
        bp, kp, vp, ltm, mtm, lo, tm, tt, pm, um = bufs
        rbm = [x[:, 5888:6144].rearrange("p (j n) -> p j n", n=CH) for x in (ta, tb)]
        rkm = [x[:, 6144:6400].rearrange("p (j n) -> p j n", n=CH) for x in (ta, tb)]
        st = ta[:, 6400:7424].rearrange("p (t n) -> p t n", n=P)
        keep = rstd[:, 0:NP_]
        spread_to = g2[0:RH, :]
        kn = ht_flat[0:RH, 3136:3136 + NT]
        sr_new = pj_flat[:, W8:W8 + 1024].rearrange("p (t n) -> p t n", n=P)
        SI = 8
        rs = [tb[:, 6400 + i * 512:6912 + i * 512].rearrange("p (i j) -> p i j", j=RD) for i in range(2)]
        rt = tb[:, 7424:7936].rearrange("p (i j) -> p i j", j=RD)
        sa_row, y_row = misc[:, 800:808], misc[:, 864:928]

        at = [0]

        def room(cols):
            at[0] += cols
            return pj_flat[:, at[0] - cols:at[0]]

        w_rt = room(KD * 36).rearrange("p (k c) -> p k c", c=NG + NEXP)
        lg_t = room(NT)[0:NG + NEXP]
        lg = room(3 * 36).rearrange("p (c n) -> p c n", n=36)
        comb = room(3 * 34).rearrange("p (c e) -> p c e", e=NEXP + 2)
        slots = room(TC * 34).rearrange("p (c e) -> p c e", e=NEXP + 2)
        wide = room(3 * NEXP).rearrange("p (c g e) -> p c g e", g=NG, e=NE)
        pick, le, oh_1, oh_2 = (room(3 * NE).rearrange("p (c e) -> p c e", e=NE) for _ in range(4))
        g_exp, oh_g = (room(3 * NG).rearrange("p (c g) -> p c g", g=NG) for _ in range(2))
        top_g, top_1, top_2, least, e2, w_1, w_2 = (room(3) for _ in range(7))
        most_f, most = room(1), room(1).bitcast(I32)
        h_tok = room(TC * D).rearrange("p (c d) -> p c d", d=D)
        xg = room(2 * KD * SLOT).rearrange("p (q k s) -> p q k s", q=2, s=SLOT)
        y_slot = room(2 * 1024).rearrange("p (q d) -> p q d", q=2)
        sg = room(512).rearrange("p (q f) -> p q f", q=2)
        hid_t = room(512).rearrange("p (q f) -> p q f", q=2)
        pw = room(2 * 3 * P).rearrange("p (q c s) -> p q c s", q=2, c=3)
        disp = room(TC * P).rearrange("p (c s) -> p c s", c=TC)
        pwt = room(2 * NT).rearrange("p (q n) -> p q n", q=2)
        assert at[0] <= NTILE * NT
        h2s = misc[:, 0:KD * NS].rearrange("p (k n) -> p k n", n=NS)
        slot_no = misc[:, 128:256].rearrange("p (a s) -> p a s", a=2)
        own_slot = misc[0:NS, 256:384].rearrange("p (a s) -> p a s", a=2)
        own_w = comb[:, TC, :]
        eight = misc[:, 384:392]
        y_tok, ys_tok = h_tok, xg.rearrange("p q k s -> p (q k s)")[0:NS]

        def slot(s):
            return ring[:, s * RING:(s + 1) * RING]

        def weight_tile(mem, s, m):
            return mem[:, s * RING:(s + 1) * RING].rearrange("p (k c) -> p k c", c=256)[:, :, m * P:(m + 1) * P]

        def ada_src(sec):
            return (w_ada[0, :, sec * D:(sec + 1) * D] if sec < 6 else
                    w_ada_final[:, (sec - 6) * D:(sec - 5) * D]).rearrange("(k p) c -> p k c", p=P)

        IN_ROUND = 4
        IN_TILES = 50

        block = ctx.enter_context(nc.Block())

        class Chain:

            def __init__(self, eng, name):
                self.eng, self.sem, self.n = eng, S(name), 0

            def __call__(self, ins):
                self.n += 1
                ins.then_inc(self.sem, 1)
                self.eng.wait_ge(self.sem, self.n)

        def levels(flat, size):
            v = flat.rearrange("p (b n) -> p b n", n=size)
            return v, v[:, :, size // 2 - 1:size // 2].to_broadcast([P, GLA_H * NP_ // size, size])

        G_BANKS = ((0, 1, 2, 6), (3, 4, 5, 6))
        LEVELS = 8

        @block.sync
        def _(sp):
            def ada_load(sec):
                src = ada_src(sec)
                for i in range(8):
                    rnd, s = 2 * sec + i // 4, i % 4
                    if rnd > 0:
                        sp.wait_ge(S("ring_free"), MIX_SLOTS * (rnd - 1) + s + 1)
                    sp.dma_start(slot(s).rearrange("p (k c) -> p k c", c=D), src[:, 2 * i:2 * i + 2, :])\
                        .then_inc(S(f"ring_full{s}"), 16)

            sp.dma_start(c_row[0:1, :], c_prompt).then_inc(S("c_in"), 16)
            sp.dma_start(c_row[1:COND, :], c_sample).then_inc(S("c_in"), 16)
            ada_load(M_SH1)
            ada_load(M_SC1)
            for pair in range(3):
                skip = (0, GATE_RANK, GATE_RANK + RD)[pair]
                with sp.Fori(2 * pair, 2 * pair + 2) as g:
                    for s in range(4):
                        sp.wait_ge(S("ring_free"), (g + IN_ROUND - 1) * 4 + s + 1)
                        src = w_in[0, :, bass.ds(g * 1024 + skip + s * 256, 256)]
                        sp.dma_start(slot(s).rearrange("p (k c) -> p k c", c=256),
                                     src.rearrange("(k p) c -> p k c", p=P)).then_inc(S(f"ring_full{s}"), 16)
            sp.wait_ge(S("ring_free"), (IN_ROUND + 5) * 4 + 1)
            w = slot(0).rearrange("p (k c) -> p k c", c=256)
            for at, col in ((0, GCOLS + 1024), (RD, GCOLS + 3136)):
                sp.dma_start(w[:, :, at:at + RD], w_in[0, :, col:col + RD].rearrange("(k p) c -> p k c", p=P))\
                    .then_inc(S("small_w_in"), 16)
            sp.wait_ge(S("small_w_in"), 32)
            sp.dma_start(w[:, :, P:2 * P], w_in[0, :, GCOLS + 3200:GCOLS + 3328].rearrange("(k p) c -> p k c", p=P))\
                .then_inc(S("ring_full0"), 16)

            def ada_load2(weights, sec, at, peeled=0):
                for i in range(8):
                    s = 1 - i % 2
                    if i < peeled:
                        sp.wait_ge(S("ring_free"), (IN_ROUND + 5) * 4 + 2 if s else (IN_ROUND + 6) * 4 + 1)
                    else:
                        sp.wait_ge(S("r2_free"), (sec - 2) * 8 + (i - 1))
                    src = weights[:, bass.ds(at * D, D)].rearrange("(k p) c -> p k c", p=P)
                    sp.dma_start(slot(s).rearrange("p (k c) -> p k c", c=D), src[:, 2 * i:2 * i + 2, :])\
                        .then_inc(S(f"r2_full{s}"), 16)

            ada_load2(w_ada[0], 2, 2, peeled=2)
            with sp.Fori(3, 6) as sec:
                ada_load2(w_ada[0], sec, sec)
            with sp.Fori(6, 8) as sec:
                ada_load2(w_ada_final, sec, sec - 6)
            for i in range(8):
                s = i % 4
                if i >= 4:
                    sp.wait_ge(S("out_ps"), 2 * s + 2)
                elif s < 2:
                    sp.wait_ge(S("r2_free"), 48 - s)
                else:
                    sp.wait_ge(S("ck_y"), 2 * NCH)
                    sp.wait_ge(S("ck_yev"), 2 * NCH)
                    sp.wait_ge(S("rs_out"), 16 * RD // SI)
                    sp.wait_ge(S("ys_row"), RD // SI)
                sp.dma_start(slot(s).rearrange("p (k c) -> p k c", c=256),
                             w_out[0, :, i * 256:(i + 1) * 256].rearrange("(k p) c -> p k c", p=P))\
                    .then_inc(S(f"wo_full{s}"), 16)
            sp.wait_ge(*once("sr_ps"))
            sp.wait_ge(S("ck_s"), 2 * NCH)

            def expert_load(expert, before=None):
                for s in range(MOE_SLOTS):
                    if before is not None:
                        sp.wait_ge(S("m_free"), before + (s + 1))
                    elif s < MIX_SLOTS:
                        sp.wait_ge(S("out_ps"), 8 + 2 * s + 2)
                    else:
                        sp.wait_ge(S("out_ps"), KD)
                    half, w = s % 2, (w_exp_gate, w_exp_up, w_exp_down)[s // 2]
                    src = w[0].rearrange("g e a b -> (g e) a b")[bass.ds(expert, 1)]
                    if s < 4:
                        src = src.rearrange("o (k p) f -> p (o k) f", p=P)[:, 8 * half:8 * half + 8, :]
                    else:
                        src = src.rearrange("o (k p) f -> p (o k) f", p=P)[:, 2 * half:2 * half + 2, :]
                    sp.dma_start(slot(s).rearrange("p (k f) -> p k f", f=src.shape[2]), src)\
                        .then_inc(S(f"m_full{s}"), 16)

            expert_load(0)
            with sp.Fori(1, NEXP) as e:
                expert_load(e, (e - 1) * MOE_SLOTS)
            sp.wait_ge(*once("cap_ready"))
            count = sp.value_load(most[0:1, 0:1], min_val=0, max_val=NP_)
            with sp.If(count > CAP):
                with sp.Fori(1, PASSES) as ps:
                    with sp.Fori(0, NEXP) as e:
                        expert_load(e, ps * (NEXP * MOE_SLOTS) + e * MOE_SLOTS - MOE_SLOTS)
            for c in range(TC):
                sp.wait_ge(S("yo_evac"), 4 * c + 4)
                sp.dma_start(y_prompt[0, c * P:(c + 1) * P, :], y_tok[:, c, :]).then_inc(S("y_out"), 16)
            sp.wait_ge(S("yo_evac"), 12)
            sp.dma_start(y_sample[:, 0, :], ys_tok).then_inc(S("y_out"), 16)
            sp.wait_ge(S("y_out"), 48)

        @block.gpsimd
        def _(pool):
            link = Chain(pool, "consts")
            link(pool.memset(ident[:], 0.0))
            link(pool.memset(bones[:], 0.0))
            link(pool.memset(ones[:], 1.0))
            link(pool.memset(head_at[:], 0.0))
            pool.iota(idx_f, pattern=[[1, P]], base=0, channel_multiplier=0).then_inc(S("iotas"), 1)
            pool.iota(idx_p, pattern=[[0, P]], base=0, channel_multiplier=1).then_inc(S("iotas"), 1)
            link(pool.affine_select(out=ident[:], in_=ident[:], compare_op=ALU.not_equal, fill=1.0, base=0,
                                    pattern=[[-1, P]], channel_multiplier=1))
            link(pool.affine_select(out=mstrict[:], in_=ones[:], compare_op=ALU.is_gt, fill=0.0, base=0,
                                    pattern=[[1, P]], channel_multiplier=-1))
            for h in range(2):
                r = slice(RD * h, RD * h + RD)
                link(pool.memset(bones[r, r], 1.0))
                link(pool.memset(head_at[r, 14 + h:15 + h], 1.0))
                link(pool.affine_select(out=mincl[r, :], in_=ones[r, 0:CH], compare_op=ALU.is_ge, fill=0.0, base=0,
                                        pattern=[[1, CH]], channel_multiplier=-1))
            assert link.n == N_CONSTS
            for tile, part, col, width in SHIFT_PARTS:
                at = tile * P + part
                pool.dma_start(shift_row[:, at:at + width], state_shift[0, :, col:col + width])\
                    .then_inc(S("shift_in"), 16)
            pool.dma_start(gl_w, w_in[0, :, D:D + GATE_RANK].rearrange("(k p) c -> p k c", p=P)).then_inc(S("shift_in"), 16)
            pool.wait_ge(S("ring_free"), (IN_ROUND + 6) * 4)
            pool.wait_ge(S("in_evac_a"), 25)
            pool.wait_ge(S("in_evac_d"), 25)
            pool.wait_ge(*once("shs_ready"))
            pool.wait_ge(S("so_ps"), 7)
            mix = Chain(pool, "mix_chain")
            rp = pj[:, TR:TG7 + 1, :]
            mix(pool.tensor_tensor(dl[:, :, NP_:NT], shs, rp[:, :, NP_:NT], ALU.subtract))
            pool.tensor_scalar(dl[:, :, 0:1], rp[:, :, 0:1], -1.0, None, ALU.mult)
            mix(pool.tensor_tensor(dl[:, :, 1:NP_], rp[:, :, 0:NP_ - 1], rp[:, :, 1:NP_], ALU.subtract))
            mu = vecs[:, V_MU:V_MU + 26].unsqueeze(2).to_broadcast([P, 26, NT])
            mix(pool.tensor_tensor(dl, dl, mu, ALU.mult))
            pool.tensor_tensor(rp, rp, dl, ALU.add).then_inc(S("shift_mixed"), 1)
            pool.wait_ge(S("shift_mixed"), 1)
            pool.wait_ge(S("so_evac"), 7)
            for tile, part, col, width in SHIFT_PARTS:
                at = tile * P + part
                pool.dma_start(ss_prompt[0, :, col:col + width], shift_out[0:1, at:at + width]).then_inc(S("ss_out"), 16)
                pool.dma_start(ss_sample[0, :, col:col + width], shift_out[1:COND, at:at + width])\
                    .then_inc(S("ss_out"), 16)
            pool.wait_ge(S("ss_out"), 16 * 2 * len(SHIFT_PARTS))
            pool.dma_start(wa2[0:RD, :], rwkv_w2[0]).then_inc(S("low_rank_in"), 16)
            pool.dma_start(wa2[RD:P, :], rwkv_a2[0]).then_inc(S("low_rank_in"), 16)
            for h in range(GLA_H):
                pool.dma_start(gs[h], state_gla[0, :, h].rearrange("b k v -> k b v")).then_inc(S(f"sgs_in{h}"), 16)
            pool.wait_ge(*once("gst_evac"))
            pool.dma_start(sg_prompt[0, 0].rearrange("h k v -> k h v"), sg_new).then_inc(S("sg_out"), 16)
            pool.wait_ge(S("sg_out"), 16)
            for h in range(GLA_H):
                pool.wait_ge(S("gs_s"), h + 1)
                pool.dma_start(sg_sample[0, :, h].rearrange("b k v -> k b v"), gs[h]).then_inc(S("sgs_out"), 16)
            pool.tensor_copy(spread_to.rearrange("p (h d) -> p h d", d=RD),
                             ident[0:RH, 0:RH].unsqueeze(2).to_broadcast([RH, RH, RD])).then_inc(S("rk_mixed"), 1)
            pool.wait_ge(*once("rate"))
            pool.tensor_tensor(rk, rk, bonus, ALU.mult).then_inc(S("rk_mixed"), 1)
            pool.wait_ge(S("rk_mixed"), 2)
            pool.tensor_tensor(bonus, rr, rk, ALU.mult).then_inc(S("rk_mixed"), 1)
            pool.wait_ge(S("rk_mixed"), 3)
            pool.wait_ge(S("ki_ps"), 8)
            pool.dma_start(g2[:], rwkv_g2[0]).then_inc(S("g2_in"), 16)
            pool.wait_ge(S("sgs_out"), 16 * GLA_H)
            pool.wait_ge(S("cw_exp"), 3)
            pool.wait_ge(*once("rb_done"))
            for x in (rb, rk):
                pool.tensor_tensor(x[:, :, 0:NP_], x[:, :, 0:NP_], t1[:, :, 0:NP_], ALU.mult).then_inc(S("rk_mixed"), 1)
            pool.wait_ge(*once("sv_evac"))
            pool.dma_start(scratch, sv_row).then_inc(S("sv_store"), 16)
            pool.wait_ge(S("sv_store"), 16)
            for v in range(6):
                pool.dma_start(svt[:, v, :], scratch[v * NS:(v + 1) * NS, :].rearrange("b (h d) -> (b h) d", d=RD))\
                    .then_inc(S("sv_in"), 16)
            pool.wait_ge(S("sv_in"), 96)
            vr, vw, vk, vv, vkk, vb = (svt[:, i, :] for i in range(6))

            def over_i(x):
                return x.unsqueeze(1).to_broadcast([P, SI, RD])

            def over_j(x):
                return x.unsqueeze(2).to_broadcast([P, SI, RD])

            state_in = state_rwkv[0].rearrange("b h i j -> (b h) i j")
            state_out = sr_sample[0].rearrange("b h i j -> (b h) i j")
            STEPS = 20
            rs_link = Chain(pool, "rs_chain")

            def sum_keys(x):
                w = RD
                while w > 1:
                    w //= 2
                    rs_link(pool.tensor_tensor(x[:, :, 0:w], x[:, :, 0:w], x[:, :, w:2 * w], ALU.add))

            for n in range(RD // SI):
                rows = slice(n * SI, (n + 1) * SI)
                s_ = rs[n % 2]
                if n == 0:
                    for q in range(2):
                        pool.dma_start(rs[q], state_in[:, q * SI:(q + 1) * SI, :]).then_inc(S(f"rs_in{q}"), 16)
                pool.wait_ge(S(f"rs_in{n % 2}"), (n // 2 + 1) * 16)
                rs_link(pool.tensor_tensor(rt, s_, over_i(vkk), ALU.mult))
                sum_keys(rt)
                rs_link(pool.tensor_copy(sa_row.unsqueeze(2), rt[:, :, 0:1]))
                rs_link(pool.tensor_tensor(s_, s_, over_i(vw), ALU.mult))
                rs_link(pool.tensor_tensor(rt, over_j(sa_row), over_i(vb), ALU.mult))
                rs_link(pool.tensor_tensor(s_, s_, rt, ALU.subtract))
                rs_link(pool.tensor_tensor(rt, over_j(vv[:, rows]), over_i(vk), ALU.mult))
                rs_link(pool.tensor_tensor(s_, s_, rt, ALU.add))
                pool.dma_start(state_out[:, rows, :], s_).then_inc(S("rs_out"), 16)
                rs_link(pool.tensor_tensor(rt, s_, over_i(vr), ALU.mult))
                sum_keys(rt)
                pool.tensor_copy(y_row[:, rows].unsqueeze(2), rt[:, :, 0:1]).then_inc(S("ys_row"), 1)
                pool.wait_ge(S("ys_row"), n + 1)
                if n + 2 < RD // SI:
                    pool.wait_ge(S("rs_out"), (n + 1) * 16)
                    pool.dma_start(s_, state_in[:, (n + 2) * SI:(n + 3) * SI, :]).then_inc(S(f"rs_in{n % 2}"), 16)
            pool.wait_ge(S("rs_out"), 16 * RD // SI)
            pool.wait_ge(*once("sr_evac"))
            for h in range(2):
                r = slice(RD * h, RD * h + RD)
                pool.dma_start(sr_prompt[0, 0].rearrange("(p h) i j -> h i p j", h=2)[h], sr_new[r, :, r])\
                    .then_inc(S("sr_out"), 16)
            def out_lo(n, ks):
                pool.wait_ge(*once(f"o_hi{n}"))
                pool.tensor_tensor(ht_lo[:, ks, :], ht[:, ks, :], ht_hi[:, ks, :].bitcast(F32), ALU.subtract)\
                    .then_inc(S("out_lo"), 1)

            def out_weight_lo(t):
                pool.wait_ge(S("w_hi"), IN_TILES + t + 1)
                s, m = t // 2 % 4, t % 2
                pool.tensor_tensor(weight_tile(ring_r, s, m), weight_tile(ring, s, m), w_hi[:, m].bitcast(F32),
                                   ALU.subtract).then_inc(S("w_lo"), 1)

            out_lo(0, slice(0, 8))
            out_weight_lo(0)
            out_weight_lo(1)
            out_lo(1, slice(8, 12))
            out_lo(2, slice(12, 16))
            pool.wait_ge(S("o_rwkv"), 8)
            pool.dma_start(w_rt[:, :, 0:NG], w_router_group[0].rearrange("(k p) c -> p k c", p=P)).then_inc(S("rt_in"), 16)
            pool.dma_start(w_rt[:, :, NG:NG + NEXP], w_router_expert[0].rearrange("(k p) c -> p k c", p=P))\
                .then_inc(S("rt_in"), 16)
            rlink = Chain(pool, "rt_consts")
            rlink(pool.iota(slot_no, pattern=[[0, 2], [1, SLOT]], base=0, channel_multiplier=0,
                            allow_small_or_imprecise_dtypes=True))
            rlink(pool.memset(slot_no[:, :, 0:NS], -4096.0))
            rlink(pool.iota(eight, pattern=[[1, NE]], base=0, channel_multiplier=0, allow_small_or_imprecise_dtypes=True))
            rlink(pool.memset(own_slot, 0.0))
            rlink(pool.tensor_copy(own_slot[:, :, 0:NS], ident[0:NS, 0:NS].unsqueeze(1).to_broadcast([NS, 2, NS])))
            for t in range(2, KD):
                out_weight_lo(t)
            pool.wait_ge(S("sr_out"), 32)

        @block.scalar
        def _(act):
            act.wait_ge(S("c_in"), 32)
            act.activation(c_row, c_row, ACT.Silu).then_inc(once("c_silu")[0], 1)
            act.dma_start(x_tok, x_prompt[0].rearrange("(c p) d -> p c d", p=P)).then_inc(S("x_in"), 16)
            act.dma_start(x_row, x_sample[:, 0, :]).then_inc(S("x_in"), 16)
            rows = [[b_ada[0], b_ada_final],
                    [norm_mix[0], norm_ffn[0], norm_final, rwkv_mu[0, 0:1024], rwkv_mu[0, 1088:2112],
                     rwkv_mu[0, 2112:3136], (rwkv_mu[0, 1024:1088], 0), (rwkv_mu[0, 3136:3200], RD),
                     rwkv_mu[0, 3200:3328], gla_gate_b[0], gla_norm[0]],
                    [rwkv_w0[0], rwkv_a0[0], rwkv_k_k[0], rwkv_k_a[0], rwkv_r_k[0].rearrange("h d -> (h d)"),
                     rwkv_gn_w[0], rwkv_gn_b[0]]]
            n_vec = 0
            for g, group in enumerate(rows):
                at = 0
                for v in group:
                    if isinstance(v, tuple):
                        v, c = v
                        act.dma_start(vec_rows[at:at + 1, g, c:c + RD], v.rearrange("(r c) -> r c", c=RD))\
                            .then_inc(S("vec_in"), 16)
                        at += c // RD
                    else:
                        n = v.shape[0] // P
                        act.dma_start(vec_rows[at:at + n, g, :], v.rearrange("(r c) -> r c", c=P))\
                            .then_inc(S("vec_in"), 16)
                        at += n
                    n_vec += 1
            assert n_vec + 1 == N_VEC
            act.dma_start(gw2, gla_gate_w2[0]).then_inc(S("vec_in"), 16)
            def square(sem, out, in_):
                act.activation(out, in_, ACT.Square).then_inc(S(sem), 1)

            def root(n):
                act.wait_ge(S("ms_sum"), n)
                act.activation(rstd, rstd, ACT.Sqrt).then_inc(S("rms_root"), 1)

            def ada(sec):
                n = sec
                if isinstance(sec, int) and sec < 2:
                    act.wait_ge(S("ring_free"), (2 * sec + 2) * 4)
                else:
                    act.wait_ge(S("r2_free"), (sec - 2) * 8 + 8)
                act.wait_ge(S("ada_tr"), n)
                act.copy(ada_row[:], pb[7][:]).then_inc(S("ada_evac"), 1)

            ada(M_SH1)
            for k in range(KD):
                act.wait_ge(S("xT_ps"), k + 1)
                act.copy(xt[:, k, :], pb[2 + k % 4][:, 0:NT]).then_inc(S("xT_evac"), 1)
            act.wait_ge(S("xT_evac"), KD)
            square("norm_sq", ht[:, :, :], xt[:, :, :])
            root(1)
            ada(M_SC1)
            for k in range(8, KD):
                act.wait_ge(S("mod_g"), 1)
                act.activation(ht[:, k, 0:NP_], ht[:, k, 0:NP_], ACT.Identity, bias=mod[:, M_SH1, k, 0:1],
                               scale=gscale[:, k, 0:1]).then_inc(S("h_act"), 1)
            act.wait_ge(S("h_dve"), 1)
            act.wait_ge(S("h_act"), KD - 8)
            for i in range(2):
                k8 = slice(8 * i, 8 * i + 8)
                act.copy(ht_hi[:, k8, :], ht[:, k8, :]).then_inc(once(f"h_hi{i}")[0], 1)
            act.wait_ge(S("shift_in"), 16 * (len(SHIFT_PARTS) + 1))
            act.copy(gl_hi, gl_w).then_inc(once("gl_hi")[0], 1)

            def weight_hi(g, t):
                s, m = t // 2, t % 2
                if m:
                    act.wait_ge(S("ring_free"), (g + IN_ROUND) * 4 + s)
                else:
                    act.wait_ge(S(f"ring_full{s}"), (g + IN_ROUND + 1) * 16)
                    act.wait_ge(S("in_ps"), g * 4 + s)
                act.copy(w_hi[:, m], weight_tile(ring, s, m)).then_inc(S("w_hi"), 1)

            weight_hi(0, 0)
            with act.Fori(0, 6) as g:
                for t in range(8):
                    weight_hi(g + (t + 1) // 8, (t + 1) % 8)
                    if t % 2 == 0:
                        act.wait_ge(S("in_ps"), g * 4 + t // 2 + 1)
                        act.copy(pj[:, bass.ds(g * 8 + t, 1), :], pb[t % 4][:, 0:NT].rearrange("p (o n) -> p o n", o=1))\
                            .then_inc(S("in_evac_a"), 1)
            weight_hi(6, 1)
            act.wait_ge(S("in_ps"), 25)
            act.copy(pj[:, TWA, :], pb[0][:, 0:NT]).then_inc(S("in_evac_a"), 1)
            for b in range(7):
                act.wait_ge(S("so_ps"), b + 1)
                n = min(BANK, RCOLS - b * BANK)
                act.copy(shift_out[:, b * BANK:b * BANK + n], pb[3 + b % 2][0:COND, 0:n]).then_inc(S("so_evac"), 1)
            for b in range(4):
                act.wait_ge(S("vt_ps"), b + 1)
                act.copy(v_tok[:, b // 2, (b % 2) * BANK:(b % 2 + 1) * BANK], pb[b][:]).then_inc(S("vt_evac"), 1)
            act.wait_ge(*once("vs_ps"))
            act.wait_ge(S("mix_chain"), 1)
            for b in range(2):
                last = act.copy(v_row[:, b * BANK:(b + 1) * BANK], pb[4 + b][0:NS, :])
            last.then_inc(once("vs_evac")[0], 1)
            act.wait_ge(*once("ks_ps"))
            act.copy(k_row, pb[0][0:NS, :]).then_inc(once("ks_evac")[0], 1)
            act.wait_ge(*once("g_z"))
            link = Chain(act, "act_chain")
            link(act.activation(l4, z4, ACT.Abs))
            link(act.activation(l4, l4, ACT.Exp, scale=-1.0))
            act.activation(l4, l4, ACT.Ln, bias=1.0).then_inc(once("g_ln")[0], 1)
            act.wait_ge(*once("g_log"))
            act.activation(eg.rearrange("p (h b) -> p h b", b=NS), z4[:, :, NP_:NT], ACT.Exp).then_inc(once("eg")[0], 1)
            for l in range(LEVELS):
                act.wait_ge(S("lv_d"), l + 1)
                link(act.activation(e_flat, e_flat, ACT.Abs))
                act.activation(e_flat, e_flat, ACT.Exp, scale=-1.0).then_inc(S("lv_e"), 1)
            act.wait_ge(S("lv_qk"), LEVELS)
            for h in range(GLA_H):
                last = act.activation(e_flat[:, h * NP_:(h + 1) * NP_], cum4[:, h, :], ACT.Exp, scale=-1.0,
                                      bias=cum4[:, h, NP_ - 1:NP_])
            last.then_inc(once("kd_e")[0], 1)
            act.wait_ge(*once("kd_ps"))
            for c in range(TC):
                last = act.copy(kd_tok[:, c, :], pb[4 + c][:])
            last.then_inc(once("kd_evac")[0], 1)
            ada(2)
            act.wait_ge(S("ss_out"), 16 * 2 * len(SHIFT_PARTS))
            for b in range(4):
                act.wait_ge(S("go_ps"), b + 1)
                act.copy(ht[:, 2 * b:2 * b + 2, 0:NP_], pb[b][:].rearrange("p (t n) -> p t n", n=NP_))\
                    .then_inc(S("go_evac"), 1)
            act.wait_ge(*once("gst_ps"))
            act.wait_ge(*once("kd_e"))
            act.copy(sg_new[:, 0:2, :], pb[4][:].rearrange("p (h e) -> p h e", e=GLA_DV)).then_inc(once("gst_evac_a")[0], 1)
            act.wait_ge(*once("gst_evac_a"))
            act.copy(sg_new[:, 2:4, :], pb[5][:].rearrange("p (h e) -> p h e", e=GLA_DV)).then_inc(once("gst_evac")[0], 1)
            act.wait_ge(S("shift_mixed"), 1)
            link(act.activation(pj[:, TOG:TOG + 8, :], pj[:, TOG:TOG + 8, :], ACT.Silu))
            link(act.activation(pj[0:RD, TWA, :], pj[0:RD, TWA, :], ACT.Tanh))
            act.activation(pj[:, TG7, :], pj[:, TG7, :], ACT.Sigmoid).then_inc(once("gates_act")[0], 1)
            act.wait_ge(*once("gs_o"))
            for b in range(4):
                last = act.copy(o_rows[:, b // 2, (b % 2) * BANK:(b % 2 + 1) * BANK], pb[b][:])
            last.then_inc(once("or_evac")[0], 1)
            ada(3)
            act.wait_ge(*once("os_ps"))
            for a in range(2):
                for i in range(2):
                    last = act.copy(ht[:, 4 * i:4 * i + 4, NP_ + 4 * a:NP_ + 4 * a + 4],
                                    pb[2 * a + i][:].rearrange("p (t g r) -> p t g r", g=4, r=CPAD)[:, :, :, CPAD - 1])
            last.then_inc(once("gos_evac")[0], 1)
            act.wait_ge(*once("gos_evac"))
            act.wait_ge(S("go_evac"), 4)
            act.activation(gla_sq, o_gla, ACT.Square).then_inc(once("gla_sq")[0], 1)
            act.wait_ge(*once("gla_ms"))
            act.activation(gla_r, gla_r, ACT.Sqrt).then_inc(once("gla_root")[0], 1)
            act.wait_ge(S("sg_out"), 16)
            for i in range(16):
                t = i % 8
                act.wait_ge(S("rs_ps"), i + 1)
                dst, at = ((t0, V_W0), (rb, V_A0))[i // 8]
                act.activation(dst[:, t, :], pb[i % 4][:, 0:NT], ACT.Sigmoid, bias=vecs[:, at + t:at + t + 1])\
                    .then_inc(S("rs_evac"), 1)
            act.wait_ge(*once("kk_raw"))
            act.activation(t2, ra, ACT.Square).then_inc(once("kk_sq")[0], 1)
            act.wait_ge(*once("kn_ps"))
            act.activation(kn, pb[4][0:RH, 0:NT], ACT.Sqrt).then_inc(once("kn_root")[0], 1)
            act.wait_ge(S("rs_evac"), 16)
            for t in range(8):
                last = act.activation(bonus[:, t, :], rb[:, t, :], ACT.Identity, scale=vecs[:, V_KA + t:V_KA + t + 1],
                                      bias=om_ka[:, t:t + 1])
            last.then_inc(once("rate")[0], 1)
            act.activation(sv[:, :, 1, :], t0[:, :, NP_:NT], ACT.Exp, scale=-HALF_E).then_inc(once("sv_w")[0], 1)
            act.wait_ge(*once("sv_ps"))
            for b in range(2):
                last = act.copy(sv_row[:, b * BANK:(b + 1) * BANK], pb[6 + b][0:48, :])
            last.then_inc(once("sv_evac")[0], 1)
            act.wait_ge(S("rk_mixed"), 3)
            for t in range(8):
                last = act.mul(bonus[:, t, :], bonus[:, t, :], vecs[:, V_RK + t:V_RK + t + 1])
            last.then_inc(once("bonus_in")[0], 1)
            act.wait_ge(*once("cw"))
            for x, scale in ((t2, -HALF_E), (t0, -HALF_E), (t1, HALF_E)):
                src = t2 if x is t2 else t1
                act.activation(x[:, :, 0:NP_], src[:, :, 0:NP_], ACT.Exp, scale=scale).then_inc(S("cw_exp"), 1)

            act.wait_ge(S("sv_store"), 16)

            def tiles(bank):
                return pb[bank][:].rearrange("p (j n) -> p j n", n=P)

            with act.Fori(0, NCH) as c:
                for hf in range(2):
                    js = slice(4 * hf, 4 * hf + 4)
                    act.wait_ge(S("ck_y"), c * 2)
                    act.wait_ge(*once("ck_zero"))
                    for h in range(2):
                        r = slice(CH * h, CH * h + CH)
                        act.copy(kp[hf][r, :, r], rk[r, js, bass.ds(c * CH, CH)])
                        last = act.copy(vp[hf][r, :, r], rv[r, js, bass.ds(c * CH, CH)])
                    last.then_inc(S("ck_pad_a"), 1)
                for hf in range(2):
                    act.wait_ge(S("ck_t1"), c * 2 + (hf + 1))
                    for i, x in enumerate((bp, kp, vp)):
                        last = act.copy(x[hf], tiles(3 * hf + i))
                    last.then_inc(S("ck_t1e"), 1)
                for hf in range(2):
                    act.wait_ge(S("ck_t0"), c * 2 + (hf + 1))
                    act.copy(tm[hf], tiles(3 * hf)).then_inc(S("ck_t0e"), 1)
                    act.wait_ge(S("ck_u"), c * 2 + (hf + 1))
                    act.copy(um[hf], tiles(3 * hf + 1)).then_inc(S("ck_ue"), 1)
                for l in range(1, 6):
                    for hf in range(2):
                        act.wait_ge(S("iv_p"), c * 10 + (2 * l - 1 + hf))
                        act.copy(pm[hf], tiles(3 * hf + 2)).then_inc(S("iv_pe"), 1)
                for hf in range(2):
                    act.wait_ge(S("ck_sa"), c * 2 + (hf + 1))
                    act.copy(tm[hf], tiles(3 * hf + 2)).then_inc(S("ck_sae"), 1)
                ada(c + 4)
                for hf in range(2):
                    act.wait_ge(S("ck_y"), c * 2 + (hf + 1))
                    act.copy(y8[:, 4 * hf:4 * hf + 4, bass.ds(c * CH, CH)], tiles(3 * hf)[:, :, 0:CH])\
                        .then_inc(S("ck_yev"), 1)
            act.wait_ge(*once("sr_ps"))
            for b in range(2):
                last = act.copy(sr_new[:, 4 * b:4 * b + 4, :], pb[b][:].rearrange("p (j n) -> p j n", n=P))
            last.then_inc(once("sr_evac")[0], 1)
            def out_hi(n, ks):
                act.copy(ht_hi[:, ks, :], ht[:, ks, :]).then_inc(once(f"o_hi{n}")[0], 1)

            def out_weight_hi(t):
                s, m = t // 2 % 4, t % 2
                act.wait_ge(S(f"wo_full{s}"), 16 * (t // 8 + 1))
                if t >= 2:
                    act.wait_ge(S("out_ps"), t - 1)
                act.copy(w_hi[:, m], weight_tile(ring, s, m)).then_inc(S("w_hi"), 1)

            act.wait_ge(S("ck_s"), 2 * NCH)
            out_hi(0, slice(0, 8))
            out_weight_hi(0)
            act.wait_ge(*once("gn_c"))
            act.activation(ra, y8, ACT.Square).then_inc(once("gn_sq")[0], 1)
            act.wait_ge(*once("gn_ms"))
            act.activation(rr, rr, ACT.Sqrt).then_inc(once("gn_root")[0], 1)
            out_weight_hi(1)
            for i in range(2):
                act.wait_ge(S("o_rwkv"), 4 * i + 4)
                out_hi(i + 1, slice(8 + 4 * i, 12 + 4 * i))
            for t in range(2, KD):
                out_weight_hi(t)

            def scale_upper(n, sh):
                for k in range(8, KD):
                    act.wait_ge(S("mod_g"), n)
                    act.activation(ht[:, k, 0:NP_], ht[:, k, 0:NP_], ACT.Identity, bias=mod[:, sh, k, 0:1],
                                   scale=gscale[:, k, 0:1]).then_inc(S("h_act"), 1)

            act.wait_ge(S("x1"), KD)
            square("norm_sq", ht[:, :, :], xt[:, :, :])
            root(2)
            scale_upper(2, M_SH2)
            act.wait_ge(*once("lg_ps"))
            act.copy(lg_t, pb[1][0:NG + NEXP, 0:NT]).then_inc(once("lg_evac")[0], 1)
            for b in range(8):
                act.wait_ge(S("h2t_ps"), b + 1)
                act.copy(h_tok[:, b // 4, (b % 4) * BANK:(b % 4 + 1) * BANK], pb[3 + b % 4][:]).then_inc(S("h2t_evac"), 1)
            act.wait_ge(*once("rt_d1"))
            act.activation(g_exp, g_exp, ACT.Exp).then_inc(once("rt_e1")[0], 1)
            act.wait_ge(*once("rt_d2"))
            act.activation(e2, e2, ACT.Exp).then_inc(once("rt_e2")[0], 1)

            def moe_gather_out(n):
                for b in range(2):
                    act.wait_ge(S("m_ga"), n * 4 + (b + 1))
                    act.copy(xg[:, :, 4 * b:4 * b + 4, :], pb[b][:].rearrange("p (k q s) -> p q k s", q=2, s=SLOT))\
                        .then_inc(S("m_ga_a"), 1)

            def moe_act(ps):
                moe_gather_out(ps * 17)
                with act.Fori(0, NEXP // 2) as i:
                    t = ps * 16 + i
                    for q in range(2):
                        used = (t * 2 + q) * MOE_SLOTS
                        act.wait_ge(S(f"m_wt{q}"), t + 1)
                        act.copy(pwt[:, q, :], pb[5 - q][:, 0:NT]).then_inc(S(f"m_wte{q}"), 1)
                        act.wait_ge(S("m_free"), used + 4)
                        act.activation(sg[:, q, :], pb[4 + q][:, 0:256], ACT.Silu).then_inc(S(f"m_sg{q}"), 1)
                        if q == 1:
                            moe_gather_out(ps * 17 + i + 1)
                        act.wait_ge(S(f"m_hp{q}"), t + 1)
                        act.copy(hid_t[:, q, :], pb[4 + q][:, 0:256]).then_inc(S(f"m_ht{q}"), 1)
                        act.wait_ge(S("m_free"), used + 6)
                        act.wait_ge(S(f"m_sc{q}"), (t + q) * KD + ps * (KD if q else 0))
                        act.copy(y_slot[:, q, 0:BANK], pb[6][:])
                        act.copy(y_slot[:, q, BANK:2 * BANK], pb[7][:]).then_inc(S(f"m_ye{q}"), 1)

            moe_act(0)
            act.wait_ge(*once("cap_ready"))
            count = act.value_load(most[0:1, 0:1], min_val=0, max_val=NP_)
            with act.If(count > CAP):
                with act.Fori(1, PASSES) as ps:
                    moe_act(ps)
            act.wait_ge(S("x2"), 1)
            square("norm_sq", ht[:, :, :], xt[:, :, :])
            root(3)
            scale_upper(3, M_SHF)
            for b in range(0, 12, 2):
                act.wait_ge(S("yo_ps"), b + 1)
                dst = (y_tok[:, b // 4, (b % 4) * BANK:(b % 4 + 1) * BANK] if b < 8 else
                       ys_tok[:, (b - 8) * BANK:(b - 7) * BANK])
                act.wait_ge(S("yo_evac"), b)
                act.copy(dst, pb[1 + b % 4][0:dst.shape[0], :]).then_inc(S("yo_evac"), 1)

        @block.vector
        def _(dve):
            link = Chain(dve, "dve_chain")
            dve.memset(ct, 0.0).then_inc(once("c_zeroed")[0], 1)
            dve.wait_ge(*once("cT_ps"))
            dve.wait_ge(*once("c_zeroed"))
            dve.tensor_copy(ct[:, :, 0:COND], pb[0][:, 0:KD * COND].rearrange("p (k n) -> p k n", n=COND))\
                .then_inc(once("cT_ready")[0], 1)
            dve.wait_ge(S("iotas"), 2)
            link(dve.tensor_tensor(idx_x, idx_f, idx_p, ALU.bitwise_xor))
            dve.tensor_copy(xor_f, idx_x)
            link(dve.tensor_tensor(tri_f, idx_f, idx_p, ALU.is_gt))
            dve.tensor_scalar(lm[:, 7, :], xor_f, 0.0, None, ALU.is_equal)
            link(dve.tensor_tensor(tri_f, xor_f, tri_f, ALU.mult))
            for l in range(7):
                link(dve.tensor_scalar(ge_f, tri_f, float(2 ** l), None, ALU.is_ge))
                link(dve.scalar_tensor_tensor(out=lm[:, l, :], in0=tri_f, scalar=float(2 ** (l + 1)), in1=ge_f,
                                              op0=ALU.is_lt, op1=ALU.mult))
            dve.wait_ge(*once("vec_ps"))
            dve.tensor_copy(vecs[:], pb[1][:, 0:V_END]).then_inc(once("vecs_ready")[0], 1)
            dve.wait_ge(*once("vecs_ready"))
            dve.tensor_scalar(om_ka[:], vecs[:, V_KA:V_KA + 8], -1.0, 1.0, ALU.mult, ALU.add)

            def vec(at, n, m):
                return vecs[:, at:at + n].unsqueeze(2).to_broadcast([P, n, m])

            def rms_start(n):
                dve.wait_ge(S("ms_ps"), n)
                dve.tensor_scalar(rstd, pb[0][:, 0:NT], 1.0 / D, EPS, ALU.mult, ALU.add).then_inc(S("ms_sum"), 1)
                dve.wait_ge(S("rms_root"), n)
                link(dve.reciprocal(rstd, rstd))
                link(dve.tensor_tensor(ht[:, :, :], xt[:, :, :], rstd.unsqueeze(1).to_broadcast([P, KD, NT]), ALU.mult))

            def modulate(n, norm, sc, sh):
                dve.scalar_tensor_tensor(out=gscale[:, :, :], in0=mod[:, sc], scalar=1.0, in1=vec(norm, KD, COND),
                                         op0=ALU.add, op1=ALU.mult).then_inc(S("mod_g"), 1)
                dve.wait_ge(S("mod_g"), n)
                for k in range(8):
                    dve.tensor_scalar(ht[:, k, 0:NP_], ht[:, k, 0:NP_], gscale[:, k, 0:1], mod[:, sh, k, 0:1],
                                      ALU.mult, ALU.add)
                link(dve.tensor_tensor(ht[:, :, NP_:NT], ht[:, :, NP_:NT], gscale[:, :, 1:COND], ALU.mult))
                dve.tensor_tensor(ht[:, :, NP_:NT], ht[:, :, NP_:NT], mod[:, sh, :, 1:COND], ALU.add)\
                    .then_inc(S("h_dve"), 1)

            def ada(sec):
                n = sec
                dve.wait_ge(S("ada_tr"), n + 1)
                src = pb[6][:].rearrange("p (j g r) -> p g j r", j=4, g=4)[:, :, :, 0:COND]
                dst = mod[:, bass.ds(sec, 1)].rearrange("p o (g j) r -> p (o g) j r", g=4)
                b = vecs[:, bass.ds(sec * KD + V_ADA, KD)].rearrange("p (g j) -> p g j", g=4)
                dve.tensor_tensor(dst, src, b.unsqueeze(3).to_broadcast([P, 4, 4, COND]), ALU.add)\
                    .then_inc(S("ada_mod"), 1)

            ada(M_SH1)
            rms_start(1)
            ada(M_SC1)
            dve.wait_ge(S("ada_mod"), 2)
            modulate(1, V_NMIX, M_SC1, M_SH1)
            dve.wait_ge(*once("shs_ps"))
            dve.tensor_copy(shs, pb[5][:, 0:26 * NS].rearrange("p (t n) -> p t n", n=NS)).then_inc(once("shs_ready")[0], 1)
            for i in range(2):
                k8 = slice(8 * i, 8 * i + 8)
                dve.wait_ge(*once(f"h_hi{i}"))
                dve.tensor_tensor(ht_lo[:, k8, :], ht[:, k8, :], ht_hi[:, k8, :].bitcast(F32), ALU.subtract)\
                    .then_inc(once(f"h_lo{i}")[0], 1)
            dve.wait_ge(*once("gl_hi"))
            dve.tensor_tensor(gl_lo, gl_w, gl_hi.bitcast(F32), ALU.subtract).then_inc(once("gl_lo")[0], 1)

            def weight_lo(g, t):
                s, m = t // 2, t % 2
                dve.wait_ge(S("w_hi"), g * 8 + t + 1)
                dve.tensor_tensor(weight_tile(ring_r, s, m), weight_tile(ring, s, m), w_hi[:, m].bitcast(F32), ALU.subtract).then_inc(S("w_lo"), 1)

            weight_lo(0, 0)
            with dve.Fori(0, 6) as g:
                for t in range(8):
                    weight_lo(g + (t + 1) // 8, (t + 1) % 8)
                    if t % 2:
                        dve.wait_ge(S("ring_free"), g * 4 + IN_ROUND * 4 + t // 2 + 1)
                        dve.tensor_copy(pj[:, bass.ds(g * 8 + t, 1), :],
                                        pb[t % 4][:, 0:NT].rearrange("p (o n) -> p o n", o=1)).then_inc(S("in_evac_d"), 1)
            weight_lo(6, 1)
            dve.wait_ge(*once("gl_ps"))
            dve.tensor_copy(pj[0:GATE_RANK, TGL, :], pb[2][0:GATE_RANK, 0:NT]).then_inc(once("gl_ready")[0], 1)
            dve.wait_ge(S("ring_free"), (IN_ROUND + 6) * 4 + 1)
            dve.tensor_copy(pj[:, TG7, :], pb[1][:, 0:NT]).then_inc(S("in_evac_d"), 1)
            dve.wait_ge(*once("gz_ps"))
            for h in range(GLA_H):
                last = dve.tensor_scalar(z4[:, h, :], pb[h][:, 0:NT], vecs[:, V_GB + h:V_GB + h + 1], None, ALU.add)
            last.then_inc(once("g_z")[0], 1)
            link(dve.tensor_scalar(pj[:, TQ:TQ + 4, :], pj[:, TQ:TQ + 4, :], GLA_DK ** -0.5, None, ALU.mult))
            dve.memset(at0[:, :, 0:P], 0.0)
            link(dve.memset(at1, 0.0))
            dve.wait_ge(*once("g_ln"))
            link(dve.scalar_tensor_tensor(out=z4, in0=z4, scalar=0.0, in1=l4, op0=ALU.min, op1=ALU.subtract))
            dve.tensor_scalar(z4, z4, 1.0 / 16.0, None, ALU.mult).then_inc(once("g_log")[0], 1)
            dve.wait_ge(*once("g_log"))
            for h in range(GLA_H):
                last = dve.tensor_tensor_scan(cum4[:, h, :], ones[:, 0:1].to_broadcast([P, NP_]), z4[:, h, 0:NP_], 0.0,
                                              ALU.mult, ALU.add)
            link(last)
            dve.wait_ge(*once("eg"))

            def level_diff(l):
                b, ref = levels(cum, NP_ >> l)
                e, _ = levels(e_flat, NP_ >> l)
                dve.tensor_tensor(e, b, ref, ALU.subtract).then_inc(S("lv_d"), 1)

            level_diff(0)
            e4 = e_flat.rearrange("p (h n) -> p h n", n=NP_)
            for l in range(LEVELS + 1):
                if l < LEVELS:
                    dve.wait_ge(S("lv_e"), l + 1)
                    if l > 0:
                        dve.wait_ge(S("lv_ps"), l)
                    dve.tensor_tensor(q4, pj[:, TQ:TQ + 4, 0:NP_], e4, ALU.mult)
                    dve.tensor_tensor(k4, pj[:, TK:TK + 4, 0:NP_], e4, ALU.mult).then_inc(S("lv_qk"), 1)
                if l + 1 < LEVELS:
                    dve.wait_ge(S("lv_qk"), l + 1)
                    level_diff(l + 1)
                dve.wait_ge(S("lv_ps"), l + 1)
                b = 2 * (l % 2)
                src = [pb[b + i][:].rearrange("p (h n) -> p h n", n=P) for i in range(2)]
                if l == 0:
                    dve.tensor_copy(at0[:, :, P:NP_], src[0]).then_inc(S("lv_sel"), 1)
                    continue
                m = lm[:, 7 - l if l < LEVELS else 7, :].bitcast(I32).unsqueeze(1).to_broadcast([P, GLA_H, P])
                dve.wait_ge(S("lv_sel"), l)
                dve.copy_predicated(at0[:, :, 0:P], m, src[0])
                dve.copy_predicated(at1, m, src[1]).then_inc(S("lv_sel"), 1)
            dve.wait_ge(*once("kd_e"))
            dve.wait_ge(S("lv_ps"), LEVELS + 1)
            dve.tensor_tensor(k4, pj[:, TK:TK + 4, 0:NP_], e4, ALU.mult).then_inc(once("kd")[0], 1)
            ada(2)
            for h in range(GLA_H):
                if h == 0:
                    dve.wait_ge(*once("ks_evac"))
                    dve.wait_ge(*once("gst_evac"))
                else:
                    dve.wait_ge(S("gs_kv"), 4 * h)
                dve.tensor_tensor(kz, k_row[:, h * GLA_DK:(h + 1) * GLA_DK].unsqueeze(1).to_broadcast([NS, NS, GLA_DK]),
                                  ident[0:NS, 0:NS].unsqueeze(2).to_broadcast([NS, NS, GLA_DK]), ALU.mult)\
                    .then_inc(S("kz"), 1)
                dve.wait_ge(S(f"sgs_in{h}"), 16)
                for b in range(NS):
                    if b % 2 == 0:
                        dve.wait_ge(S("gs_kv"), 4 * h + b // 2 + 1)
                    last = dve.scalar_tensor_tensor(
                        out=gs[h][:, b, :], in0=gs[h][:, b, :], scalar=eg[:, h * NS + b:h * NS + b + 1],
                        in1=pb[b // 2][:, (b % 2) * GLA_DV:(b % 2 + 1) * GLA_DV], op0=ALU.mult, op1=ALU.add)
                last.then_inc(S("gs_s"), 1)
            ada(3)
            dve.wait_ge(*once("gn_ps"))
            for h in range(GLA_H):
                last = dve.tensor_scalar(gla_r[:, h, :], pb[h][:, 0:NT], 1.0 / GLA_DV, GLA_EPS, ALU.mult, ALU.add)
            last.then_inc(once("gla_ms")[0], 1)
            dve.wait_ge(*once("gla_root"))
            link(dve.reciprocal(gla_r, gla_r))
            oh = o_gla.rearrange("p (h e) n -> p h e n", e=2)
            link(dve.tensor_tensor(oh, oh, gla_r.unsqueeze(2).to_broadcast([P, GLA_H, 2, NT]), ALU.mult))
            og = pj[:, TOG:TOG + 8, :].rearrange("p (h e) n -> p h e n", e=2)
            dve.wait_ge(*once("gates_act"))
            for e in range(2):
                last = dve.scalar_tensor_tensor(out=oh[:, :, e, :], in0=oh[:, :, e, :], scalar=vecs[:, V_GN + e:V_GN + e + 1],
                                                in1=og[:, :, e, :], op0=ALU.mult, op1=ALU.mult)
            last.then_inc(once("gla_done")[0], 1)
            dve.wait_ge(*once("gla_done"))
            dve.tensor_tensor(ra, rk, vec(V_KK, 8, NT), ALU.mult).then_inc(once("kk_raw")[0], 1)
            link(dve.memset(keep, 1.0))
            link(dve.memset(keep.rearrange("p (c n) -> p c n", n=CH)[:, :, 0:1], 0.0))
            dve.wait_ge(S("rs_evac"), 8)
            for t in range(4):
                dve.tensor_tensor_scan(t1[:, t, 0:NP_], keep, t0[:, t, 0:NP_], 0.0, ALU.mult, ALU.add)
            dve.wait_ge(*once("kn_root"))
            link(dve.tensor_scalar(kn, kn, 1e-12, None, ALU.max))
            dve.reciprocal(kn, kn).then_inc(once("kn_inv")[0], 1)
            for t in range(4, 8):
                last = dve.tensor_tensor_scan(t1[:, t, 0:NP_], keep, t0[:, t, 0:NP_], 0.0, ALU.mult, ALU.add)
            link(last)
            dve.tensor_tensor(t2[:, :, 0:NP_], t1[:, :, 0:NP_], t0[:, :, 0:NP_], ALU.subtract).then_inc(once("cw")[0], 1)
            for t in range(8):
                dve.wait_ge(S("ki_ps"), t + 1)
                dve.tensor_tensor(ra[:, t, :], ra[:, t, :], pb[t % 4][:, 0:NT], ALU.mult).then_inc(S("ki_evac"), 1)
            dve.wait_ge(S("ki_evac"), 8)
            dve.engine_nop().then_inc(once("kk_done")[0], 1)
            dve.wait_ge(S("rs_evac"), 16)
            dve.wait_ge(*once("rate"))
            dve.tensor_tensor(rb, rb, ra, ALU.mult).then_inc(once("rb_done")[0], 1)
            dve.wait_ge(*once("rb_done"))
            dve.wait_ge(S("rk_mixed"), 2)
            for v, src in ((0, rr), (2, rk), (3, rv), (4, ra), (5, rb)):
                last = dve.tensor_copy(sv[:, :, v, :], src[:, :, NP_:NT])
            last.then_inc(once("sv_rest")[0], 1)
            for t in range(8):
                dve.wait_ge(S("bonus_ps"), t + 1)
                dve.tensor_tensor(bonus[:, t, :], pb[t % 4][:, 0:NT], rv[:, t, :], ALU.mult).then_inc(S("bonus_evac"), 1)

            def pr(x):
                return x[:, :, 0:NP_]

            dve.wait_ge(S("cw_exp"), 1)
            dve.scalar_tensor_tensor(out=pr(ra), in0=pr(ra), scalar=-1.0, in1=pr(t2), op0=ALU.mult, op1=ALU.mult)
            dve.wait_ge(S("cw_exp"), 2)
            dve.wait_ge(S("rk_mixed"), 3)
            dve.tensor_tensor(pr(rr), pr(rr), pr(t0), ALU.mult)
            link(dve.tensor_copy(wc, pr(t0).rearrange("p t (c n) -> p t c n", n=CH)[:, :, :, CH - 1]))
            dve.wait_ge(S("sgs_out"), 16 * GLA_H)
            dve.wait_ge(S("rk_mixed"), 5)
            for x in (ar, bp, kp, vp):
                for hf in range(2):
                    dve.memset(x[hf], 0.0)
            dve.memset(st, 0.0).then_inc(once("ck_zero")[0], 1)
            dve.wait_ge(*once("ck_zero"))

            def masks(m, count):
                return m.unsqueeze(1).to_broadcast([P, count, m.shape[1]])

            def tiles(bank):
                return pb[bank][:].rearrange("p (j n) -> p j n", n=P)

            with dve.Fori(0, NCH) as c:
                for hf in range(2):
                    js = slice(4 * hf, 4 * hf + 4)
                    dve.wait_ge(S("ck_y"), c * 2)
                    for h in range(2):
                        r = slice(CH * h, CH * h + CH)
                        dve.tensor_copy(ar[hf][r, :, r], ra[r, js, bass.ds(c * CH, CH)])
                        dve.tensor_copy(bp[hf][r, :, r], rb[r, js, bass.ds(c * CH, CH)])
                    dve.tensor_copy(ar[hf][:, :, P:192], rr[:, js, bass.ds(c * CH, CH)]).then_inc(S("ck_pad_d"), 1)
                for hf in range(2):
                    n = c * 2 + hf
                    dve.wait_ge(S("ck_g"), n + 1)
                    g = [pb[i][:, 0:384].rearrange("p (j n) -> p j n", n=192) for i in G_BANKS[hf]]
                    for i in range(2):
                        s2 = slice(2 * i, 2 * i + 2)
                        dve.tensor_tensor(ltm[hf][:, s2, :], g[i][:, :, 0:P], masks(mstrict[:], 2), ALU.mult)
                        dve.tensor_tensor(mtm[hf][:, s2, :], g[2 + i][:, :, 0:P], masks(mstrict[:], 2), ALU.mult)
                        dve.tensor_tensor(rbm[hf][:, s2, :], g[i][:, :, P:192], masks(mincl[:], 2), ALU.mult)
                        last = dve.tensor_tensor(rkm[hf][:, s2, :], g[2 + i][:, :, P:192], masks(mincl[:], 2), ALU.mult)
                    last.then_inc(S("ck_m"), 1)
                for hf in range(2):
                    n = c * 2 + hf
                    dve.wait_ge(S("ck_m"), n + 1)
                    dve.tensor_tensor(lo[hf], ltm[hf], masks(lm[:, 0, :], 4), ALU.mult).then_inc(S("ck_l0"), 1)
                    dve.wait_ge(S("ck_l0"), n + 1)
                    dve.tensor_tensor(tt[hf], lo[hf], masks(ident[:], 4), ALU.add).then_inc(S("ck_tt0"), 1)
                    dve.wait_ge(S("ck_tt0"), n + 1)
                    dve.tensor_tensor(lo[hf], ltm[hf], masks(lm[:, 1, :], 4), ALU.mult).then_inc(S("iv_lo"), 1)
                for l in range(1, 6):
                    for hf in range(2):
                        if l < 5:
                            dve.wait_ge(S("iv_p"), c * 10 + (2 * l - 1 + hf))
                            dve.tensor_tensor(lo[hf], ltm[hf], masks(lm[:, l + 1, :], 4), ALU.mult)\
                                .then_inc(S("iv_lo"), 1)
                    for hf in range(2):
                        dve.wait_ge(S("iv_t"), c * 10 + (2 * l - 1 + hf))
                        last = dve.tensor_tensor(tt[hf], tt[hf], tiles(3 * hf), ALU.add)
                        if l < 5:
                            last = dve.tensor_tensor(tm[hf], tm[hf], tiles(3 * hf + 1), ALU.add)
                        last.then_inc(S("iv_tn"), 1)
                for hf in range(2):
                    n = c * 2 + hf
                    js = slice(4 * hf, 4 * hf + 4)
                    dve.wait_ge(S("ck_y"), n + 1)
                    dve.tensor_tensor(st[:, js, :], st[:, js, :], tiles(3 * hf + 1), ALU.add).then_inc(S("ck_sadd"), 1)
                    dve.wait_ge(S("ck_sadd"), n + 1)
                    dve.tensor_tensor(st[:, js, :], st[:, js, :],
                                      wc[:, js, bass.ds(c, 1)].to_broadcast([P, 4, P]), ALU.mult).then_inc(S("ck_s"), 1)
                ada(c + 4)
            dve.wait_ge(*once("ys_ps"))
            dve.wait_ge(S("ck_yev"), 2 * NCH)
            for h in range(2):
                last = dve.tensor_copy(y8[RD * h:RD * h + RD, :, NP_:NT],
                                       pb[2][0:RD, 0:P].rearrange("p (b t h) -> p h t b", b=NS, h=2)[:, h])
            last.then_inc(once("y_all")[0], 1)
            dve.wait_ge(*once("y_all"))
            for t in range(8):
                dve.wait_ge(S("mu_ps"), t + 1)
                last = dve.scalar_tensor_tensor(out=y8[:, t, :], in0=pb[t % 4][:, 0:NT], scalar=-1.0 / RD, in1=y8[:, t, :],
                                                op0=ALU.mult, op1=ALU.add)
                last.then_inc(S("mu_evac"), 1)
            dve.wait_ge(S("mu_evac"), 8)
            dve.engine_nop().then_inc(once("gn_c")[0], 1)
            for t in range(8):
                dve.wait_ge(S("var_ps"), t + 1)
                last = dve.tensor_scalar(rr[:, t, :], pb[t % 4][:, 0:NT], 1.0 / RD, GN_EPS, ALU.mult, ALU.add)
                last.then_inc(S("var_evac"), 1)
            dve.wait_ge(S("var_evac"), 8)
            dve.engine_nop().then_inc(once("gn_ms")[0], 1)
            dve.wait_ge(*once("gn_root"))
            link(dve.reciprocal(rr, rr))
            link(dve.tensor_tensor(y8, y8, rr, ALU.mult))
            link(dve.tensor_tensor(y8, y8, vec(V_GW, 8, NT), ALU.mult))
            link(dve.tensor_tensor(y8, y8, vec(V_GBI, 8, NT), ALU.add))
            link(dve.tensor_tensor(y8, y8, bonus, ALU.add))
            for t in range(8):
                dve.wait_ge(S("g_ps"), t + 1)
                dve.tensor_tensor(y8[:, t, :], y8[:, t, :], pb[t % 4][:, 0:NT], ALU.mult).then_inc(S("o_rwkv"), 1)
            for t in range(KD):
                dve.wait_ge(S("out_ps"), t + 1)
                b = pb[4 + t % 4]
                dve.scalar_tensor_tensor(out=xt[:, t, 0:NP_], in0=b[:, 0:NP_], scalar=mod[:, M_GT1, t, 0:1],
                                         in1=xt[:, t, 0:NP_], op0=ALU.mult, op1=ALU.add)
                dve.wait_ge(S("x1"), t)
                link(dve.tensor_tensor(tmp_s, b[:, NP_:NT], mod[:, M_GT1, t, 1:COND], ALU.mult))
                dve.tensor_tensor(xt[:, t, NP_:NT], xt[:, t, NP_:NT], tmp_s, ALU.add).then_inc(S("x1"), 1)
            rms_start(2)
            modulate(2, V_NFFN, M_SC2, M_SH2)
            dve.wait_ge(S("rt_consts"), 5)
            dve.wait_ge(S("g_ps"), 8)
            link(dve.memset(lg, 0.0))
            link(dve.memset(slots, -1.0))
            link(dve.memset(comb, 0.0))
            dve.wait_ge(*once("lgt_ps"))
            dve.tensor_copy(lg[:, 0:TC, :], pb[2][:, 0:TC * 36].rearrange("p (c n) -> p c n", n=36))
            link(dve.tensor_copy(lg[0:NS, TC, :], pb[2][0:NS, TC * 36:3 * 36]))
            dve.wait_ge(S("h_dve"), 2)
            link(dve.tensor_copy(h2s, ht[:, :, NP_:NT]))

            def first_max(x, n, top, one_hot):
                link(dve.tensor_reduce(top, x, axis=AX.X, op=ALU.max))
                c = pick[:, :, 0:n]
                link(dve.tensor_tensor(c, x, top.unsqueeze(2).to_broadcast([P, 3, n]), ALU.is_equal))
                link(dve.scalar_tensor_tensor(out=c, in0=c, scalar=-64.0, in1=eight[:, 0:n].unsqueeze(1).to_broadcast([P, 3, n]),
                                              op0=ALU.mult, op1=ALU.add))
                link(dve.tensor_reduce(least, c, axis=AX.X, op=ALU.min))
                link(dve.tensor_tensor(one_hot, c, least.unsqueeze(2).to_broadcast([P, 3, n]), ALU.is_equal))

            first_max(lg[:, :, 0:NG], NG, top_g, oh_g)
            dve.tensor_tensor(g_exp, lg[:, :, 0:NG], top_g.unsqueeze(2).to_broadcast([P, 3, NG]), ALU.subtract)\
                .then_inc(once("rt_d1")[0], 1)
            le4 = lg[:, :, NG:].rearrange("p c (g e) -> p c g e", e=NE)
            by_g = oh_g.unsqueeze(3).to_broadcast([P, 3, NG, NE])
            link(dve.tensor_tensor(wide, le4, by_g, ALU.mult))
            link(dve.tensor_reduce(le, wide.rearrange("p c g e -> p c e g"), axis=AX.X, op=ALU.add))
            first_max(le, NE, top_1, oh_1)
            link(dve.scalar_tensor_tensor(out=le, in0=oh_1, scalar=-1e30, in1=le, op0=ALU.mult, op1=ALU.add))
            first_max(le, NE, top_2, oh_2)
            dve.tensor_tensor(e2, top_2, top_1, ALU.subtract).then_inc(once("rt_d2")[0], 1)
            dve.wait_ge(*once("rt_e1"))
            link(dve.tensor_reduce(w_1, g_exp, axis=AX.X, op=ALU.add))
            dve.wait_ge(*once("rt_e2"))
            link(dve.scalar_tensor_tensor(out=w_1, in0=e2, scalar=1.0, in1=w_1, op0=ALU.add, op1=ALU.mult))
            link(dve.reciprocal(w_1, w_1))
            link(dve.tensor_tensor(w_2, w_1, e2, ALU.mult))
            dve.tensor_tensor(le, oh_1, w_1.unsqueeze(2).to_broadcast([P, 3, NE]), ALU.mult)
            link(dve.tensor_tensor(pick, oh_2, w_2.unsqueeze(2).to_broadcast([P, 3, NE]), ALU.mult))
            link(dve.tensor_tensor(le, le, pick, ALU.add))
            link(dve.tensor_tensor(oh_1, oh_1, oh_2, ALU.add))
            c4 = comb[:, :, 0:NEXP].rearrange("p c (g e) -> p c g e", e=NE)
            dve.tensor_tensor(c4, le.unsqueeze(2).to_broadcast([P, 3, NG, NE]), by_g, ALU.mult)
            dve.tensor_tensor(wide, oh_1.unsqueeze(2).to_broadcast([P, 3, NG, NE]), by_g, ALU.mult).then_inc(once("routed")[0], 1)
            dve.wait_ge(*once("routed"))
            dve.wait_ge(*once("rk_ps"))
            sl = slots[:, :, 0:NEXP]
            link(dve.tensor_reduce(most_f, pb[1][:, 2 * NEXP:3 * NEXP], axis=AX.X, op=ALU.max))
            dve.tensor_copy(most[:, 0:1], most_f).then_inc(once("cap_ready")[0], 1)
            link(dve.scalar_tensor_tensor(out=sl, in0=pb[1][:, 0:2 * NEXP].rearrange("p (c e) -> p c e", e=NEXP),
                                          scalar=float(NS + 1), in1=wide.rearrange("p c g e -> p c (g e)")[:, 0:TC],
                                          op0=ALU.add, op1=ALU.mult))
            link(dve.tensor_scalar(sl, sl, -1.0, None, ALU.add))
            dve.wait_ge(S("h2t_ps"), 8)
            dve.wait_ge(*once("lg_ps"))
            dve.wait_ge(S("h_act"), 2 * (KD - 8))
            link(dve.memset(ht, 0.0))

            def moe_dispatch(n, t):
                dve.wait_ge(S("m_ga"), n * 4)
                for q in range(2):
                    for c in range(TC):
                        last = dve.tensor_scalar(disp[:, c, q * SLOT:(q + 1) * SLOT], slot_no[:, 0, :],
                                                 slots[:, c, bass.ds(t * 2 + q, 1)], None, ALU.is_equal)
                last.then_inc(S("m_dp"), 1)

            def moe_gather_out(n):
                for b in range(2, 4):
                    dve.wait_ge(S("m_ga"), n * 4 + (b + 1))
                    last = dve.tensor_copy(xg[:, :, 4 * b:4 * b + 4, :],
                                           pb[b][:].rearrange("p (k q s) -> p q k s", q=2, s=SLOT))
                last.then_inc(S("m_ga_d"), 1)
                dve.wait_ge(S("m_ga_a"), (n + 1) * 2)
                dve.wait_ge(S("m_ga_d"), n + 1)
                dve.tensor_copy(xg[:, :, :, 0:NS], h2s.unsqueeze(1).to_broadcast([P, 2, KD, NS])).then_inc(S("m_xg"), 1)

            def moe_add(q, n):
                for i in range(KD):
                    k = (i % 2) * 8 + i // 2
                    dve.wait_ge(S(f"m_sc{q}"), n * KD + (i + 1))
                    dve.tensor_tensor(ht[:, k, :], ht[:, k, :], pb[i % 4][:, 0:NT], ALU.add)\
                        .then_inc(S(f"m_add{q}"), 1)

            def moe_dve(ps):
                if not isinstance(ps, int):
                    dve.tensor_scalar(sl, sl, -float(CAP), None, ALU.add)
                    dve.memset(own_w, 0.0).then_inc(S("m_next"), 1)
                    dve.wait_ge(S("m_next"), ps)
                dve.wait_ge(S("m_sc1"), ps * (17 * KD))
                dve.memset(pwt[:, 1, :], 0.0)
                dve.memset(y_slot[:, 1, :], 0.0).then_inc(S("m_zero"), 1)
                moe_dispatch(ps * 17, 0)
                moe_gather_out(ps * 17)
                with dve.Fori(0, NEXP // 2) as i:
                    t = ps * 16 + i
                    for q in range(2):
                        dve.wait_ge(S(f"m_wt{q}"), t)
                        for c in range(TC):
                            dve.tensor_scalar(pw[:, q, c, :], slot_no.rearrange("p a s -> p (a s)"),
                                              slots[:, c, bass.ds(i * 2 + q, 1)], comb[:, c, bass.ds(i * 2 + q, 1)],
                                              ALU.is_equal, ALU.mult)
                        dve.tensor_scalar(pw[0:NS, q, TC, :], own_slot.rearrange("p a s -> p (a s)"),
                                          comb[0:NS, TC, bass.ds(i * 2 + q, 1)], None, ALU.mult)\
                            .then_inc(S(f"m_pw{q}"), 1)
                    moe_dispatch(ps * 17 + i + 1, i + 1)
                    for q in range(2):
                        dve.wait_ge(S(f"m_sg{q}"), t + 1)
                        dve.wait_ge(S("m_free"), (t * 2 + q) * MOE_SLOTS + 4)
                        dve.tensor_tensor(sg[:, q, :], sg[:, q, :], pb[4 + q][:, 256:512], ALU.mult)\
                            .then_inc(S(f"m_hid{q}"), 1)
                        moe_add(1 - q, ps * (17 if q == 0 else 16) + i)
                        if q == 1:
                            moe_gather_out(ps * 17 + i + 1)
                moe_add(1, ps * 17 + 16)
                dve.wait_ge(S("m_add1"), ps * (17 * KD) + 17 * KD)

            moe_dve(0)
            dve.wait_ge(*once("cap_ready"))
            count = dve.value_load(most[0:1, 0:1], min_val=0, max_val=NP_)
            with dve.If(count > CAP):
                with dve.Fori(1, PASSES) as ps:
                    moe_dve(ps)
            for k in range(KD):
                dve.scalar_tensor_tensor(out=xt[:, k, 0:NP_], in0=ht[:, k, 0:NP_], scalar=mod[:, M_GT2, k, 0:1],
                                         in1=xt[:, k, 0:NP_], op0=ALU.mult, op1=ALU.add)
            link(dve.tensor_tensor(ht[:, :, NP_:NT], ht[:, :, NP_:NT], mod[:, M_GT2, :, 1:COND], ALU.mult))
            dve.tensor_tensor(xt[:, :, NP_:NT], xt[:, :, NP_:NT], ht[:, :, NP_:NT], ALU.add).then_inc(S("x2"), 1)
            rms_start(3)
            modulate(3, V_NFIN, M_SCF, M_SHF)
            for b in range(1, 12, 2):
                dve.wait_ge(S("yo_ps"), b + 1)
                dst = (y_tok[:, b // 4, (b % 4) * BANK:(b % 4 + 1) * BANK] if b < 8 else
                       ys_tok[:, (b - 8) * BANK:(b - 7) * BANK])
                dve.wait_ge(S("yo_evac"), b)
                dve.tensor_copy(dst, pb[1 + b % 4][0:dst.shape[0], :]).then_inc(S("yo_evac"), 1)

        @block.tensor
        def _(pe):
            pe.wait_ge(S("consts"), N_CONSTS)
            pe.wait_ge(*once("c_silu"))
            for k in range(KD):
                last = pe.transpose(pb[0][:, k * COND:(k + 1) * COND], c_row[:, k * P:(k + 1) * P], ident[0:COND, 0:COND])
            last.then_inc(once("cT_ps")[0], 1)
            def sum_squares(n):
                pe.wait_ge(S("norm_sq"), n)
                for k in range(KD):
                    last = pe.matmul(pb[0][:, 0:NT], ones[:], ht[:, k, :], start=(k == 0), stop=(k == KD - 1))
                last.then_inc(S("ms_ps"), 1)

            def ada_piece(sec, i):
                if i == 0:
                    pe.wait_ge(S("ada_evac"), sec)
                if isinstance(sec, int) and sec < 2:
                    s, full, free = i % 4, "ring_full", "ring_free"
                    pe.wait_ge(S(f"ring_full{s}"), (2 * sec + i // 4 + 1) * 16)
                else:
                    s, full, free = 1 - i % 2, "r2_full", "r2_free"
                    pe.wait_ge(S(f"r2_full{s}"), (sec - 2) * 64 + (i // 2 + 1) * 16)
                w = slot(s).rearrange("p (k c) -> p k c", c=D)
                for j in range(2):
                    k = 2 * i + j
                    for g in range(4):
                        last = pe.matmul(pb[7][g * CPAD:(g + 1) * CPAD, :], ct[:, k, :],
                                         w[:, j, g * BANK:(g + 1) * BANK], start=(k == 0), stop=(k == KD - 1))
                last.then_inc(S(free), 1)

            def ada_turn(sec):
                pe.wait_ge(S("ada_evac"), sec + 1)
                pe.wait_ge(S("ada_mod"), sec)
                for j in range(4):
                    last = pe.transpose(pb[6][:, j * P:(j + 1) * P], ada_row[:, j * P:(j + 1) * P], ident[:])
                last.then_inc(S("ada_tr"), 1)

            pe.wait_ge(*once("cT_ready"))
            for i in range(8):
                ada_piece(M_SH1, i)
            pe.wait_ge(S("vec_in"), 16 * N_VEC)
            for g, (at, n) in enumerate(((V_ADA, 128), (V_NMIX, 80), (V_W0, 56))):
                last = pe.transpose(pb[1][:, at:at + n], vec_rows[0:n, g, :], ident[0:n, 0:n])
            last.then_inc(once("vec_ps")[0], 1)
            ada_turn(M_SH1)
            pe.wait_ge(S("x_in"), 32)
            for k in range(KD):
                if k >= 4:
                    pe.wait_ge(S("xT_evac"), k - 3)
                bank = pb[2 + k % 4]
                for c in range(TC):
                    pe.transpose(bank[:, c * P:(c + 1) * P], x_tok[:, c, k * P:(k + 1) * P], ident[:])
                pe.transpose(bank[:, NP_:NT], x_row[:, k * P:(k + 1) * P], ident[0:NS, 0:NS]).then_inc(S("xT_ps"), 1)
            sum_squares(1)
            for i in range(8):
                ada_piece(M_SC1, i)
            ada_turn(M_SC1)
            pe.wait_ge(S("shift_in"), 16 * (len(SHIFT_PARTS) + 1))
            for t in range(26):
                last = pe.transpose(pb[5][:, t * NS:(t + 1) * NS], shift_row[:, t * P:(t + 1) * P], ident[0:NS, 0:NS])
            last.then_inc(once("shs_ps")[0], 1)

            def project(out, hi, lo, first=0, end=KD):
                for k in range(first, end):
                    pe.matmul(out, hi[:, k, :], ht_lo[:, k, :], start=(k == 0), stop=False)
                    pe.matmul(out, lo[:, k, :], ht_hi[:, k, :], start=False, stop=False)
                    last = pe.matmul(out, hi[:, k, :], ht_hi[:, k, :], start=False, stop=(k == KD - 1))
                return last

            pe.wait_ge(*once("h_lo1"))

            def in_tile(g, t):
                s, m = t // 2, t % 2
                pe.wait_ge(S("w_lo"), g * 8 + t + 1)
                taken = S("in_evac_d" if m else "in_evac_a")
                if t >= 4:
                    pe.wait_ge(taken, g * 4 + (t - 4) // 2 + 1)
                elif isinstance(g, int):
                    pe.wait_ge(taken, g * 4 + (t - 4) // 2 + 1)
                else:
                    pe.wait_ge(taken, g * 4)
                project(pb[t % 4][:, 0:NT], w_hi[:, m], weight_tile(ring_r, s, m)).then_inc(S("ring_free" if m else "in_ps"), 1)

            with pe.Fori(0, 6) as g:
                for t in range(8):
                    in_tile(g, t)
            pe.wait_ge(*once("gl_lo"))
            pe.wait_ge(S("in_evac_a"), 24)
            project(pb[2][0:GATE_RANK, 0:NT], gl_hi, gl_lo).then_inc(once("gl_ps")[0], 1)
            for t in range(2):
                in_tile(6, t)
            for b in range(7):
                if b >= 2:
                    pe.wait_ge(S("so_evac"), b - 1)
                if b == 0:
                    pe.wait_ge(S("in_evac_a"), 25)
                    pe.wait_ge(S("in_evac_d"), 25)
                for j in range(4 if b < 6 else 2):
                    last = pe.transpose(pb[3 + b % 2][0:COND, j * P:(j + 1) * P], pj[:, TR + 4 * b + j, NP_ - 1:NT],
                                        ident[:])
                last.then_inc(S("so_ps"), 1)
            pe.wait_ge(S("so_evac"), 7)
            for c in range(TC):
                for t in range(8):
                    last = pe.transpose(pb[2 * c + t // 4][:, (t % 4) * P:(t % 4 + 1) * P],
                                        pj[:, TV + t, c * P:(c + 1) * P], ident[:])
                    if t % 4 == 3:
                        last.then_inc(S("vt_ps"), 1)
            pe.wait_ge(*once("shs_ready"))
            for t in range(8):
                last = pe.transpose(pb[4 + t // 4][0:NS, (t % 4) * P:(t % 4 + 1) * P], pj[:, TV + t, NP_:NT], ident[:])
            last.then_inc(once("vs_ps")[0], 1)
            pe.wait_ge(S("vt_evac"), 1)
            for t in range(4):
                last = pe.transpose(pb[0][0:NS, t * P:(t + 1) * P], pj[:, TK + t, NP_:NT], ident[:])
            last.then_inc(once("ks_ps")[0], 1)
            pe.wait_ge(*once("gl_ready"))
            pe.wait_ge(*once("ks_evac"))
            pe.wait_ge(S("vt_evac"), 4)
            for h in range(GLA_H):
                last = pe.matmul(pb[h][:, 0:NT], gw2[:, h * GLA_DK:(h + 1) * GLA_DK], pj[0:GATE_RANK, TGL, :],
                                 start=True, stop=True)
            last.then_inc(once("gz_ps")[0], 1)
            pe.wait_ge(*once("g_z"))
            for l in range(LEVELS + 1):
                if l < LEVELS:
                    pe.wait_ge(S("lv_qk"), l + 1)
                if l >= 2:
                    pe.wait_ge(S("lv_sel"), l - 1)
                q, k = (q4, k4) if l < LEVELS else (pj[:, TQ:TQ + 4, :], pj[:, TK:TK + 4, :])
                for i in range(1 if l == 0 else 2):
                    for h in range(GLA_H):
                        ks, qs = (0, 1) if l == 0 else (i, i)
                        last = pe.matmul(pb[2 * (l % 2) + i][:, h * P:(h + 1) * P], k[:, h, ks * P:(ks + 1) * P],
                                         q[:, h, qs * P:(qs + 1) * P], start=True, stop=True)
                last.then_inc(S("lv_ps"), 1)
                if l < LEVELS:
                    ada_piece(2, l)
            pe.wait_ge(*once("kd"))
            pe.wait_ge(*once("vs_evac"))
            for c in range(TC):
                for h in range(GLA_H):
                    last = pe.transpose(pb[4 + c][:, h * P:(h + 1) * P], k4[:, h, c * P:(c + 1) * P], ident[:])
            last.then_inc(once("kd_ps")[0], 1)
            ada_turn(2)
            pe.wait_ge(S("lv_sel"), LEVELS + 1)
            for t in range(8):
                h, b = t // 2, pb[t // 2]
                o = (t % 2) * NP_
                v0, v1 = (v_tok[:, c, t * P:(t + 1) * P] for c in range(TC))
                pe.matmul(b[:, o:o + P], v0, at0[:, h, 0:P], start=True, stop=True)
                pe.matmul(b[:, o + P:o + NP_], v0, at0[:, h, P:NP_], start=True, stop=False)
                last = pe.matmul(b[:, o + P:o + NP_], v1, at1[:, h, :], start=False, stop=True)
                if t % 2:
                    last.then_inc(S("go_ps"), 1)
            pe.wait_ge(*once("kd_evac"))
            for h in range(GLA_H):
                for c in range(TC):
                    last = pe.matmul(pb[4 + h // 2][:, (h % 2) * GLA_DV:(h % 2 + 1) * GLA_DV],
                                     kd_tok[:, c, h * GLA_DK:(h + 1) * GLA_DK], v_tok[:, c, h * GLA_DV:(h + 1) * GLA_DV],
                                     start=(c == 0), stop=(c == TC - 1))
            last.then_inc(once("gst_ps")[0], 1)
            pe.wait_ge(*once("gst_evac"))
            for h in range(GLA_H):
                pe.wait_ge(S("kz"), h + 1)
                if h == 0:
                    pe.wait_ge(S("go_evac"), 4)
                else:
                    pe.wait_ge(S("gs_s"), h)
                for b in range(NS):
                    last = pe.matmul(pb[b // 2][:, (b % 2) * GLA_DV:(b % 2 + 1) * GLA_DV], kz[:, b, :],
                                     v_row[:, h * GLA_DV:(h + 1) * GLA_DV], start=True, stop=True)
                    if b % 2:
                        last.then_inc(S("gs_kv"), 1)
                ada_piece(3, 2 * h)
                ada_piece(3, 2 * h + 1)
            pe.wait_ge(S("gs_s"), GLA_H)
            for a in range(2):
                for h in range(GLA_H):
                    for g in range(4):
                        b = 4 * a + g
                        last = pe.matmul(pb[2 * a + h // 2][g * CPAD:(g + 1) * CPAD, (h % 2) * GLA_DV:(h % 2 + 1) * GLA_DV],
                                         pj[:, TQ + h, NP_ + b - CPAD + 1:NP_ + b + 1], gs[h][:, b, :],
                                         start=True, stop=True)
            last.then_inc(once("gs_o")[0], 1)
            ada_turn(3)
            pe.wait_ge(*once("or_evac"))
            for a in range(2):
                for t in range(8):
                    last = pe.transpose(pb[2 * a + t // 4][:, (t % 4) * P:(t % 4 + 1) * P],
                                        o_rows[:, a, t * P:(t + 1) * P], ident[:])
            last.then_inc(once("os_ps")[0], 1)
            pe.wait_ge(*once("gos_evac"))
            pe.wait_ge(*once("gla_sq"))
            for h in range(GLA_H):
                for e in range(2):
                    last = pe.matmul(pb[h][:, 0:NT], ones[:], gla_sq[:, 2 * h + e, :], start=(e == 0), stop=(e == 1))
            last.then_inc(once("gn_ps")[0], 1)
            pe.wait_ge(S("low_rank_in"), 32)
            pe.wait_ge(*once("gates_act"))
            pe.wait_ge(*once("gla_ms"))
            for i in range(16):
                r = slice(RD * (i // 8), RD * (i // 8) + RD)
                if i >= 4:
                    pe.wait_ge(S("rs_evac"), i - 3)
                pe.matmul(pb[i % 4][:, 0:NT], wa2[r, (i % 8) * P:(i % 8 + 1) * P], pj[r, TWA, :], start=True, stop=True)\
                    .then_inc(S("rs_ps"), 1)

            def head_sums(src, ps_sem, free_sem, base=0, banks=(0, 1, 2, 3)):
                n = len(banks)
                for t in range(8):
                    if t >= n:
                        pe.wait_ge(S(free_sem), base + t - n + 1)
                    pe.matmul(pb[banks[t % n]][:, 0:NT], bones[:], src[:, t, :], start=True, stop=True)\
                        .then_inc(S(ps_sem), 1)

            def head_rows(bank, src):
                for t in range(8):
                    last = pe.matmul(pb[bank][0:RH, 0:NT], head_at[:, 14 - 2 * t:14 - 2 * t + RH], src[:, t, :],
                                     start=(t == 0), stop=(t == 7))
                return last

            def spread(bank, rows, t):
                return pe.matmul(pb[bank][:, 0:NT], spread_to[:, t * P:(t + 1) * P], rows, start=True, stop=True)

            pe.wait_ge(*once("kk_sq"))
            head_rows(4, t2).then_inc(once("kn_ps")[0], 1)
            pe.wait_ge(*once("kn_inv"))
            pe.wait_ge(S("rk_mixed"), 1)
            pe.wait_ge(S("rs_evac"), 16)
            for t in range(8):
                if t >= 4:
                    pe.wait_ge(S("ki_evac"), t - 3)
                spread(t % 4, kn, t).then_inc(S("ki_ps"), 1)
            pe.wait_ge(*once("sv_rest"))
            pe.wait_ge(*once("sv_w"))
            for t in range(8):
                last = pe.transpose(pb[6 + t // 4][0:48, (t % 4) * P:(t % 4 + 1) * P],
                                    sv[:, t].rearrange("p v b -> p (v b)"), ident[:])
            last.then_inc(once("sv_ps")[0], 1)
            pe.wait_ge(*once("bonus_in"))
            pe.wait_ge(S("ki_evac"), 8)
            head_sums(bonus, "bonus_ps", "bonus_evac")
            pe.wait_ge(*once("sv_evac"))
            pe.wait_ge(S("bonus_evac"), 8)
            def four(bank, lhs, rhs, start=True, stop=True):
                for j in range(4):
                    last = pe.matmul(pb[bank][:, j * P:(j + 1) * P], lhs[:, j, :], rhs[:, j, :], start=start, stop=stop)
                return last

            def turn(bank, x):
                for j in range(4):
                    last = pe.transpose(pb[bank][:, j * P:(j + 1) * P], x[:, j, :], ident[:])
                return last

            def twice(x):
                return x.unsqueeze(1).to_broadcast([P, 2, CH])

            with pe.Fori(0, NCH) as c:
                for hf in range(2):
                    n = c * 2 + hf
                    pe.wait_ge(S("ck_pad_d"), n + 1)
                    pe.wait_ge(S("ck_pad_a"), n + 1)
                    pe.wait_ge(S("ck_s"), c * 2)
                    pe.wait_ge(S("ck_yev"), c * 2)
                    if hf == 0:
                        pe.wait_ge(S("ada_mod"), c + 4)
                    else:
                        pe.wait_ge(S("ck_m"), n)
                    for i, x in enumerate((bp, kp)):
                        for j in range(4):
                            last = pe.matmul(pb[G_BANKS[hf][2 * i + j // 2]][:, (j % 2) * 192:(j % 2 + 1) * 192],
                                             x[hf][:, j, :], ar[hf][:, j, :], start=True, stop=True)
                    last.then_inc(S("ck_g"), 1)
                    ada_piece(c + 4, hf)
                for hf in range(2):
                    pe.wait_ge(S("ck_m"), c * 2 + (hf + 1))
                    for i, x in enumerate((bp, kp, vp)):
                        last = turn(3 * hf + i, x[hf])
                    last.then_inc(S("ck_t1"), 1)
                for hf in range(2):
                    n = c * 2 + hf
                    pe.wait_ge(S("ck_tt0"), n + 1)
                    pe.wait_ge(S("ck_t1e"), n + 1)
                    turn(3 * hf, tt[hf]).then_inc(S("ck_t0"), 1)
                    for j in range(4):
                        o = pb[3 * hf + 1][:, j * P:(j + 1) * P]
                        pe.matmul(o, ar[hf][:, j, 0:P], st[:, 4 * hf + j, :], start=True, stop=False)
                        last = pe.matmul(o, mtm[hf][:, j, :], vp[hf][:, j, :], start=False, stop=True)
                    last.then_inc(S("ck_u"), 1)
                for l in range(1, 6):
                    for hf in range(2):
                        if l == 1:
                            pe.wait_ge(S("ck_t0e"), c * 2 + (hf + 1))
                            pe.wait_ge(S("ck_ue"), c * 2 + (hf + 1))
                        else:
                            pe.wait_ge(S("iv_tn"), c * 10 + (2 * l - 3 + hf))
                        pe.wait_ge(S("iv_lo"), c * 10 + (2 * l - 1 + hf))
                        four(3 * hf + 2, lo[hf], tm[hf]).then_inc(S("iv_p"), 1)
                    ada_piece(c + 4, 1 + l)
                    for hf in range(2):
                        pe.wait_ge(S("iv_pe"), c * 10 + (2 * l - 1 + hf))
                        last = four(3 * hf, pm[hf], tt[hf])
                        if l < 5:
                            last = four(3 * hf + 1, tt[hf], pm[hf])
                        last.then_inc(S("iv_t"), 1)
                ada_piece(c + 4, 7)
                for hf in range(2):
                    pe.wait_ge(S("iv_tn"), c * 10 + (9 + hf))
                    four(3 * hf + 2, tt[hf], um[hf]).then_inc(S("ck_sa"), 1)
                for hf in range(2):
                    pe.wait_ge(S("ck_sae"), c * 2 + (hf + 1))
                    for j in range(4):
                        o = pb[3 * hf][:, j * P:(j + 1) * P]
                        pe.matmul(o, st[:, 4 * hf + j, :], twice(ar[hf][:, j, P:192]), start=True, stop=False)
                        pe.matmul(o, tm[hf][:, j, :], twice(rbm[hf][:, j, :]), start=False, stop=False)
                        pe.matmul(o, vp[hf][:, j, :], twice(rkm[hf][:, j, :]), start=False, stop=True)
                        o = pb[3 * hf + 1][:, j * P:(j + 1) * P]
                        pe.matmul(o, bp[hf][:, j, :], tm[hf][:, j, :], start=True, stop=False)
                        last = pe.matmul(o, kp[hf][:, j, :], vp[hf][:, j, :], start=False, stop=True)
                    last.then_inc(S("ck_y"), 1)
                ada_turn(c + 4)
            pe.wait_ge(S("ck_s"), 2 * NCH)
            pe.wait_ge(S("ck_yev"), 2 * NCH)
            for t in range(8):
                last = pe.transpose(pb[t // 4][:, (t % 4) * P:(t % 4 + 1) * P], st[:, t, :], ident[:])
            last.then_inc(once("sr_ps")[0], 1)
            pe.wait_ge(S("ys_row"), RD // SI)
            pe.transpose(pb[2][0:RD, 0:P], y_row, ident[:]).then_inc(once("ys_ps")[0], 1)
            pe.wait_ge(*once("sr_evac"))
            pe.wait_ge(*once("y_all"))
            head_sums(y8, "mu_ps", "mu_evac")
            pe.wait_ge(*once("gn_sq"))
            head_sums(ra, "var_ps", "var_evac")
            def out_tile(t, first=0, end=KD):
                return project(pb[4 + t % 4][:, 0:NT], w_hi[:, t % 2], weight_tile(ring_r, t // 2 % 4, t % 2), first, end)

            pe.wait_ge(S("out_lo"), 1)
            for t in range(2):
                pe.wait_ge(S("w_lo"), IN_TILES + t + 1)
                out_tile(t, 0, 8)
            pe.wait_ge(S("g2_in"), 16)
            for t in range(8):
                pe.wait_ge(S("var_evac"), min(8, t + 5))
                if t >= 4:
                    pe.wait_ge(S("o_rwkv"), t - 3)
                pe.matmul(pb[t % 4][:, 0:NT], g2[:, t * P:(t + 1) * P], pj[:, TG7, :], start=True, stop=True)\
                    .then_inc(S("g_ps"), 1)
            pe.wait_ge(S("out_lo"), 3)
            for t in range(KD):
                if t >= 2:
                    pe.wait_ge(S("w_lo"), IN_TILES + t + 1)
                if t >= 4:
                    pe.wait_ge(S("x1"), t - 3)
                out_tile(t, 8 if t < 2 else 0).then_inc(S("out_ps"), 1)
            pe.wait_ge(S("x1"), KD)
            sum_squares(2)
            pe.wait_ge(S("rt_in"), 32)
            pe.wait_ge(S("h_dve"), 2)
            pe.wait_ge(S("h_act"), 2 * (KD - 8))
            for k in range(KD):
                last = pe.matmul(pb[1][0:NG + NEXP, 0:NT], w_rt[:, k, :], ht[:, k, :], start=(k == 0), stop=(k == KD - 1))
            last.then_inc(once("lg_ps")[0], 1)
            for b in range(8):
                if b >= 4:
                    pe.wait_ge(S("h2t_evac"), b - 3)
                if b == 1:
                    pe.wait_ge(*once("lg_evac"))
                    for c in range(3):
                        m = P if c < TC else NS
                        last = pe.transpose(pb[2][0:m, c * 36:(c + 1) * 36], lg_t[:, c * P:c * P + m], ident[0:36, 0:36])
                    last.then_inc(once("lgt_ps")[0], 1)
                for j in range(4):
                    k = 4 * (b % 4) + j
                    last = pe.transpose(pb[3 + b % 4][:, j * P:(j + 1) * P], ht[:, k, (b // 4) * P:(b // 4 + 1) * P],
                                        ident[:])
                last.then_inc(S("h2t_ps"), 1)
            pe.wait_ge(*once("routed"))
            m = [wide[:, c].rearrange("p g e -> p (g e)") for c in range(TC)]
            pe.matmul(pb[1][:, 0:NEXP], mstrict[:], m[0], start=True, stop=True)
            pe.matmul(pb[1][:, NEXP:2 * NEXP], ones[:], m[0], start=True, stop=False)
            pe.matmul(pb[1][:, NEXP:2 * NEXP], mstrict[:], m[1], start=False, stop=True)
            pe.matmul(pb[1][:, 2 * NEXP:3 * NEXP], ones[:], m[0], start=True, stop=False)
            pe.matmul(pb[1][:, 2 * NEXP:3 * NEXP], ones[:], m[1], start=False, stop=True).then_inc(once("rk_ps")[0], 1)
            pe.wait_ge(S("h2t_evac"), 8)
            pe.wait_ge(*once("cap_ready"))

            def moe_gather(n):
                pe.wait_ge(S("m_dp"), n + 1)
                for b in range(4):
                    for j in range(4):
                        k = 4 * b + j
                        for c in range(TC):
                            last = pe.matmul(pb[b][:, j * P:(j + 1) * P], h_tok[:, c, k * P:(k + 1) * P], disp[:, c, :],
                                             start=(c == 0), stop=(c == TC - 1))
                    last.then_inc(S("m_ga"), 1)

            def moe_scatter(q, n):
                for i in range(KD):
                    k = (i % 2) * 8 + i // 2
                    r = slice(SLOT * (i % 2), SLOT * (i % 2) + SLOT)
                    if i >= 4:
                        pe.wait_ge(S(f"m_add{q}"), n * KD + (i - 3))
                    pe.matmul(pb[i % 4][:, 0:NT], y_slot[r, q, (k % 8) * P:(k % 8 + 1) * P], pwt[r, q, :],
                              start=True, stop=True).then_inc(S(f"m_sc{q}"), 1)

            def moe_pe(ps):
                pe.wait_ge(S("m_zero"), ps + 1)
                pe.wait_ge(S("m_add1"), ps * (17 * KD))
                moe_gather(ps * 17)
                with pe.Fori(0, NEXP // 2) as i:
                    t = ps * 16 + i
                    for q in range(2):
                        pe.wait_ge(S(f"m_pw{q}"), t + 1)
                        bank = pb[5 - q]
                        pe.wait_ge(S(f"m_ht{1 - q}"), t + q)
                        for c in range(3):
                            m = P if c < TC else NS
                            last = pe.transpose(bank[:, c * P:c * P + m], pw[0:m, q, c, :], ident[0:m, 0:m])
                        last.then_inc(S(f"m_wt{q}"), 1)
                        if q == 0:
                            pe.wait_ge(S("m_wte1"), t)
                            pe.wait_ge(S("m_xg"), ps * 17 + i + 1)
                        else:
                            pe.wait_ge(S("m_wte0"), t + 1)
                        for s in range(4):
                            pe.wait_ge(S(f"m_full{s}"), (t * 2 + q + 1) * 16)
                            w = slot(s).rearrange("p (k f) -> p k f", f=FF)
                            o = (s // 2) * 256
                            for j in range(8):
                                k = (s % 2) * 8 + j
                                for h in range(2):
                                    last = pe.matmul(pb[4 + q][SLOT * h:SLOT * h + SLOT, o:o + 256], xg[:, q, k, :],
                                                     w[:, j, h * 256:(h + 1) * 256], start=(k == 0), stop=(k == KD - 1))
                            last.then_inc(S("m_free"), 1)
                        if q == 0:
                            pe.wait_ge(S("m_ye1"), t)
                            moe_scatter(1, ps * 17 + i)
                        else:
                            pe.wait_ge(S("m_ye0"), t + 1)
                            pe.wait_ge(S("m_add1"), ps * (17 * KD) + (i + 1) * KD)
                            moe_scatter(0, t)
                            pe.wait_ge(S("m_add0"), (t + 1) * KD)
                            moe_gather(ps * 17 + i + 1)
                        pe.wait_ge(S(f"m_hid{q}"), t + 1)
                        for j in range(2):
                            last = pe.transpose(pb[4 + q][:, j * P:(j + 1) * P], sg[:, q, j * P:(j + 1) * P], ident[:])
                        last.then_inc(S(f"m_hp{q}"), 1)
                        pe.wait_ge(S(f"m_ht{q}"), t + 1)
                        pe.wait_ge(S(f"m_ye{1 - q}"), t + q)
                        for s in range(4, MOE_SLOTS):
                            pe.wait_ge(S(f"m_full{s}"), (t * 2 + q + 1) * 16)
                            w = slot(s).rearrange("p (k f) -> p k f", f=D)
                            for j in range(2):
                                fc = (s - 4) * 2 + j
                                x = hid_t[:, q, (fc % 2) * P + (fc // 2) * SLOT:(fc % 2) * P + (fc // 2 + 1) * SLOT]
                                for n in range(2):
                                    for h in range(2):
                                        at = h * 1024 + n * BANK
                                        last = pe.matmul(pb[6 + n][SLOT * h:SLOT * h + SLOT, :], x, w[:, j, at:at + BANK],
                                                         start=(fc == 0), stop=(fc == 3))
                            last.then_inc(S("m_free"), 1)
                pe.wait_ge(S("m_ye1"), ps * 16 + 16)
                pe.wait_ge(S("m_xg"), ps * 17 + 17)
                moe_scatter(1, ps * 17 + 16)

            moe_pe(0)
            count = pe.value_load(most[0:1, 0:1], min_val=0, max_val=NP_)
            with pe.If(count > CAP):
                with pe.Fori(1, PASSES) as ps:
                    moe_pe(ps)
            pe.wait_ge(S("x2"), 1)
            sum_squares(3)
            pe.wait_ge(S("h_dve"), 3)
            pe.wait_ge(S("h_act"), 3 * (KD - 8))
            for b in range(12):
                if b >= 4:
                    pe.wait_ge(S("yo_evac"), b - 3)
                m = P if b < 8 else NS
                at = (b // 4) * P
                for j in range(4):
                    k = 4 * (b % 4) + j
                    last = pe.transpose(pb[1 + b % 4][0:m, j * P:(j + 1) * P], ht[:, k, at:at + m], ident[:])
                last.then_inc(S("yo_ps"), 1)


N_VEC = 2 + 11 + 7 + 1
N_CONSTS = 12

_OUTS = [("y_prompt", (1, NP_, D)), ("y_sample", (NS, 1, D)), ("sg_prompt", (1, 1, GLA_H, GLA_DK, GLA_DV)),
         ("sr_prompt", (1, 1, RH, RD, RD)), ("ss_prompt", (1, 1, RCOLS)), ("sg_sample", (1, NS, GLA_H, GLA_DK, GLA_DV)),
         ("sr_sample", (1, NS, RH, RD, RD)), ("ss_sample", (1, NS, RCOLS))]


def kernel(**inputs):
    import concourse.bacc as bacc
    from concourse.bass_utils import run_bass_kernel_spmd

    nc = bacc.Bacc("TRN2", target_bir_lowering=False, num_devices=1)
    arrays, args = {}, {}
    for name, value in inputs.items():
        a = np.ascontiguousarray(value)
        arrays[f"in_{name}"] = a
        args[name] = nc.dram_tensor(f"in_{name}", a.shape, mybir.dt.from_np(a.dtype), kind="ExternalInput").ap()
    for name, shape in _OUTS:
        args[name] = nc.dram_tensor(f"out_{name}", shape, F32, kind="ExternalOutput").ap()
    args["scratch"] = nc.dram_tensor("vector_scratch", (48, 1024), F32, kind="Internal").ap()
    hymba_layer(nc, **args)
    r = run_bass_kernel_spmd(nc, [arrays], core_ids=[0])
    return tuple(r.results[0][f"out_{name}"] for name, _ in _OUTS)
```
